# Optimizing a Trainium2 kernel written in Bass

```python
import jax, jax.numpy as jnp
from jax import lax
import numpy as np

D_MODEL = 1024
BATCH = 1
SEQ = 2048
DEPTH = 1

HEAD_DIM = 64
NA_HEADS = 8
SWA_HEADS = 8
SWA_KV_HEADS = 2
A_WIDTH = NA_HEADS * HEAD_DIM
B_WIDTH = SWA_HEADS * HEAD_DIM
B_KV_WIDTH = SWA_KV_HEADS * HEAD_DIM
MIX_WIDTH = A_WIDTH + B_WIDTH
IN_WIDTH = 3 * A_WIDTH + B_WIDTH + 2 * B_KV_WIDTH
GRID_W = 64
NA_ROWS_MAX = 8
NA_COLS = 16
NA_QROWS = 2
NA_QCOLS = 16
NA_HCOLS = NA_COLS + NA_QCOLS
SWA_WINDOW = 128
SWA_BLOCK = 128
ROPE_THETA = 500000.0
ROPE_DIM = HEAD_DIM // 4
D_FF = -(-8 * D_MODEL // (3 * 256)) * 256
RMS_EPS = 1e-6
NEG_INF = -1e30

kernel_name = "hybrid_natten_swa_sink_encoder_block"

def rmsnorm(x, g):
    xf = x.astype(jnp.float32)
    y = xf * lax.rsqrt(jnp.mean(xf * xf, axis=-1, keepdims=True) + RMS_EPS)
    return (y * g.astype(jnp.float32)).astype(x.dtype)

def partial_rope(x, pos):
    inv_freq = ROPE_THETA ** (-jnp.arange(0, ROPE_DIM, 2, dtype=jnp.float32) / ROPE_DIM)
    ang = pos.astype(jnp.float32)[:, None] * inv_freq[None, :]
    cos = jnp.cos(ang)[None, :, None, :]
    sin = jnp.sin(ang)[None, :, None, :]
    xr = x[..., :ROPE_DIM].astype(jnp.float32)
    x1, x2 = xr[..., : ROPE_DIM // 2], xr[..., ROPE_DIM // 2:]
    rot = jnp.concatenate([x1 * cos - x2 * sin, x2 * cos + x1 * sin], axis=-1)
    return jnp.concatenate([rot.astype(x.dtype), x[..., ROPE_DIM:]], axis=-1)

def _axis_windows(n, k, q_blk, halo):
    nb = n // q_blk
    q_pos = np.arange(n).reshape(nb, q_blk)
    start = np.clip(q_pos - k // 2, 0, n - k)
    h0 = np.clip(q_pos[:, 0] - k // 2, 0, n - halo)
    k_pos = h0[:, None] + np.arange(halo)[None, :]
    ok = (k_pos[:, None, :] >= start[:, :, None]) & (k_pos[:, None, :] < start[:, :, None] + k)
    off = k_pos[:, None, :] - q_pos[:, :, None]
    return q_pos, k_pos, ok, off

def neighbourhood_attention(q, k, v, rpb):
    b, s, h, d = q.shape
    rows = s // GRID_W
    kr = min(NA_ROWS_MAX, rows)
    hr = min(kr + NA_QROWS, rows)
    _, r_keys, r_ok, r_off = _axis_windows(rows, kr, NA_QROWS, hr)
    _, c_keys, c_ok, c_off = _axis_windows(GRID_W, NA_COLS, NA_QCOLS, NA_HCOLS)
    rb, cb = rows // NA_QROWS, GRID_W // NA_QCOLS
    nq, nk = NA_QROWS * NA_QCOLS, hr * NA_HCOLS

    key_idx = (r_keys[:, None, :, None] * GRID_W + c_keys[None, :, None, :]).astype(np.int32)
    key_idx = key_idx.reshape(-1)
    kb = jnp.take(k, key_idx, axis=1).reshape(b, rb, cb, nk, h, d)
    vb = jnp.take(v, key_idx, axis=1).reshape(b, rb, cb, nk, h, d)
    qb = q.reshape(b, rb, NA_QROWS, cb, NA_QCOLS, h, d).transpose(0, 1, 3, 2, 4, 5, 6)
    qb = qb.reshape(b, rb, cb, nq, h, d)

    mask = (r_ok[:, None, :, None, :, None] & c_ok[None, :, None, :, None, :]).reshape(rb, cb, nq, nk)
    r_idx = np.clip(r_off + NA_ROWS_MAX - 1, 0, 2 * NA_ROWS_MAX - 2).astype(np.int32)
    c_idx = np.clip(c_off + NA_COLS - 1, 0, 2 * NA_COLS - 2).astype(np.int32)
    bias = rpb[:, r_idx[:, None, :, None, :, None], c_idx[None, :, None, :, None, :]]
    bias = bias.reshape(h, rb, cb, nq, nk).transpose(1, 2, 0, 3, 4).astype(jnp.float32)

    scale = HEAD_DIM ** -0.5
    logits = jnp.einsum('bnmqhd,bnmkhd->bnmhqk', qb, kb).astype(jnp.float32) * scale + bias
    logits = jnp.where(mask[:, :, None], logits, NEG_INF)
    p = jax.nn.softmax(logits, axis=-1).astype(vb.dtype)
    o = jnp.einsum('bnmhqk,bnmkhd->bnmqhd', p, vb)
    o = o.reshape(b, rb, cb, NA_QROWS, NA_QCOLS, h, d).transpose(0, 1, 3, 2, 4, 5, 6)
    return o.reshape(b, s, h, d)

def windowed_gqa_sink(q, k, v, sink):
    b, s, hq, d = q.shape
    hkv = k.shape[2]
    g = hq // hkv
    nb = s // SWA_BLOCK
    qb = q.reshape(b, nb, SWA_BLOCK, hkv, g, d)

    def band(t):
        tp = jnp.pad(t, ((0, 0), (SWA_BLOCK, SWA_BLOCK), (0, 0), (0, 0)))
        tp = tp.reshape(b, nb + 2, SWA_BLOCK, hkv, d)
        return jnp.concatenate([tp[:, :-2], tp[:, 1:-1], tp[:, 2:]], axis=2)

    kb, vb = band(k), band(v)
    q_pos = np.arange(nb)[:, None] * SWA_BLOCK + np.arange(SWA_BLOCK)[None, :]
    k_pos = (np.arange(nb)[:, None] - 1) * SWA_BLOCK + np.arange(3 * SWA_BLOCK)[None, :]
    mask = ((np.abs(q_pos[:, :, None] - k_pos[:, None, :]) <= SWA_WINDOW)
            & (k_pos[:, None, :] >= 0) & (k_pos[:, None, :] < s))

    scale = HEAD_DIM ** -0.5
    logits = jnp.einsum('bnqkgd,bnjkd->bnkgqj', qb, kb).astype(jnp.float32) * scale
    logits = jnp.where(mask[None, :, None, None], logits, NEG_INF)
    sk = sink.astype(jnp.float32).reshape(hkv, g)[None, None, :, :, None, None]
    m = jnp.maximum(jnp.max(logits, axis=-1, keepdims=True), sk)
    p = jnp.exp(logits - m)
    denom = jnp.sum(p, axis=-1, keepdims=True) + jnp.exp(sk - m)
    p = (p / denom).astype(vb.dtype)
    o = jnp.einsum('bnkgqj,bnjkd->bnqkgd', p, vb)
    return o.reshape(b, s, hq, d)

def setup_inputs(seed: int = 0) -> dict:
    key = jax.random.key(seed)
    ks = jax.random.split(key, 14)
    f32 = jnp.float32

    def nrm(k, shape, scale):
        return jax.random.normal(k, shape, f32) * scale

    def gain(k, shape):
        return 1.0 + 0.05 * jax.random.normal(k, shape, f32)

    return {
        "x": jax.random.normal(ks[0], (BATCH, SEQ, D_MODEL), f32),
        "g_norm_mix": gain(ks[1], (DEPTH, D_MODEL)),
        "w_in": nrm(ks[2], (DEPTH, D_MODEL, IN_WIDTH), D_MODEL ** -0.5),
        "na_rpb": nrm(ks[3], (DEPTH, NA_HEADS, 2 * NA_ROWS_MAX - 1, 2 * NA_COLS - 1), 0.2),
        "swa_sink": nrm(ks[4], (DEPTH, SWA_HEADS), 0.5),
        "g_out_na": gain(ks[5], (DEPTH, A_WIDTH)),
        "g_out_swa": gain(ks[6], (DEPTH, B_WIDTH)),
        "w_out": nrm(ks[7], (DEPTH, MIX_WIDTH, D_MODEL), MIX_WIDTH ** -0.5),
        "g_norm_ffn": gain(ks[8], (DEPTH, D_MODEL)),
        "w_gate": nrm(ks[9], (DEPTH, D_MODEL, D_FF), D_MODEL ** -0.5),
        "w_up": nrm(ks[10], (DEPTH, D_MODEL, D_FF), D_MODEL ** -0.5),
        "w_down": nrm(ks[11], (DEPTH, D_FF, D_MODEL), D_FF ** -0.5),
        "g_final": gain(ks[12], (D_MODEL,)),
    }

def reference(x, g_norm_mix, w_in, na_rpb, swa_sink, g_out_na, g_out_swa, w_out,
              g_norm_ffn, w_gate, w_up, w_down, g_final):
    b, s, _ = x.shape
    pos = jnp.arange(s, dtype=jnp.int32)
    split_at = [A_WIDTH, 2 * A_WIDTH, 3 * A_WIDTH, 3 * A_WIDTH + B_WIDTH,
                3 * A_WIDTH + B_WIDTH + B_KV_WIDTH]
    for l in range(DEPTH):
        h = rmsnorm(x, g_norm_mix[l])
        proj = h @ w_in[l]
        qa, ka, va, qb, kb, vb = jnp.split(proj, split_at, axis=-1)
        qa = qa.reshape(b, s, NA_HEADS, HEAD_DIM)
        ka = ka.reshape(b, s, NA_HEADS, HEAD_DIM)
        va = va.reshape(b, s, NA_HEADS, HEAD_DIM)
        qb = partial_rope(qb.reshape(b, s, SWA_HEADS, HEAD_DIM), pos)
        kb = partial_rope(kb.reshape(b, s, SWA_KV_HEADS, HEAD_DIM), pos)
        vb = vb.reshape(b, s, SWA_KV_HEADS, HEAD_DIM)

        oa = neighbourhood_attention(qa, ka, va, na_rpb[l]).reshape(b, s, A_WIDTH)
        ob = windowed_gqa_sink(qb, kb, vb, swa_sink[l]).reshape(b, s, B_WIDTH)
        o = jnp.concatenate([rmsnorm(oa, g_out_na[l]), rmsnorm(ob, g_out_swa[l])], axis=-1)
        x = x + o @ w_out[l]

        h = rmsnorm(x, g_norm_ffn[l])
        x = x + (jax.nn.silu(h @ w_gate[l]) * (h @ w_up[l])) @ w_down[l]
    return rmsnorm(x, g_final)


_drawn_inputs = setup_inputs


def setup_inputs(seed=0):
    import zlib

    import numpy as np

    out = dict(_drawn_inputs(seed))
    spreads = {}
    factors = {'swa_sink': 8.0}
    for name, (base, spread) in spreads.items():
        noise = np.random.default_rng([zlib.crc32(name.encode()), seed]).standard_normal(out[name].shape)
        drawn = base * np.exp(spread * noise) if base else spread * noise
        out[name] = __import__('jax').numpy.asarray(drawn.astype(out[name].dtype))
    for name, factor in factors.items():
        out[name] = (out[name] * factor).astype(out[name].dtype)
    return out
```

```python
from contextlib import ExitStack

import numpy as np
import concourse.bass as bass
from concourse import mybir

ALU = mybir.AluOpType
ACT = mybir.ActivationFunctionType
F32 = mybir.dt.float32
F32R = mybir.dt.float32r

P = 128
BANK = 512
D = 1024
S = 2048
HD = 64
GW = 64
NAH, SWH, SWKV = 8, 8, 2
AW = NAH * HD
KT = D // P
NT = S // P
HS = S // 2
HT = NT // 2
FF = 2816
EPS = 1e-6
SCALE = HD ** -0.5
HEADS = 2 * NAH + SWH + SWKV
V_WIDTH = AW + SWKV * HD
ROPE = HD // 4
HALF = ROPE // 2
MASKED = 1e30
ROWS_REL, COLS_REL = 16, 48
PAD_R, PAD_C = 23, 63


def project_phase(nc, x, g_mix, w_in, rpb, cos2, sin2, ident_in, zeros_in, qk_dram, v_dram,
                  pad_dram, rel_dram):
    with ExitStack() as ctx:
        def sb(name, shape, dt=F32):
            return ctx.enter_context(nc.sbuf_tensor(name, shape, dt))

        def sem(name):
            return nc.alloc_semaphore(name)

        XS, RAW = 3, 4
        hT_hi = sb("hT_hi", [P, KT, S], F32R)
        hT_lo = sb("hT_lo", [P, KT, S], F32R)
        w_hi = sb("w_hi", [P, KT, BANK], F32R)
        w_lo = sb("w_lo", [P, KT, BANK], F32R)
        raw = sb("w_raw", [P, RAW, 1024])
        xt = sb("x_tile", [P, XS, D])
        xn = sb("x_normed", [P, D])
        gmix = sb("g_mix_rows", [P, D])
        ident = sb("ident1", [P, P])
        out_hi = sb("stage_hi", [P, 2, BANK], F32R)
        out_lo = sb("stage_lo", [P, 2, BANK], F32R)
        cosb = sb("cos_rows", [P, NT, ROPE])
        sinb = sb("sin_rows", [P, NT, ROPE])
        rope_c = sb("rope_c", [P, SWH, ROPE])
        rope_s = sb("rope_s", [P, SWH, ROPE])
        ssq = sb("ssq1", [P, NT])
        msq = sb("msq1", [P, NT])
        inv = sb("inv1", [P, NT])
        rstd = sb("rstd1", [P, NT])
        tok = xt
        mm = ctx.enter_context(nc.psum_tensor("proj_psum", [P, 4, BANK], F32))
        tp = ctx.enter_context(nc.psum_tensor("turn_psum", [P, 2, 2 * BANK], F32))

        x_in = [sem(f"x_in{i}") for i in range(XS)]
        w_arrived = [sem(f"w_arrived{i}") for i in range(RAW)]
        const_in, rope_in = sem("const_in1"), sem("rope_in")
        squared, mean_done, inv_done = sem("squared"), sem("mean_done"), sem("inv_done")
        rstd_done, normed, turned = sem("rstd_done"), sem("normed"), sem("turned")
        h_hi_done, h_lo_done = sem("h_hi_done"), sem("h_lo_done")
        w_hi_done, w_lo_done = sem("w_hi_done"), sem("w_lo_done")
        proj_done, panel_read = sem("proj_done"), sem("panel_read")
        res_hi, res_lo = sem("res_hi"), sem("res_lo")
        tok_done, rope_step, roped, tok_turned = sem("tok_done"), sem("rope_step"), sem("roped"), sem("tok_turned")
        stored = [sem(f"stored{i}") for i in range(2)]
        v_stored = [sem(f"v_stored{i}") for i in range(2)]
        table_made = sem("table_made")

        slices = [(p, slice(0, KT), slice(g * P, (g + 1) * P)) for p in (0, 1) for g in range(4)]
        slices += [(p, slice(2 * i, 2 * i + 2), slice(0, BANK)) for p in (2, 3) for i in range(4)]
        slices += [(4, slice(4 * i, 4 * i + 4), slice(0, 256)) for i in range(2)]
        w_view = w_in.rearrange("(k p) n -> p k n", p=P)
        x_view = x.rearrange("(t p) d -> t p d", p=P)
        AHEAD = 6
        QK_STEPS = 32
        STEPS = QK_STEPS + 3 * NT

        block = ctx.enter_context(nc.Block())

        def raw_of(n):
            _, ks, _ = slices[n]
            return raw[:, n % RAW, :].rearrange("p (k n) -> p k n", k=ks.stop - ks.start)

        def w_part(w, n):
            _, ks, cs = slices[n]
            return w[:, ks, cs]

        def staged(stage, m):
            order = "p (b r c) -> p r b c" if m < 16 else "p (r b c) -> p r b c"
            return stage[:, m % 2, :].rearrange(order, b=4, c=16)

        def result(m):
            return mm[:, m % 4, :].rearrange("p (r b c) -> p r b c", b=4, c=16)

        def split_at(m):
            return {12: [4], 13: [5], 14: [6], 15: [7], QK_STEPS - 1: [8, 9, 10, 11],
                    QK_STEPS + NT - 1: [12, 13, 14, 15], QK_STEPS + 2 * NT - 1: [16, 17]}.get(m, [])

        def wait_panel(eng, n):
            if 4 <= n < 8:
                eng.wait_ge(proj_done, 12 + n - 4 + 1)
            elif 8 <= n < 12:
                eng.wait_ge(proj_done, QK_STEPS)
            elif n in (15, 17):
                eng.wait_ge(proj_done, QK_STEPS + (NT if n == 15 else 2 * NT))
            elif n >= 12:
                eng.wait_ge(panel_read, n - 11)

        def wait_tok_slot(eng, t):
            u = t - 2
            if u < 0:
                return
            if u < NT:
                eng.wait_ge(v_stored[u % 2], 16 * (u // 2 + 1))
            else:
                eng.wait_ge(tok_turned, u - NT + 1)
            if u >= 2 * NT:
                eng.wait_ge(v_stored[u % 2], 16 * (NT // 2 + (u - 2 * NT) // 2 + 1))

        @block.sync
        def _(sp):
            def load_w(n):
                if n >= RAW:
                    sp.wait_ge(w_lo_done, n - RAW + 1)
                p, ks, cs = slices[n]
                sp.dma_start(raw_of(n), w_view[:, ks, p * 512 + cs.start:p * 512 + cs.stop]) \
                  .then_inc(w_arrived[n % RAW], 16)

            sp.dma_start(ident[:], ident_in).then_inc(const_in, 16)
            for n in range(8):
                load_w(n)
            for m in range(QK_STEPS):
                p, tb, g = m // 16, m // 4 % 4, m % 4
                r0 = p * 512 + g * P
                sp.wait_ge(res_lo, m + 1)
                for part, stage in enumerate((out_hi, out_lo)):
                    sp.dma_start(qk_dram[part, r0:r0 + P, tb * BANK:(tb + 1) * BANK],
                                 stage[:, m % 2, :].bitcast(F32)).then_inc(stored[m % 2], 16)
                if m == 15:
                    for n in range(8, 12):
                        load_w(n)
            for n in range(12, 16):
                load_w(n)
            for t in range(3 * NT):
                p, tt = 2 + t // NT, t % NT
                rows = slice(tt * P, (tt + 1) * P)
                m = QK_STEPS + t - NT
                if p == 2:
                    sp.wait_ge(tok_done, t + 1)
                    sp.dma_start(v_dram[rows, 0:AW], tok[:, t % 2, 0:AW]).then_inc(v_stored[t % 2], 16)
                    continue
                if p == 4:
                    sp.wait_ge(tok_done, t + 1)
                    sp.dma_start(v_dram[rows, AW:V_WIDTH], tok[:, t % 2, P:2 * P]) \
                        .then_inc(v_stored[t % 2], 16)
                if t == NT:
                    for n in (16, 17):
                        load_w(n)
                sp.wait_ge(res_lo, m + 1)
                for part, stage in enumerate((out_hi, out_lo)):
                    if p == 3:
                        dst = qk_dram[part, 8 * P:12 * P, rows].rearrange("(g p) s -> p g s", p=P)
                        src = stage[:, m % 2, :].bitcast(F32).rearrange("p (g s) -> p g s", g=4)
                    else:
                        dst, src = qk_dram[part, 12 * P:13 * P, rows], stage[:, m % 2, 0:P].bitcast(F32)
                    sp.dma_start(dst, src).then_inc(stored[m % 2], 16)
            for i in range(2):
                sp.wait_ge(stored[i], 16 * (QK_STEPS + 2 * NT))
                sp.wait_ge(v_stored[i], 16 * NT)

        @block.gpsimd
        def _(pool):
            pool.dma_start(cosb[:], cos2.rearrange("(t p) c -> p t c", p=P)).then_inc(rope_in, 16)
            pool.dma_start(sinb[:], sin2.rearrange("(t p) c -> p t c", p=P)).then_inc(rope_in, 16)
            pool.dma_start(pad_dram.rearrange("h r c -> (h r c)"), zeros_in).then_inc(table_made, 16)
            pool.wait_ge(table_made, 16)
            with nc.allow_non_contiguous_dma(reason="small table"):
                pool.dma_start(pad_dram[:, 4:19, 16:47], rpb).then_inc(table_made, 16)
            pool.wait_ge(table_made, 32)
            for h in range(NAH):
                for qr in range(8):
                    src = bass.AP(pad_dram.tensor, (h * PAD_R + 7 - qr) * PAD_C + 15,
                                  [[PAD_C, ROWS_REL], [-1, 16], [1, COLS_REL]])
                    dst = rel_dram[h, qr * 16:(qr + 1) * 16, :].rearrange("q (j c) -> j q c", c=COLS_REL)
                    pool.dma_start(dst, src).then_inc(table_made, 16)
            pool.wait_ge(table_made, 16 * (2 + 8 * NAH))

        @block.scalar
        def _(act):
            def load_x(t):
                act.dma_start(xt[:, t % XS, :], x_view[t]).then_inc(x_in[t % XS], 16)

            load_x(0)
            act.dma_start(gmix[:], g_mix.broadcast_to([P, D])).then_inc(const_in, 16)
            load_x(1)
            load_x(2)

            def norm_step(n):
                t = n - 1
                if 0 <= t < NT:
                    act.wait_ge(turned, t + 1)
                    nc.scalar.copy(hT_hi[:, :, t * P:(t + 1) * P],
                                   tp[:, t % 2, :].rearrange("p (k s) -> p k s", k=KT)).then_inc(h_hi_done, 1)
                if n < NT:
                    act.wait_ge(x_in[n % XS], 16 * (n // XS + 1))
                    if 1 <= n <= NT - XS:
                        load_x(n - 1 + XS)
                    nc.scalar.activation(xn[:], xt[:, n % XS, :], ACT.Square,
                                         accum_out=ssq[:, n:n + 1]).then_inc(squared, 1)
                    act.wait_ge(inv_done, n + 1)
                    nc.scalar.activation(rstd[:, n:n + 1], inv[:, n:n + 1], ACT.Sqrt).then_inc(rstd_done, 1)

            def split_hi(n):
                wait_panel(act, n)
                act.wait_ge(w_arrived[n % RAW], 16 * (n // RAW + 1))
                nc.scalar.mul(w_part(w_hi, n), raw_of(n), -SCALE if n < 4 else 1.0).then_inc(w_hi_done, 1)

            def turn_hi(t):
                m, w = QK_STEPS + t - NT, 4 * P if t < 2 * NT else P
                act.wait_ge(tok_turned, t - NT + 1)
                act.wait_ge(stored[m % 2], 32 * (m // 2))
                nc.scalar.copy(out_hi[:, m % 2, 0:w], tp[:, t % 2, 0:w]).then_inc(res_hi, 1)

            for n in range(AHEAD):
                norm_step(n)
                if n < 4:
                    split_hi(n)
            for m in range(QK_STEPS):
                act.wait_ge(proj_done, m + 1)
                if m >= 2:
                    act.wait_ge(stored[m % 2], 32 * (m // 2))
                nc.scalar.copy(staged(out_hi, m), result(m)).then_inc(res_hi, 1)
                if m + AHEAD < NT + 1:
                    norm_step(m + AHEAD)
                for n in split_at(m):
                    split_hi(n)
            for t in range(3 * NT):
                m, w = QK_STEPS + t, BANK if t < 2 * NT else 2 * P
                act.wait_ge(proj_done, m + 1)
                wait_tok_slot(act, t)
                nc.scalar.mul(tok[:, t % 2, 0:w], mm[:, m % 4, 0:w],
                              -SCALE if NT <= t < 2 * NT else 1.0).then_inc(tok_done, 1)
                if t > NT:
                    turn_hi(t - 1)
                for n in split_at(m):
                    split_hi(n)
            turn_hi(3 * NT - 1)

        @block.vector
        def _(dve):
            def norm_step(n):
                t = n - 1
                if 0 <= t < NT:
                    dve.wait_ge(h_hi_done, t + 1)
                    nc.vector.tensor_tensor(hT_lo[:, :, t * P:(t + 1) * P],
                                            tp[:, t % 2, :].rearrange("p (k s) -> p k s", k=KT),
                                            hT_hi[:, :, t * P:(t + 1) * P], ALU.subtract).then_inc(h_lo_done, 1)
                if n < NT:
                    dve.wait_ge(squared, n + 1)
                    nc.vector.tensor_scalar(msq[:, n:n + 1], ssq[:, n:n + 1], 1.0 / D, EPS,
                                            ALU.mult, ALU.add).then_inc(mean_done, 1)
                    dve.wait_ge(mean_done, n + 1)
                    nc.vector.reciprocal(inv[:, n:n + 1], msq[:, n:n + 1]).then_inc(inv_done, 1)
                    dve.wait_ge(rstd_done, n + 1)
                    nc.vector.scalar_tensor_tensor(out=xn[:], in0=xt[:, n % XS, :], scalar=rstd[:, n:n + 1],
                                                   in1=gmix[:], op0=ALU.mult, op1=ALU.mult).then_inc(normed, 1)

            def split_lo(n):
                dve.wait_ge(w_hi_done, n + 1)
                nc.vector.scalar_tensor_tensor(out=w_part(w_lo, n), in0=raw_of(n),
                                               scalar=-SCALE if n < 4 else 1.0, in1=w_part(w_hi, n),
                                               op0=ALU.mult, op1=ALU.subtract).then_inc(w_lo_done, 1)

            def rope(t):
                heads, tt, done = (SWH, t % NT, 3 * (t - NT)) if t < 2 * NT else (SWKV, t % NT, 3 * (t - NT))
                v = tok[:, t % 2, 0:heads * HD].rearrange("p (h d) -> p h d", d=HD)
                cos = cosb[:, tt:tt + 1, :].broadcast_to([P, heads, ROPE])
                sin = sinb[:, tt:tt + 1, :].broadcast_to([P, heads, ROPE])
                dve.wait_ge(tok_done, t + 1)
                nc.vector.tensor_tensor(rope_c[:, 0:heads, :], v[:, :, 0:ROPE], cos, ALU.mult).then_inc(rope_step, 1)
                nc.vector.tensor_tensor(rope_s[:, 0:heads, 0:HALF], v[:, :, HALF:ROPE], sin[:, :, 0:HALF],
                                        ALU.mult).then_inc(rope_step, 1)
                nc.vector.tensor_tensor(rope_s[:, 0:heads, HALF:ROPE], v[:, :, 0:HALF], sin[:, :, HALF:ROPE],
                                        ALU.mult).then_inc(rope_step, 1)
                dve.wait_ge(rope_step, done + 3)
                nc.vector.tensor_tensor(v[:, :, 0:ROPE], rope_c[:, 0:heads, :], rope_s[:, 0:heads, :],
                                        ALU.add).then_inc(roped, 1)
                dve.wait_ge(roped, t - NT + 1)

            def turn_lo(t):
                m, w = QK_STEPS + t - NT, 4 * P if t < 2 * NT else P
                dve.wait_ge(res_hi, m + 1)
                nc.vector.tensor_tensor(out_lo[:, m % 2, 0:w], tp[:, t % 2, 0:w], out_hi[:, m % 2, 0:w],
                                        ALU.subtract).then_inc(res_lo, 1)

            dve.wait_ge(const_in, 32)
            for n in range(AHEAD):
                norm_step(n)
                if n < 4:
                    split_lo(n)
            for m in range(QK_STEPS):
                dve.wait_ge(res_hi, m + 1)
                nc.vector.tensor_tensor(staged(out_lo, m), result(m), staged(out_hi, m), ALU.subtract) \
                    .then_inc(res_lo, 1)
                if m + AHEAD < NT + 1:
                    norm_step(m + AHEAD)
                for n in split_at(m):
                    split_lo(n)
            dve.wait_ge(rope_in, 32)
            for t in range(3 * NT):
                if t >= NT:
                    rope(t)
                if t > NT:
                    turn_lo(t - 1)
                for n in split_at(QK_STEPS + t):
                    split_lo(n)
            turn_lo(3 * NT - 1)

        @block.tensor
        def _(pe):
            def turn_tile(n):
                pe.wait_ge(normed, n + 1)
                if n >= 2:
                    pe.wait_ge(h_lo_done, n - 1)
                for k in range(KT):
                    last = pe.transpose(tp[:, n % 2, k * P:(k + 1) * P], xn[:, k * P:(k + 1) * P], ident[:])
                last.then_inc(turned, 1)

            def turn_tok(t):
                pe.wait_ge(roped, t - NT + 1)
                if t - NT >= 2:
                    pe.wait_ge(res_lo, QK_STEPS + t - NT - 1)
                for g in range(4 if t < 2 * NT else 1):
                    last = pe.transpose(tp[:, t % 2, g * P:(g + 1) * P], tok[:, t % 2, g * P:(g + 1) * P], ident[:])
                last.then_inc(tok_turned, 1)

            pe.wait_ge(const_in, 32)
            for n in range(AHEAD - 1):
                turn_tile(n)
            for m in range(QK_STEPS):
                p, tb, g = m // 16, m // 4 % 4, m % 4
                cols, toks = slice(g * P, (g + 1) * P), slice(tb * BANK, (tb + 1) * BANK)
                pe.wait_ge(w_lo_done, 4 * p + g + 1)
                pe.wait_ge(h_lo_done, min(4 * tb + 4, NT) if p == 0 else NT)
                if m >= 4:
                    pe.wait_ge(res_lo, m - 3)
                for k in range(KT):
                    pe.matmul(mm[:, m % 4, :], w_hi[:, k, cols], hT_hi[:, k, toks], start=(k == 0), stop=False)
                    pe.matmul(mm[:, m % 4, :], w_hi[:, k, cols], hT_lo[:, k, toks], start=False, stop=False)
                    last = pe.matmul(mm[:, m % 4, :], w_lo[:, k, cols], hT_hi[:, k, toks], start=False,
                                     stop=(k == KT - 1))
                last.then_inc(proj_done, 1)
                if m + AHEAD - 1 < NT:
                    turn_tile(m + AHEAD - 1)
            for t in range(3 * NT):
                m, p = QK_STEPS + t, 2 + t // NT
                w, toks = BANK if p < 4 else 2 * P, slice(t % NT * P, (t % NT + 1) * P)
                if t < 4:
                    pe.wait_ge(res_lo, m - 3)
                else:
                    pe.wait_ge(tok_done, t - 3)
                for k in range(KT):
                    pe.wait_ge(w_lo_done, 8 + 4 * (p - 2) + (k // 2 if p < 4 else k // 4) + 1)
                    pe.matmul(mm[:, m % 4, 0:w], hT_hi[:, k, toks], w_hi[:, k, 0:w], start=(k == 0), stop=False)
                    pe.matmul(mm[:, m % 4, 0:w], hT_hi[:, k, toks], w_lo[:, k, 0:w], start=False, stop=False)
                    last = pe.matmul(mm[:, m % 4, 0:w], hT_lo[:, k, toks], w_hi[:, k, 0:w], start=False,
                                     stop=(k == KT - 1))
                    if k % 2 and k < KT - 1 and t % NT == NT - 1:
                        last.then_inc(panel_read, 1)
                last.then_inc(proj_done, 1)
                if t > NT:
                    turn_tok(t - 1)
            turn_tok(3 * NT - 1)


class Tiles:

    def __init__(self, near):
        self.near = near
        self.unit = 256 if near else 128
        self.portions = [(0, 1), (1, 3), (3, 5), (5, 8)] if near else [(0, 3), (3, 7), (7, 11), (11, 16)]

    def chunks(self, t):
        if self.near:
            return key_rows(t // 4)[1] // 4
        return 2 if t in (0, NT - 1) else 3

    def keys(self, ap, t):
        if self.near:
            (r0, rows), c0 = key_rows(t // 4), key_col(t % 4)
            return ap.rearrange("p (r c) -> p r c", c=GW)[:, r0:r0 + rows, c0:c0 + 32]
        k0 = max(t - 1, 0) * P
        return ap[:, k0:k0 + self.chunks(t) * P]

    def value_chunk(self, t, j):
        if self.near:
            return (key_rows(t // 4)[0] // 4 + j) * 4 + t % 4
        return max(t - 1, 0) + j

    def score_cols(self, t):
        n = self.chunks(t) * P
        if self.near:
            return 0, 0, n
        if t == 0:
            return 1 + P, 1 + P, 2 + 3 * P
        return (1, 0, 1 + n) if t == NT - 1 else (1, 1, 2 + n)


def attention_phase(nc, near, qk_dram, v_dram, rel_dram, mask_in, sink_in, ident_in, o_dram):
    tiles = Tiles(near)
    name = "na" if near else "swa"
    ROUNDS, UNITS = 4, 2 * NT
    TURN_LAG, PV_LAG, NORM_LAG = 2, 4, 1
    OUT_LAG = PV_LAG + 1
    q0, k0 = (0, NAH) if near else (2 * NAH, 2 * NAH + SWH)
    W = 512 if near else 3 * P + 2
    with ExitStack() as ctx:
        def sb(n, shape, dt=F32):
            return ctx.enter_context(nc.sbuf_tensor(f"{name}_{n}", shape, dt))

        def sem(n):
            return nc.alloc_semaphore(f"{name}_{n}")

        q_st = sb("q_stack", [P, 2, S], F32R)
        k_hh = sb("k_hi_twice", [P, 2, S], F32R)
        k_ll = sb("k_lo_twice", [P, 2, S], F32R)
        v_sb = sb("values", [P, 32 if near else NT, P])
        ident = sb("ident", [P, P])
        sn = sb("neg_scores", [P, 2, W])
        pr = sb("probs", [P, 2, W])
        pt = sb("probs_turned", [P, 4, 4 * P])
        o_st = sb("o_stage", [P, 2, BANK])
        negmax = sb("negmax", [P, 2])
        total = sb("total", [P, 2])
        rtotal = sb("rtotal", [P, 2])
        if near:
            mask = sb("mask", [P, 3, 1280])
            rel = sb("rel", [P, 2, ROWS_REL * COLS_REL])
            bias = sb("bias", [P, 2, 3, 1280])
        else:
            mask = sb("mask", [P, 3 * P])
            sinks = sb("sinks", [P, SWH])
        sc = ctx.enter_context(nc.psum_tensor(f"{name}_scores", [P, 4, BANK], F32))
        tp = ctx.enter_context(nc.psum_tensor(f"{name}_turned", [P, 2, BANK], F32))
        op = ctx.enter_context(nc.psum_tensor(f"{name}_out", [P, 2, BANK], F32))

        qk_in = [sem(f"qk_in{b}") for b in range(4)]
        v_in = [sem(f"v_in{b}") for b in range(4)]
        const_in, rel_in, sinks_negated = sem("const_in"), sem("rel_in"), sem("sinks_negated")
        bias_made = sem("bias_made")
        scored, shifted, exped = sem("scored"), sem("shifted"), sem("exped")
        sink_set, may_shift = sem("sink_set"), sem("may_shift")
        summed, probs_done = sem("summed"), sem("probs_done")
        p_turned, pt_copied = sem("p_turned"), sem("pt_copied")
        pv_done, o_copied = sem("pv_done"), sem("o_copied")
        o_stored = [sem(f"o_stored{i}") for i in range(2)]

        SC_BUFS, SN_BUFS, PT_BANKS, PT_BUFS, O_BANKS = 4, 2, 2, 4, 2

        def stream(eng, stages):
            deepest = max(lag for lag, _ in stages)

            def step(r, s, first, last):
                for lag, stage in stages:
                    u = s - lag
                    if (first and u < 0) or (last and u >= UNITS):
                        continue
                    stage(r + u // UNITS, u % UNITS)

            for s in range(deepest):
                step(0, s, True, False)
            with eng.Fori(0, ROUNDS - 1) as r:
                for s in range(deepest, UNITS + deepest):
                    step(r, s, False, False)
            for s in range(deepest, UNITS + deepest):
                step(ROUNDS - 1, s, False, True)

        block = ctx.enter_context(nc.Block())

        def f32(ap):
            return ap.bitcast(F32)

        @block.sync
        def _(sp):
            heads = qk_dram.rearrange("l (h d) s -> l h d s", d=HD)

            def load_qk(r, b):
                qs = slice(b * BANK, (b + 1) * BANK)
                lo, hi = tiles.portions[b]
                ks = slice(lo * tiles.unit, hi * tiles.unit)
                for e in range(2):
                    qh = q0 + 2 * r + e if near else q0 + r + 4 * e
                    for part in range(2):
                        sp.dma_start(f32(q_st[part * HD:(part + 1) * HD, e, qs]), heads[part, qh, :, qs]) \
                            .then_inc(qk_in[b], 16)
                    if near or isinstance(r, int) and r == 0:
                        kh = k0 + 2 * r + e if near else k0 + e
                        for part, dst in enumerate((k_hh, k_ll)):
                            for half in range(2):
                                sp.dma_start(f32(dst[half * HD:(half + 1) * HD, e, ks]),
                                             heads[part, kh, :, ks]).then_inc(qk_in[b], 16)

            def load_v(r, b):
                lo, hi = tiles.portions[b]
                if near:
                    for g in range(lo, hi):
                        for w in range(4):
                            src = v_dram.rearrange("(g r c) f -> g r c f", r=4, c=GW)[
                                g, :, key_col(w):key_col(w) + 32, bass.ds(r * P, P)]
                            sp.dma_start(v_sb[:, 4 * g + w, :], src).then_inc(v_in[b], 16)
                else:
                    sp.dma_start(v_sb[:, lo:hi, :],
                                 v_dram[lo * P:hi * P, AW:V_WIDTH].rearrange("(c p) f -> p c f", p=P)) \
                        .then_inc(v_in[b], 16)

            def load_rel(r):
                sp.dma_start(rel[:], rel_dram[bass.ds(2 * r, 2)].rearrange("h p f -> p h f")).then_inc(rel_in, 16)

            def store(r, b):
                sp.wait_ge(o_copied, O_BANKS + NT * r + 4 * (b + 1))
                dst = o_dram[bass.ds((r if near else r + 4) * P, P), b * BANK:(b + 1) * BANK]
                sp.dma_start(dst, o_st[:, b % 2, :]).then_inc(o_stored[b % 2], 16)

            if near:
                sp.dma_start(mask[:], mask_in).then_inc(const_in, 16)
                load_rel(0)
            else:
                sp.dma_start(mask[:], mask_in).then_inc(const_in, 16)
                sp.dma_start(sinks[:], sink_in.broadcast_to([P, SWH])).then_inc(const_in, 16)
            sp.dma_start(ident[:], ident_in).then_inc(const_in, 16)
            for b in range(4):
                load_qk(0, b)
                load_v(0, b)
            with sp.Fori(0, ROUNDS - 1) as r:
                if near:
                    sp.wait_ge(bias_made, 3 * r + 3)
                    load_rel(r + 1)
                for b in range(4):
                    sp.wait_ge(scored, UNITS * r + 8 * (b + 1))
                    load_qk(r + 1, b)
                    if near:
                        sp.wait_ge(pv_done, PT_BUFS // 2 + NT * r + 4 * (b + 1))
                        load_v(r + 1, b)
                    store(r, b)
            for b in range(4):
                store(ROUNDS - 1, b)
            for i in range(2):
                sp.wait_ge(o_stored[i], 16 * (2 * ROUNDS + 1))

        @block.gpsimd
        def _(pool):
            def make_bias(r):
                pool.wait_ge(rel_in, 16 * r + 16)
                for kind, (at, rows, j0, freed) in enumerate(((0, 12, 4, 1), (384, 16, 0, 3), (896, 12, 0, 4))):
                    pool.wait_ge(shifted, UNITS * r + 8 * freed)
                    for e in range(2):
                        for ck, c0 in enumerate((16, 8, 0)):
                            out = bias[:, e, ck, at:at + rows * 32].rearrange("p (r c) -> p r c", c=32)
                            m = mask[:, ck, at:at + rows * 32].rearrange("p (r c) -> p r c", c=32)
                            b = rel[:, e, :].rearrange("p (j c) -> p j c", c=COLS_REL)[:, j0:j0 + rows, c0:c0 + 32]
                            last = nc.gpsimd.tensor_tensor(out, m, b, ALU.subtract)
                    last.then_inc(bias_made, 1)

            if near:
                pool.wait_ge(const_in, 32)
                with pool.Fori(0, ROUNDS) as r:
                    make_bias(r)

        @block.scalar
        def _(act):
            def exp(r, u):
                e, t = u % 2, u // 2
                _, lo, hi = tiles.score_cols(t)
                act.wait_ge(shifted, UNITS * (r + 1) + u + 1)
                act.wait_ge(p_turned, UNITS * r + u + 1)
                nc.scalar.activation(pr[:, e, lo:hi], sn[:, e, lo:hi], ACT.Exp, bias=negmax[:, e:e + 1],
                                     scale=-1.0, accum_out=total[:, e:e + 1]).then_inc(exped, 1)

            def copy_turned(r, u):
                n = tiles.chunks(u // 2) * P
                act.wait_ge(p_turned, SN_BUFS + UNITS * r + u + 1)
                act.wait_ge(pv_done, PT_BUFS // 2 + NT * r + u // 2 - 1)
                nc.scalar.copy(pt[:, u % 4, 0:n], tp[:, u % 2, 0:n]).then_inc(pt_copied, 1)

            stream(act, [(TURN_LAG, copy_turned), (0, exp)])

        @block.vector
        def _(dve):
            def shift(r, u):
                e, t = u % 2, u // 2
                n = tiles.chunks(t) * P
                c0, _, _ = tiles.score_cols(t)
                dve.wait_ge(exped, UNITS * r + u + 1)
                if near:
                    if u % 8 == 0 and t // 4 != 2:
                        dve.wait_ge(bias_made, 3 * r + {0: 1, 1: 2, 3: 3}[t // 4])
                    b, cb = t // 4, t % 4
                    at, ck = {0: 0, 1: 384, 2: 384, 3: 896}[b], {0: 0, 1: 1, 2: 1, 3: 2}[cb]
                    add, start = bias[:, e, ck, at:at + n], 3.0e38
                else:
                    if u < 2:
                        nc.vector.tensor_copy(sn[:, e, 0:W:W - 1],
                                              sinks[:, bass.ds(r + 4 * e, 1)].broadcast_to([P, 2])) \
                            .then_inc(sink_set, 1)
                        dve.wait_ge(sink_set, 2 * r + u + 1)
                    add, start = mask[:, c0 - 1:c0 - 1 + n], sn[:, e, 0:1]
                dve.wait_ge(scored, UNITS * r + u + 1)
                dve.sem_inc(may_shift, 1)
                nc.vector.tensor_tensor_reduce(sn[:, e, c0:c0 + n], sc[:, u % 4, 0:n], add, 1.0, start,
                                               ALU.add, ALU.min, negmax[:, e:e + 1]).then_inc(shifted, 1)

            def normalise(r, u):
                e, t = u % 2, u // 2
                n = tiles.chunks(t) * P
                c0, _, _ = tiles.score_cols(t)
                dve.wait_ge(exped, SN_BUFS + UNITS * r + u + 1)
                nc.vector.reciprocal(rtotal[:, e:e + 1], total[:, e:e + 1]).then_inc(summed, 1)
                dve.wait_ge(summed, UNITS * r + u + 1)
                nc.vector.tensor_scalar(pr[:, e, c0:c0 + n], pr[:, e, c0:c0 + n], rtotal[:, e:e + 1], None,
                                        ALU.mult).then_inc(probs_done, 1)

            def results(r, u):
                if u % 2 == 0:
                    return
                t = u // 2
                b = t // 4
                dve.wait_ge(pv_done, PT_BUFS // 2 + NT * r + t + 1)
                if t % 4 == 0:
                    dve.wait_ge(o_stored[b % 2], 16 * (2 * r + b // 2 + 1))
                if near:
                    dst = o_st[:, b % 2, :].rearrange("p (r c) -> p r c", c=GW)[:, :, 16 * (t % 4):16 * (t % 4) + 16]
                    src = op[:, t % 2, 0:P].rearrange("p (r c) -> p r c", c=16)
                else:
                    dst, src = o_st[:, b % 2, (t % 4) * P:(t % 4 + 1) * P], op[:, t % 2, 0:P]
                nc.vector.tensor_copy(dst, src).then_inc(o_copied, 1)

            dve.sem_inc(exped, SN_BUFS)
            dve.sem_inc(shifted, UNITS)
            dve.sem_inc(o_copied, O_BANKS)
            for i in range(2):
                dve.sem_inc(o_stored[i], 16)
            if not near:
                dve.wait_ge(const_in, 48)
                nc.vector.tensor_scalar(sinks[:], sinks[:], -1.0, None, ALU.mult).then_inc(sinks_negated, 1)
                dve.wait_ge(sinks_negated, 1)
            stream(dve, [(0, shift), (NORM_LAG, normalise), (OUT_LAG, results)])

        @block.tensor
        def _(pe):
            def score(r, u):
                e, t = u % 2, u // 2
                b, n = t // 4, tiles.chunks(t) * P
                if u % 8 == 0:
                    for i in (b, min(b + 1, 3)):
                        pe.wait_ge(qk_in[i], arrived(r, 192, 64))
                pe.wait_ge(shifted, UNITS * (r + 1) - SC_BUFS + u + 1)
                q, out = q_st[:, e, t * P:(t + 1) * P], sc[:, u % 4, 0:n]
                pe.matmul(out, q, tiles.keys(k_hh[:, e, :], t), start=True, stop=False)
                pe.matmul(out, q, tiles.keys(k_ll[:, e, :], t), start=False, stop=True).then_inc(scored, 1)

            def arrived(r, first, more):
                return 192 * (r + 1) if near else 192 + 64 * r

            def turn(r, u):
                e, t = u % 2, u // 2
                c0, _, _ = tiles.score_cols(t)
                pe.wait_ge(probs_done, UNITS * r + u + 1)
                pe.wait_ge(pt_copied, UNITS * r + u + 1)
                for j in range(tiles.chunks(t)):
                    last = pe.transpose(tp[:, u % 2, j * P:(j + 1) * P], pr[:, e, c0 + j * P:c0 + (j + 1) * P],
                                        ident[:])
                last.then_inc(p_turned, 1)

            def values(r, u):
                if u % 2 == 0:
                    return
                t = u // 2
                b, n = t // 4, tiles.chunks(t)
                if t % 4 == 0:
                    for i in (b, min(b + 1, 3)):
                        g = tiles.portions[i]
                        pe.wait_ge(v_in[i], 64 * (g[1] - g[0]) * (r + 1) if near else 16)
                pe.wait_ge(pt_copied, PT_BANKS + UNITS * r + u + 1)
                pe.wait_ge(o_copied, NT * r + t + 1)
                for j in range(n):
                    v = v_sb[:, tiles.value_chunk(t, j), :]
                    for e in range(2):
                        h = slice(e * HD, (e + 1) * HD)
                        last = pe.matmul(op[h, t % 2, 0:P], v[:, h], pt[:, (u - 1 + e) % 4, j * P:(j + 1) * P],
                                         start=(j == 0), stop=(j == n - 1))
                last.then_inc(pv_done, 1)

            pe.sem_inc(p_turned, SN_BUFS)
            pe.sem_inc(pt_copied, PT_BANKS)
            pe.sem_inc(pv_done, PT_BUFS // 2)
            pe.wait_ge(const_in, 32 if near else 48)
            stream(pe, [(0, score), (TURN_LAG, turn), (PV_LAG, values)])


def half_phases(nc, half, x, w_out, g_na, g_swa, g_ffn, w_gate, w_up, w_down, g_final, ident_in,
                ones_in, o_dram, out):
    with ExitStack() as ctx:
        def sb(n, shape, dt=F32):
            return ctx.enter_context(nc.sbuf_tensor(f"{n}_{half}", shape, dt))

        x1 = sb("x1", [P, HT, D])
        hT_hi = sb("ffn_in_hi", [P, KT, HS], F32R)
        hT_lo = sb("ffn_in_lo", [P, KT, HS], F32R)
        mix_phase(nc, half, x, w_out, g_na, g_swa, g_ffn, ident_in, ones_in, o_dram, x1, hT_hi, hT_lo)
        feed_phase(nc, half, w_gate, w_up, w_down, g_final, x1, hT_hi, hT_lo, out)


def mix_phase(nc, half, x, w_out, g_na, g_swa, g_ffn, ident_in, ones_in, o_dram, x1, hT_hi, hT_lo):
    with ExitStack() as ctx:
        def sb(n, shape, dt=F32):
            return ctx.enter_context(nc.sbuf_tensor(f"mix_{n}_{half}", shape, dt))

        def sem(n):
            return nc.alloc_semaphore(f"mix_{n}_{half}")

        w_hi = sb("w_hi", [P, KT, D], F32R)
        w_lo = sb("w_lo", [P, KT, D], F32R)
        raw = sb("raw", [P, 2, D])
        ot = sb("o", [P, 2, KT, P])
        o_hi = sb("o_hi", [P, 2, KT, P], F32R)
        o_lo = sb("o_lo", [P, 2, KT, P], F32R)
        sq = sb("squares", [P, KT, P])
        sqs = sb("squares_summed", [P, 2, P])
        xn = sb("x_normed", [P, D])
        gffn = sb("g_ffn", [P, D])
        gcol = sb("g_out", [P, KT])
        ident = sb("ident", [P, P])
        ones = sb("ones", [P, 2])
        oms, oinv, orms = (sb(n, [P, HT, 2]) for n in ("o_mean", "o_inv", "o_rms"))
        ssq, msq, inv, rstd = (sb(n, [P, HT]) for n in ("ssq", "mean", "inv", "rstd"))
        mm = ctx.enter_context(nc.psum_tensor(f"mix_mm_{half}", [P, 4, BANK], F32))
        tp = ctx.enter_context(nc.psum_tensor(f"mix_turn_{half}", [P, 2 * BANK], F32))
        st = ctx.enter_context(nc.psum_tensor(f"mix_stat_{half}", [P, BANK], F32))

        raw_in = [sem(f"raw_in{i}") for i in range(2)]
        o_in = [sem(f"o_in{i}") for i in range(2)]
        x_in, const_in = sem("x_in"), sem("const_in")
        w_hi_done, w_lo_done = sem("w_hi_done"), sem("w_lo_done")
        o_squared, o_split_hi, o_split_lo = sem("o_squared"), sem("o_split_hi"), sem("o_split_lo")
        sq_summed, o_stat, o_mean, o_inv, o_rms = (sem(n) for n in ("sq_summed", "o_stat", "o_mean", "o_inv", "o_rms"))
        mm_done, added = sem("mm_done"), sem("added")
        squared, mean_done, inv_done, rstd_done = (sem(n) for n in ("squared", "mean_done", "inv_done", "rstd_done"))
        normed, turned, h_hi_done, h_lo_done = (sem(n) for n in ("normed", "turned", "h_hi_done", "h_lo_done"))

        block = ctx.enter_context(nc.Block())

        @block.sync
        def _(sp):
            def load_w(k):
                if k >= 2:
                    sp.wait_ge(w_lo_done, k - 1)
                if k < 4:
                    sp.dma_start(raw[:, k % 2, :], w_out[k * P:(k + 1) * P, :]).then_inc(raw_in[k % 2], 32)
                else:
                    for e in range(2):
                        r0 = AW + (k - 4 + 4 * e) * HD
                        sp.dma_start(raw[e * HD:(e + 1) * HD, k % 2, :], w_out[r0:r0 + HD, :]) \
                            .then_inc(raw_in[k % 2], 16)

            def load_tile(t):
                if t >= 2:
                    sp.wait_ge(o_split_lo, t - 1)
                    sp.wait_ge(o_squared, t - 1)
                toks = slice(half * HS + t * P, half * HS + (t + 1) * P)
                sp.dma_start(ot[:, t % 2], o_dram[:, toks].rearrange("(k p) s -> p k s", p=P)) \
                    .then_inc(o_in[t % 2], 16)

            with nc.allow_non_contiguous_dma(reason="gains, one for each partition"):
                sp.dma_start(gcol[:, 0:4], g_na.rearrange("a (k p) -> p (a k)", p=P)).then_inc(const_in, 16)
                for e in range(2):
                    sp.dma_start(gcol[e * HD:(e + 1) * HD, 4:8],
                                 g_swa[:, e * 4 * HD:(e + 1) * 4 * HD].rearrange("a (k p) -> p (a k)", p=HD)) \
                        .then_inc(const_in, 16)
            load_w(0)
            load_tile(0)
            load_w(1)
            sp.dma_start(ones[:], ones_in).then_inc(const_in, 16)
            load_tile(1)
            sp.dma_start(gffn[:], g_ffn.broadcast_to([P, D])).then_inc(const_in, 16)
            sp.dma_start(ident[:], ident_in).then_inc(const_in, 16)
            for k in range(2, KT):
                load_w(k)
            for t in range(HT):
                r0 = half * HS + t * P
                sp.dma_start(x1[:, t, :], x[r0:r0 + P, :]).then_inc(x_in, 16)
            for t in range(2, HT):
                load_tile(t)

        @block.scalar
        def _(act):
            def split_w(k):
                act.wait_ge(raw_in[k % 2], 32 * (k // 2 + 1))
                nc.scalar.mul(w_hi[:, k, :], raw[:, k % 2, :], gcol[:, k:k + 1]).then_inc(w_hi_done, 1)

            def take_tile(t):
                act.wait_ge(o_in[t % 2], 16 * (t // 2 + 1))
                if t >= 1:
                    act.wait_ge(sq_summed, t)
                nc.scalar.activation(sq[:], ot[:, t % 2], ACT.Square).then_inc(o_squared, 1)
                if t >= 2:
                    act.wait_ge(mm_done, 4 * (t - 1))
                nc.scalar.copy(o_hi[:, t % 2], ot[:, t % 2]).then_inc(o_split_hi, 1)

            def o_root(t):
                act.wait_ge(o_inv, t + 1)
                nc.scalar.activation(orms[:, t, :], oinv[:, t, :], ACT.Sqrt).then_inc(o_rms, 1)

            def norm(t):
                act.wait_ge(added, 4 * (t + 1))
                if t >= 1:
                    act.wait_ge(turned, t)
                nc.scalar.activation(xn[:], x1[:, t, :], ACT.Square, accum_out=ssq[:, t:t + 1]).then_inc(squared, 1)
                act.wait_ge(inv_done, t + 1)
                nc.scalar.activation(rstd[:, t:t + 1], inv[:, t:t + 1], ACT.Sqrt).then_inc(rstd_done, 1)

            def turn_hi(t):
                act.wait_ge(turned, t + 1)
                nc.scalar.copy(hT_hi[:, :, t * P:(t + 1) * P], tp[:].rearrange("p (k s) -> p k s", k=KT)) \
                    .then_inc(h_hi_done, 1)

            act.wait_ge(const_in, 96)
            take_tile(0)
            for k in range(KT):
                split_w(k)
                if k == 0:
                    o_root(0)
            for t in range(HT):
                if t + 1 < HT:
                    take_tile(t + 1)
                    o_root(t + 1)
                if t >= 1:
                    turn_hi(t - 1)
                norm(t)
            turn_hi(HT - 1)

        @block.vector
        def _(dve):
            def split_w(k):
                dve.wait_ge(w_hi_done, k + 1)
                nc.vector.scalar_tensor_tensor(out=w_lo[:, k, :], in0=raw[:, k % 2, :], scalar=gcol[:, k:k + 1],
                                               in1=w_hi[:, k, :], op0=ALU.mult, op1=ALU.subtract) \
                    .then_inc(w_lo_done, 1)

            def take_tile(t):
                dve.wait_ge(o_squared, t + 1)
                if t >= 1:
                    dve.wait_ge(o_stat, t)
                nc.vector.tensor_reduce(sqs[:], sq[:].rearrange("p (g k) s -> p g s k", g=2),
                                        mybir.AxisListType.X, ALU.add).then_inc(sq_summed, 1)
                dve.wait_ge(o_split_hi, t + 1)
                nc.vector.tensor_tensor(o_lo[:, t % 2], ot[:, t % 2], o_hi[:, t % 2], ALU.subtract) \
                    .then_inc(o_split_lo, 1)

            def o_means(t):
                dve.wait_ge(o_stat, t + 1)
                nc.vector.tensor_scalar(oms[:, t, :], st[:, 0:4:2], 1.0 / AW, EPS, ALU.mult, ALU.add) \
                    .then_inc(o_mean, 1)
                dve.wait_ge(o_mean, t + 1)
                nc.vector.reciprocal(oinv[:, t, :], oms[:, t, :]).then_inc(o_inv, 1)

            def add(t):
                dve.wait_ge(o_rms, t + 1)
                if t == 0:
                    dve.wait_ge(x_in, 16 * HT)
                for i in range(4):
                    n, g = i // 2, i % 2
                    dst = x1[:, t, n * BANK:(n + 1) * BANK]
                    dve.wait_ge(mm_done, 4 * t + i + 1)
                    if g:
                        dve.wait_ge(added, 4 * t + i)
                    nc.vector.scalar_tensor_tensor(out=dst, in0=mm[:, i, :], scalar=orms[:, t, g:g + 1], in1=dst,
                                                   op0=ALU.mult, op1=ALU.add).then_inc(added, 1)

            def norm(t):
                dve.wait_ge(squared, t + 1)
                nc.vector.tensor_scalar(msq[:, t:t + 1], ssq[:, t:t + 1], 1.0 / D, EPS, ALU.mult, ALU.add) \
                    .then_inc(mean_done, 1)
                dve.wait_ge(mean_done, t + 1)
                nc.vector.reciprocal(inv[:, t:t + 1], msq[:, t:t + 1]).then_inc(inv_done, 1)
                dve.wait_ge(rstd_done, t + 1)
                nc.vector.scalar_tensor_tensor(out=xn[:], in0=x1[:, t, :], scalar=rstd[:, t:t + 1], in1=gffn[:],
                                               op0=ALU.mult, op1=ALU.mult).then_inc(normed, 1)

            def turn_lo(t):
                toks = slice(t * P, (t + 1) * P)
                dve.wait_ge(h_hi_done, t + 1)
                nc.vector.tensor_tensor(hT_lo[:, :, toks], tp[:].rearrange("p (k s) -> p k s", k=KT),
                                        hT_hi[:, :, toks], ALU.subtract).then_inc(h_lo_done, 1)

            dve.wait_ge(const_in, 96)
            take_tile(0)
            o_means(0)
            for k in range(KT):
                split_w(k)
            for t in range(HT):
                if t + 1 < HT:
                    take_tile(t + 1)
                    o_means(t + 1)
                if t >= 1:
                    turn_lo(t - 1)
                add(t)
                norm(t)
            turn_lo(HT - 1)

        @block.tensor
        def _(pe):
            def stats(t):
                pe.wait_ge(sq_summed, t + 1)
                if t >= 1:
                    pe.wait_ge(o_mean, t)
                for g in range(2):
                    last = pe.matmul(st[:, 2 * g:2 * g + 2], sqs[:, g, :], ones[:], start=True, stop=True)
                last.then_inc(o_stat, 1)

            def turn(t):
                pe.wait_ge(normed, t + 1)
                if t >= 1:
                    pe.wait_ge(h_lo_done, t)
                for k in range(KT):
                    last = pe.transpose(tp[:, k * P:(k + 1) * P], xn[:, k * P:(k + 1) * P], ident[:])
                last.then_inc(turned, 1)

            pe.wait_ge(const_in, 96)
            stats(0)
            for t in range(HT):
                if t + 1 < HT:
                    stats(t + 1)
                pe.wait_ge(o_split_lo, t + 1)
                for i in range(4):
                    n, g = i // 2, i % 2
                    cols = slice(n * BANK, (n + 1) * BANK)
                    if t >= 1:
                        pe.wait_ge(added, 4 * (t - 1) + i + 1)
                    for k in range(4 * g, 4 * g + 4):
                        if t == 0 and n == 0:
                            pe.wait_ge(w_lo_done, k + 1)
                        pe.matmul(mm[:, i, :], o_hi[:, t % 2, k, :], w_hi[:, k, cols], start=(k % 4 == 0), stop=False)
                        pe.matmul(mm[:, i, :], o_hi[:, t % 2, k, :], w_lo[:, k, cols], start=False, stop=False)
                        last = pe.matmul(mm[:, i, :], o_lo[:, t % 2, k, :], w_hi[:, k, cols], start=False,
                                         stop=(k % 4 == 3))
                    last.then_inc(mm_done, 1)
                if t >= 1:
                    turn(t - 1)
            turn(HT - 1)


def feed_phase(nc, half, w_gate, w_up, w_down, g_final, x1, hT_hi, hT_lo, out):
    STEPS = FF // P // 2
    TBS = HS // BANK
    DOWNS = HT * 2
    with ExitStack() as ctx:
        def sb(n, shape, dt=F32):
            return ctx.enter_context(nc.sbuf_tensor(f"ff_{n}_{half}", shape, dt))

        def sem(n):
            return nc.alloc_semaphore(f"ff_{n}_{half}")

        gu_hi = sb("gu_hi", [P, 2, 2, KT, P], F32R)
        gu_lo = sb("gu_lo", [P, 2, 2, KT, P], F32R)
        gu_raw = sb("gu_raw", [P, 2, KT, P])
        d_hi = sb("down_hi", [P, 2, D], F32R)
        d_lo = sb("down_lo", [P, 2, D], F32R)
        d_raw = sb("down_raw", [P, 2, D])
        a_hi = sb("act_hi", [P, 2, 2, HS], F32R)
        a_lo = sb("act_lo", [P, 2, 2, HS], F32R)
        silu = sb("silu", [P, 2, BANK])
        prod = sb("prod", [P, 2, BANK])
        gfin = sb("g_final", [P, D])
        ssq, msq, inv, rstd = (sb(n, [P, HT]) for n in ("ssq", "mean", "inv", "rstd"))
        gu = ctx.enter_context(nc.psum_tensor(f"ff_gu_{half}", [P, 4, BANK], F32))
        dn = ctx.enter_context(nc.psum_tensor(f"ff_down_{half}", [P, 4, BANK], F32))

        gu_in = [sem(f"gu_in{i}") for i in range(2)]
        d_in, const_in = sem("down_in"), sem("const_in")
        gu_hi_done, gu_lo_done = sem("gu_hi_done"), sem("gu_lo_done")
        d_hi_done, d_lo_done = sem("d_hi_done"), sem("d_lo_done")
        gu_done, silu_done, prod_done = sem("gu_done"), sem("silu_done"), sem("prod_done")
        a_hi_done, a_lo_done = sem("a_hi_done"), sem("a_lo_done")
        down_done, added = sem("down_done"), sem("added")
        squared, mean_done, inv_done, rstd_done, normed = (
            sem(n) for n in ("squared", "mean_done", "inv_done", "rstd_done", "normed"))
        out_stored = sem("out_stored")

        block = ctx.enter_context(nc.Block())
        gate_v = w_gate.rearrange("(k p) n -> p k n", p=P)
        up_v = w_up.rearrange("(k p) n -> p k n", p=P)

        RAW = 2

        @block.sync
        def _(sp):
            def load_gu(i, f):
                for w, view in enumerate((gate_v, up_v)):
                    sp.wait_ge(gu_lo_done, 4 * i + 2 * f + w + 1)
                    sp.dma_start(gu_raw[:, w], view[:, :, bass.ds((2 * i + f) * P, P)]).then_inc(gu_in[w], 16)

            def load_d(i):
                sp.wait_ge(d_lo_done, i + 1)
                sp.dma_start(d_raw[:], w_down[bass.ds(2 * i * P, 2 * P), :].rearrange("(f p) n -> p f n", p=P)) \
                    .then_inc(d_in, 16)

            load_gu(0, 0)
            load_gu(0, 1)
            load_d(0)
            sp.dma_start(gfin[:], g_final.broadcast_to([P, D])).then_inc(const_in, 16)
            with sp.Fori(1, STEPS) as i:
                load_gu(i, 0)
                load_gu(i, 1)
                load_d(i)
            for t in range(HT):
                sp.wait_ge(normed, t + 1)
                r0 = half * HS + t * P
                sp.dma_start(out[r0:r0 + P, :], x1[:, t, :]).then_inc(out_stored, 16)
            sp.wait_ge(out_stored, 16 * HT)

        def steps(eng, tile, down, split_gu, split_d):
            split_gu(0, 0)
            split_gu(0, 1)
            split_d(0)
            tile(0, 0, 0)
            split_gu(1, 0)
            tile(0, 1, 0)
            split_gu(1, 1)

            def body(i, par, last=False):
                tile(i, 0, par)
                if not last:
                    split_gu(i + 1, 0)
                down(i - 1, 1 - par)
                split_d(i)
                tile(i, 1, par)
                if not last:
                    split_gu(i + 1, 1)

            with eng.Fori(0, (STEPS - 3) // 2) as j:
                body(2 * j + 1, 1)
                body(2 * j + 2, 0)
            body(STEPS - 2, 1)
            body(STEPS - 1, 0, last=True)

        @block.scalar
        def _(act):
            def split_gu(i, f):
                for w in range(2):
                    if not (isinstance(i, int) and i == 0):
                        act.wait_ge(gu_done, 4 * (i - 1) + 2 * f + 2)
                    act.wait_ge(gu_in[w], 16 * (2 * i + f + 1))
                    nc.scalar.copy(gu_hi[:, f, w], gu_raw[:, w]).then_inc(gu_hi_done, 1)

            def split_d(i):
                if not (isinstance(i, int) and i == 0):
                    act.wait_ge(down_done, DOWNS * i)
                act.wait_ge(d_in, 16 * (i + 1))
                nc.scalar.copy(d_hi[:], d_raw[:]).then_inc(d_hi_done, 1)

            def tile(i, f, par):
                for tb in range(TBS):
                    n = 4 * i + 2 * f + tb
                    act.wait_ge(gu_done, n + 1)
                    act.wait_ge(prod_done, n + 1)
                    nc.scalar.activation(silu[:, tb], gu[:, 2 * tb], ACT.Silu).then_inc(silu_done, 1)
                    act.wait_ge(prod_done, n + 3)
                    nc.scalar.copy(a_hi[:, par, f, tb * BANK:(tb + 1) * BANK], prod[:, tb]).then_inc(a_hi_done, 1)

            def down(i, par):
                pass

            steps(act, tile, down, split_gu, split_d)
            spare = silu[:].rearrange("p a b -> p (a b)")
            for t in range(HT):
                act.wait_ge(added, 4 + DOWNS * (STEPS - 1) + 2 * (t + 1))
                nc.scalar.activation(spare, x1[:, t, :], ACT.Square, accum_out=ssq[:, t:t + 1]) \
                    .then_inc(squared, 1)
                act.wait_ge(inv_done, t + 1)
                nc.scalar.activation(rstd[:, t:t + 1], inv[:, t:t + 1], ACT.Sqrt).then_inc(rstd_done, 1)

        @block.vector
        def _(dve):
            def split_gu(i, f):
                for w in range(2):
                    dve.wait_ge(gu_hi_done, 4 * i + 2 * f + w + 1)
                    nc.vector.tensor_tensor(gu_lo[:, f, w], gu_raw[:, w], gu_hi[:, f, w], ALU.subtract) \
                        .then_inc(gu_lo_done, 1)

            def split_d(i):
                dve.wait_ge(d_hi_done, i + 1)
                nc.vector.tensor_tensor(d_lo[:], d_raw[:], d_hi[:], ALU.subtract).then_inc(d_lo_done, 1)

            def tile(i, f, par):
                for tb in range(TBS):
                    n = 4 * i + 2 * f + tb
                    dve.wait_ge(silu_done, n + 1)
                    nc.vector.tensor_tensor(prod[:, tb], gu[:, 2 * tb + 1], silu[:, tb], ALU.mult).then_inc(prod_done, 1)
                    dve.wait_ge(a_hi_done, n + 1)
                    nc.vector.tensor_tensor(a_lo[:, par, f, tb * BANK:(tb + 1) * BANK], prod[:, tb],
                                            a_hi[:, par, f, tb * BANK:(tb + 1) * BANK], ALU.subtract) \
                        .then_inc(a_lo_done, 1)

            def add(i, m):
                t, n = m // 2, m % 2
                dst = x1[:, t, n * BANK:(n + 1) * BANK]
                dve.wait_ge(down_done, DOWNS * i + m + 1)
                nc.vector.tensor_tensor(dst, dn[:, m % 4], dst, ALU.add).then_inc(added, 1)

            def down(i, par):
                for m in range(DOWNS):
                    add(i, m)

            def final(t):
                dve.wait_ge(squared, t + 1)
                nc.vector.tensor_scalar(msq[:, t:t + 1], ssq[:, t:t + 1], 1.0 / D, EPS, ALU.mult, ALU.add) \
                    .then_inc(mean_done, 1)
                dve.wait_ge(mean_done, t + 1)
                nc.vector.reciprocal(inv[:, t:t + 1], msq[:, t:t + 1]).then_inc(inv_done, 1)
                dve.wait_ge(rstd_done, t + 1)
                nc.vector.scalar_tensor_tensor(out=x1[:, t, :], in0=x1[:, t, :], scalar=rstd[:, t:t + 1], in1=gfin[:],
                                               op0=ALU.mult, op1=ALU.mult).then_inc(normed, 1)

            dve.sem_inc(gu_lo_done, RAW)
            dve.sem_inc(d_lo_done, 1)
            dve.sem_inc(prod_done, 2)
            dve.sem_inc(added, 4)
            steps(dve, tile, down, split_gu, split_d)
            dve.wait_ge(const_in, 16)
            for m in range(DOWNS):
                add(STEPS - 1, m)
                if m % 2 and m >= 3:
                    final(m // 2 - 1)
            final(HT - 1)

        @block.tensor
        def _(pe):
            def split_gu(i, f):
                pass

            def split_d(i):
                pass

            def tile(i, f, par):
                for tb in range(TBS):
                    toks = slice(tb * BANK, (tb + 1) * BANK)
                    pe.wait_ge(prod_done, 4 * i + 2 * f + tb + 1)
                    for w in range(2):
                        bank = gu[:, 2 * tb + w]
                        pe.wait_ge(gu_lo_done, RAW + 4 * i + 2 * f + w + 1)
                        for k in range(KT):
                            hi, lo = gu_hi[:, f, w, k, :], gu_lo[:, f, w, k, :]
                            pe.matmul(bank, hi, hT_hi[:, k, toks], start=(k == 0), stop=False)
                            pe.matmul(bank, hi, hT_lo[:, k, toks], start=False, stop=False)
                            last = pe.matmul(bank, lo, hT_hi[:, k, toks], start=False, stop=(k == KT - 1))
                    last.then_inc(gu_done, 1)

            def down(i, par):
                pe.wait_ge(d_lo_done, i + 2)
                pe.wait_ge(a_lo_done, 4 * (i + 1))
                for m in range(DOWNS):
                    t, n = m // 2, m % 2
                    toks, cols = slice(t * P, (t + 1) * P), slice(n * BANK, (n + 1) * BANK)
                    pe.wait_ge(added, DOWNS * i + m + 1)
                    for f in range(2):
                        hi, lo = a_hi[:, par, f, toks], a_lo[:, par, f, toks]
                        pe.matmul(dn[:, m % 4], hi, d_hi[:, f, cols], start=(f == 0), stop=False)
                        pe.matmul(dn[:, m % 4], hi, d_lo[:, f, cols], start=False, stop=False)
                        last = pe.matmul(dn[:, m % 4], lo, d_hi[:, f, cols], start=False, stop=(f == 1))
                    last.then_inc(down_done, 1)

            steps(pe, tile, down, split_gu, split_d)
            down(STEPS - 1, 0)


def rope_tables():
    freq = np.float32(500000.0) ** (-np.arange(0, ROPE, 2, dtype=np.float32) / np.float32(ROPE))
    angle = np.arange(S, dtype=np.float32)[:, None] * freq[None, :]
    cos, sin = np.cos(angle), np.sin(angle)
    return np.concatenate([cos, cos], 1), np.concatenate([-sin, sin], 1)


def neighbour_masks():
    out = np.zeros((P, 3, 1280), np.float32)
    for ck, cb in enumerate((0, 1, 3)):
        at = 0
        for band in (0, 1, 3):
            row0, rows = key_rows(band)
            qr, qc = np.arange(P) // 16 + 8 * band, np.arange(P) % 16 + 16 * cb
            kr, kc = row0 + np.arange(rows), key_col(cb) + np.arange(32)
            r0, c0 = np.clip(qr - 4, 0, S // GW - 8), np.clip(qc - 8, 0, GW - 16)
            rok = (kr >= r0[:, None]) & (kr < r0[:, None] + 8)
            cok = (kc >= c0[:, None]) & (kc < c0[:, None] + 16)
            ok = rok[:, :, None] & cok[:, None, :]
            out[:, ck, at:at + rows * 32] = np.where(ok, 0.0, MASKED).reshape(P, -1)
            at += rows * 32
    return out


def key_rows(band):
    return (0, 12) if band == 0 else (8 * band - 4, 16 if band < 3 else 12)


def key_col(cb):
    return min(max(16 * cb - 8, 0), GW - 32)


def window_mask():
    q, k = np.arange(P)[:, None], np.arange(3 * P)[None, :] - P
    return np.where(np.abs(q - k) <= 128, 0.0, MASKED).astype(np.float32)


def kernel(x, g_norm_mix, w_in, na_rpb, swa_sink, g_out_na, g_out_swa, w_out, g_norm_ffn, w_gate,
           w_up, w_down, g_final):
    import concourse.bacc as _bacc
    from concourse.bass_utils import run_bass_kernel_spmd as _run

    nc = _bacc.Bacc("TRN2", target_bir_lowering=False, num_devices=1)
    cos2, sin2 = rope_tables()
    given = {
        "x": np.asarray(x).reshape(S, D), "g_mix": np.asarray(g_norm_mix), "w_in": np.asarray(w_in)[0],
        "rpb": np.asarray(na_rpb)[0], "sink": np.asarray(swa_sink), "g_na": np.asarray(g_out_na),
        "g_swa": np.asarray(g_out_swa), "w_out": np.asarray(w_out)[0], "g_ffn": np.asarray(g_norm_ffn),
        "w_gate": np.asarray(w_gate)[0], "w_up": np.asarray(w_up)[0], "w_down": np.asarray(w_down)[0],
        "g_final": np.asarray(g_final).reshape(1, D),
        "cos2": cos2, "sin2": sin2, "ident": np.eye(P, dtype=np.float32),
        "na_mask": neighbour_masks(), "swa_mask": window_mask(),
        "zeros": np.zeros(NAH * PAD_R * PAD_C, np.float32), "ones": np.ones((P, 2), np.float32),
    }
    given = {k: np.ascontiguousarray(v) for k, v in given.items()}
    aps = {k: nc.dram_tensor(f"in_{k}", v.shape, F32, kind="ExternalInput").ap() for k, v in given.items()}
    out = nc.dram_tensor("out_0", (S, D), F32, kind="ExternalOutput").ap()
    program(nc, aps, out)
    r = _run(nc, [{f"in_{k}": v for k, v in given.items()}], core_ids=[0])
    return r.results[0]["out_0"].reshape(1, S, D)


def program(nc, a, out, phases=4):
    qk_dram = nc.dram_tensor("qk_scratch", (2, HEADS * HD, S), F32).ap()
    v_dram = nc.dram_tensor("v_scratch", (S, V_WIDTH), F32).ap()
    pad_dram = nc.dram_tensor("pad_scratch", (NAH, PAD_R, PAD_C), F32).ap()
    rel_dram = nc.dram_tensor("rel_scratch", (NAH, P, ROWS_REL * COLS_REL), F32).ap()
    o_dram = nc.dram_tensor("o_scratch", (D, S), F32).ap()
    with nc.cleanup_on_exit():
        project_phase(nc, a["x"], a["g_mix"], a["w_in"], a["rpb"], a["cos2"], a["sin2"], a["ident"],
                      a["zeros"], qk_dram, v_dram, pad_dram, rel_dram)
        attention_phase(nc, True, qk_dram, v_dram, rel_dram, a["na_mask"], a["sink"], a["ident"], o_dram)
        attention_phase(nc, False, qk_dram, v_dram, rel_dram, a["swa_mask"], a["sink"], a["ident"], o_dram)
    nc.all_engine_barrier()
    if phases == 3:
        return
    for half in range(2):
        half_phases(nc, half, a["x"], a["w_out"], a["g_na"], a["g_swa"], a["g_ffn"], a["w_gate"], a["w_up"],
                    a["w_down"], a["g_final"], a["ident"], a["ones"], o_dram, out)
```

```python
from contextlib import ExitStack

import numpy as np
import concourse.bass as bass
from concourse import mybir

ALU = mybir.AluOpType
ACT = mybir.ActivationFunctionType
F32 = mybir.dt.float32
F32R = mybir.dt.float32r

P = 128
BANK = 512
D = 1024
S = 2048
HD = 64
GW = 64
NAH, SWH, SWKV = 8, 8, 2
AW = NAH * HD
KT = D // P
NT = S // P
HS = S // 2
HT = NT // 2
FF = 2816
EPS = 1e-6
SCALE = HD ** -0.5
HEADS = 2 * NAH + SWH + SWKV
V_WIDTH = AW + SWKV * HD
ROPE = HD // 4
HALF = ROPE // 2
MASKED = 1e30
ROWS_REL, COLS_REL = 16, 48
PAD_R, PAD_C = 23, 63


def project_phase(nc, x, g_mix, w_in, rpb, cos2, sin2, ident_in, zeros_in, qk_dram, v_dram,
                  pad_dram, rel_dram):
    with ExitStack() as ctx:
        def sb(name, shape, dt=F32):
            return ctx.enter_context(nc.sbuf_tensor(name, shape, dt))

        def sem(name):
            return nc.alloc_semaphore(name)

        XS, RAW = 3, 4
        hT_hi = sb("hT_hi", [P, KT, S], F32R)
        hT_lo = sb("hT_lo", [P, KT, S], F32R)
        w_hi = sb("w_hi", [P, KT, BANK], F32R)
        w_lo = sb("w_lo", [P, KT, BANK], F32R)
        raw = sb("w_raw", [P, RAW, 1024])
        xt = sb("x_tile", [P, XS, D])
        xn = sb("x_normed", [P, D])
        gmix = sb("g_mix_rows", [P, D])
        ident = sb("ident1", [P, P])
        out_hi = sb("stage_hi", [P, 2, BANK], F32R)
        out_lo = sb("stage_lo", [P, 2, BANK], F32R)
        cosb = sb("cos_rows", [P, NT, ROPE])
        sinb = sb("sin_rows", [P, NT, ROPE])
        rope_c = sb("rope_c", [P, SWH, ROPE])
        rope_s = sb("rope_s", [P, SWH, ROPE])
        ssq = sb("ssq1", [P, NT])
        msq = sb("msq1", [P, NT])
        inv = sb("inv1", [P, NT])
        rstd = sb("rstd1", [P, NT])
        tok = xt
        mm = ctx.enter_context(nc.psum_tensor("proj_psum", [P, 4, BANK], F32))
        tp = ctx.enter_context(nc.psum_tensor("turn_psum", [P, 2, 2 * BANK], F32))

        x_in = [sem(f"x_in{i}") for i in range(XS)]
        w_arrived = [sem(f"w_arrived{i}") for i in range(RAW)]
        const_in, rope_in = sem("const_in1"), sem("rope_in")
        squared, mean_done, inv_done = sem("squared"), sem("mean_done"), sem("inv_done")
        rstd_done, normed, turned = sem("rstd_done"), sem("normed"), sem("turned")
        h_hi_done, h_lo_done = sem("h_hi_done"), sem("h_lo_done")
        w_hi_done, w_lo_done = sem("w_hi_done"), sem("w_lo_done")
        proj_done, panel_read = sem("proj_done"), sem("panel_read")
        res_hi, res_lo = sem("res_hi"), sem("res_lo")
        tok_done, rope_step, roped, tok_turned = sem("tok_done"), sem("rope_step"), sem("roped"), sem("tok_turned")
        stored = [sem(f"stored{i}") for i in range(2)]
        v_stored = [sem(f"v_stored{i}") for i in range(2)]
        table_made = sem("table_made")

        slices = [(p, slice(0, KT), slice(g * P, (g + 1) * P)) for p in (0, 1) for g in range(4)]
        slices += [(p, slice(2 * i, 2 * i + 2), slice(0, BANK)) for p in (2, 3) for i in range(4)]
        slices += [(4, slice(4 * i, 4 * i + 4), slice(0, 256)) for i in range(2)]
        w_view = w_in.rearrange("(k p) n -> p k n", p=P)
        x_view = x.rearrange("(t p) d -> t p d", p=P)
        AHEAD = 6
        QK_STEPS = 32
        STEPS = QK_STEPS + 3 * NT

        block = ctx.enter_context(nc.Block())

        def raw_of(n):
            _, ks, _ = slices[n]
            return raw[:, n % RAW, :].rearrange("p (k n) -> p k n", k=ks.stop - ks.start)

        def w_part(w, n):
            _, ks, cs = slices[n]
            return w[:, ks, cs]

        def staged(stage, m):
            order = "p (b r c) -> p r b c" if m < 16 else "p (r b c) -> p r b c"
            return stage[:, m % 2, :].rearrange(order, b=4, c=16)

        def result(m):
            return mm[:, m % 4, :].rearrange("p (r b c) -> p r b c", b=4, c=16)

        def split_at(m):
            return {12: [4], 13: [5], 14: [6], 15: [7], QK_STEPS - 1: [8, 9, 10, 11],
                    QK_STEPS + NT - 1: [12, 13, 14, 15], QK_STEPS + 2 * NT - 1: [16, 17]}.get(m, [])

        def wait_panel(eng, n):
            if 4 <= n < 8:
                eng.wait_ge(proj_done, 12 + n - 4 + 1)
            elif 8 <= n < 12:
                eng.wait_ge(proj_done, QK_STEPS)
            elif n in (15, 17):
                eng.wait_ge(proj_done, QK_STEPS + (NT if n == 15 else 2 * NT))
            elif n >= 12:
                eng.wait_ge(panel_read, n - 11)

        def wait_tok_slot(eng, t):
            u = t - 2
            if u < 0:
                return
            if u < NT:
                eng.wait_ge(v_stored[u % 2], 16 * (u // 2 + 1))
            else:
                eng.wait_ge(tok_turned, u - NT + 1)
            if u >= 2 * NT:
                eng.wait_ge(v_stored[u % 2], 16 * (NT // 2 + (u - 2 * NT) // 2 + 1))

        @block.sync
        def _(sp):
            def load_w(n):
                if n >= RAW:
                    sp.wait_ge(w_lo_done, n - RAW + 1)
                p, ks, cs = slices[n]
                sp.dma_start(raw_of(n), w_view[:, ks, p * 512 + cs.start:p * 512 + cs.stop]) \
                  .then_inc(w_arrived[n % RAW], 16)

            sp.dma_start(ident[:], ident_in).then_inc(const_in, 16)
            for n in range(8):
                load_w(n)
            for m in range(QK_STEPS):
                p, tb, g = m // 16, m // 4 % 4, m % 4
                r0 = p * 512 + g * P
                sp.wait_ge(res_lo, m + 1)
                for part, stage in enumerate((out_hi, out_lo)):
                    sp.dma_start(qk_dram[part, r0:r0 + P, tb * BANK:(tb + 1) * BANK],
                                 stage[:, m % 2, :].bitcast(F32)).then_inc(stored[m % 2], 16)
                if m == 15:
                    for n in range(8, 12):
                        load_w(n)
            for n in range(12, 16):
                load_w(n)
            for t in range(3 * NT):
                p, tt = 2 + t // NT, t % NT
                rows = slice(tt * P, (tt + 1) * P)
                m = QK_STEPS + t - NT
                if p == 2:
                    sp.wait_ge(tok_done, t + 1)
                    sp.dma_start(v_dram[rows, 0:AW], tok[:, t % 2, 0:AW]).then_inc(v_stored[t % 2], 16)
                    continue
                if p == 4:
                    sp.wait_ge(tok_done, t + 1)
                    sp.dma_start(v_dram[rows, AW:V_WIDTH], tok[:, t % 2, P:2 * P]) \
                        .then_inc(v_stored[t % 2], 16)
                if t == NT:
                    for n in (16, 17):
                        load_w(n)
                sp.wait_ge(res_lo, m + 1)
                for part, stage in enumerate((out_hi, out_lo)):
                    if p == 3:
                        dst = qk_dram[part, 8 * P:12 * P, rows].rearrange("(g p) s -> p g s", p=P)
                        src = stage[:, m % 2, :].bitcast(F32).rearrange("p (g s) -> p g s", g=4)
                    else:
                        dst, src = qk_dram[part, 12 * P:13 * P, rows], stage[:, m % 2, 0:P].bitcast(F32)
                    sp.dma_start(dst, src).then_inc(stored[m % 2], 16)
            for i in range(2):
                sp.wait_ge(stored[i], 16 * (QK_STEPS + 2 * NT))
                sp.wait_ge(v_stored[i], 16 * NT)

        @block.gpsimd
        def _(pool):
            pool.dma_start(cosb[:], cos2.rearrange("(t p) c -> p t c", p=P)).then_inc(rope_in, 16)
            pool.dma_start(sinb[:], sin2.rearrange("(t p) c -> p t c", p=P)).then_inc(rope_in, 16)
            pool.dma_start(pad_dram.rearrange("h r c -> (h r c)"), zeros_in).then_inc(table_made, 16)
            pool.wait_ge(table_made, 16)
            with nc.allow_non_contiguous_dma(reason="small table"):
                pool.dma_start(pad_dram[:, 4:19, 16:47], rpb).then_inc(table_made, 16)
            pool.wait_ge(table_made, 32)
            for h in range(NAH):
                for qr in range(8):
                    src = bass.AP(pad_dram.tensor, (h * PAD_R + 7 - qr) * PAD_C + 15,
                                  [[PAD_C, ROWS_REL], [-1, 16], [1, COLS_REL]])
                    dst = rel_dram[h, qr * 16:(qr + 1) * 16, :].rearrange("q (j c) -> j q c", c=COLS_REL)
                    pool.dma_start(dst, src).then_inc(table_made, 16)
            pool.wait_ge(table_made, 16 * (2 + 8 * NAH))

        @block.scalar
        def _(act):
            def load_x(t):
                act.dma_start(xt[:, t % XS, :], x_view[t]).then_inc(x_in[t % XS], 16)

            load_x(0)
            act.dma_start(gmix[:], g_mix.broadcast_to([P, D])).then_inc(const_in, 16)
            load_x(1)
            load_x(2)

            def norm_step(n):
                t = n - 1
                if 0 <= t < NT:
                    act.wait_ge(turned, t + 1)
                    nc.scalar.copy(hT_hi[:, :, t * P:(t + 1) * P],
                                   tp[:, t % 2, :].rearrange("p (k s) -> p k s", k=KT)).then_inc(h_hi_done, 1)
                if n < NT:
                    act.wait_ge(x_in[n % XS], 16 * (n // XS + 1))
                    if 1 <= n <= NT - XS:
                        load_x(n - 1 + XS)
                    nc.scalar.activation(xn[:], xt[:, n % XS, :], ACT.Square,
                                         accum_out=ssq[:, n:n + 1]).then_inc(squared, 1)
                    act.wait_ge(inv_done, n + 1)
                    nc.scalar.activation(rstd[:, n:n + 1], inv[:, n:n + 1], ACT.Sqrt).then_inc(rstd_done, 1)

            def split_hi(n):
                wait_panel(act, n)
                act.wait_ge(w_arrived[n % RAW], 16 * (n // RAW + 1))
                nc.scalar.mul(w_part(w_hi, n), raw_of(n), -SCALE if n < 4 else 1.0).then_inc(w_hi_done, 1)

            def turn_hi(t):
                m, w = QK_STEPS + t - NT, 4 * P if t < 2 * NT else P
                act.wait_ge(tok_turned, t - NT + 1)
                act.wait_ge(stored[m % 2], 32 * (m // 2))
                nc.scalar.copy(out_hi[:, m % 2, 0:w], tp[:, t % 2, 0:w]).then_inc(res_hi, 1)

            for n in range(AHEAD):
                norm_step(n)
                if n < 4:
                    split_hi(n)
            for m in range(QK_STEPS):
                act.wait_ge(proj_done, m + 1)
                if m >= 2:
                    act.wait_ge(stored[m % 2], 32 * (m // 2))
                nc.scalar.copy(staged(out_hi, m), result(m)).then_inc(res_hi, 1)
                if m + AHEAD < NT + 1:
                    norm_step(m + AHEAD)
                for n in split_at(m):
                    split_hi(n)
            for t in range(3 * NT):
                m, w = QK_STEPS + t, BANK if t < 2 * NT else 2 * P
                act.wait_ge(proj_done, m + 1)
                wait_tok_slot(act, t)
                nc.scalar.mul(tok[:, t % 2, 0:w], mm[:, m % 4, 0:w],
                              -SCALE if NT <= t < 2 * NT else 1.0).then_inc(tok_done, 1)
                if t > NT:
                    turn_hi(t - 1)
                for n in split_at(m):
                    split_hi(n)
            turn_hi(3 * NT - 1)

        @block.vector
        def _(dve):
            def norm_step(n):
                t = n - 1
                if 0 <= t < NT:
                    dve.wait_ge(h_hi_done, t + 1)
                    nc.vector.tensor_tensor(hT_lo[:, :, t * P:(t + 1) * P],
                                            tp[:, t % 2, :].rearrange("p (k s) -> p k s", k=KT),
                                            hT_hi[:, :, t * P:(t + 1) * P], ALU.subtract).then_inc(h_lo_done, 1)
                if n < NT:
                    dve.wait_ge(squared, n + 1)
                    nc.vector.tensor_scalar(msq[:, n:n + 1], ssq[:, n:n + 1], 1.0 / D, EPS,
                                            ALU.mult, ALU.add).then_inc(mean_done, 1)
                    dve.wait_ge(mean_done, n + 1)
                    nc.vector.reciprocal(inv[:, n:n + 1], msq[:, n:n + 1]).then_inc(inv_done, 1)
                    dve.wait_ge(rstd_done, n + 1)
                    nc.vector.scalar_tensor_tensor(out=xn[:], in0=xt[:, n % XS, :], scalar=rstd[:, n:n + 1],
                                                   in1=gmix[:], op0=ALU.mult, op1=ALU.mult).then_inc(normed, 1)

            def split_lo(n):
                dve.wait_ge(w_hi_done, n + 1)
                nc.vector.scalar_tensor_tensor(out=w_part(w_lo, n), in0=raw_of(n),
                                               scalar=-SCALE if n < 4 else 1.0, in1=w_part(w_hi, n),
                                               op0=ALU.mult, op1=ALU.subtract).then_inc(w_lo_done, 1)

            def rope(t):
                heads, tt, done = (SWH, t % NT, 3 * (t - NT)) if t < 2 * NT else (SWKV, t % NT, 3 * (t - NT))
                v = tok[:, t % 2, 0:heads * HD].rearrange("p (h d) -> p h d", d=HD)
                cos = cosb[:, tt:tt + 1, :].broadcast_to([P, heads, ROPE])
                sin = sinb[:, tt:tt + 1, :].broadcast_to([P, heads, ROPE])
                dve.wait_ge(tok_done, t + 1)
                nc.vector.tensor_tensor(rope_c[:, 0:heads, :], v[:, :, 0:ROPE], cos, ALU.mult).then_inc(rope_step, 1)
                nc.vector.tensor_tensor(rope_s[:, 0:heads, 0:HALF], v[:, :, HALF:ROPE], sin[:, :, 0:HALF],
                                        ALU.mult).then_inc(rope_step, 1)
                nc.vector.tensor_tensor(rope_s[:, 0:heads, HALF:ROPE], v[:, :, 0:HALF], sin[:, :, HALF:ROPE],
                                        ALU.mult).then_inc(rope_step, 1)
                dve.wait_ge(rope_step, done + 3)
                nc.vector.tensor_tensor(v[:, :, 0:ROPE], rope_c[:, 0:heads, :], rope_s[:, 0:heads, :],
                                        ALU.add).then_inc(roped, 1)
                dve.wait_ge(roped, t - NT + 1)

            def turn_lo(t):
                m, w = QK_STEPS + t - NT, 4 * P if t < 2 * NT else P
                dve.wait_ge(res_hi, m + 1)
                nc.vector.tensor_tensor(out_lo[:, m % 2, 0:w], tp[:, t % 2, 0:w], out_hi[:, m % 2, 0:w],
                                        ALU.subtract).then_inc(res_lo, 1)

            dve.wait_ge(const_in, 32)
            for n in range(AHEAD):
                norm_step(n)
                if n < 4:
                    split_lo(n)
            for m in range(QK_STEPS):
                dve.wait_ge(res_hi, m + 1)
                nc.vector.tensor_tensor(staged(out_lo, m), result(m), staged(out_hi, m), ALU.subtract) \
                    .then_inc(res_lo, 1)
                if m + AHEAD < NT + 1:
                    norm_step(m + AHEAD)
                for n in split_at(m):
                    split_lo(n)
            dve.wait_ge(rope_in, 32)
            for t in range(3 * NT):
                if t >= NT:
                    rope(t)
                if t > NT:
                    turn_lo(t - 1)
                for n in split_at(QK_STEPS + t):
                    split_lo(n)
            turn_lo(3 * NT - 1)

        @block.tensor
        def _(pe):
            def turn_tile(n):
                pe.wait_ge(normed, n + 1)
                if n >= 2:
                    pe.wait_ge(h_lo_done, n - 1)
                for k in range(KT):
                    last = pe.transpose(tp[:, n % 2, k * P:(k + 1) * P], xn[:, k * P:(k + 1) * P], ident[:])
                last.then_inc(turned, 1)

            def turn_tok(t):
                pe.wait_ge(roped, t - NT + 1)
                if t - NT >= 2:
                    pe.wait_ge(res_lo, QK_STEPS + t - NT - 1)
                for g in range(4 if t < 2 * NT else 1):
                    last = pe.transpose(tp[:, t % 2, g * P:(g + 1) * P], tok[:, t % 2, g * P:(g + 1) * P], ident[:])
                last.then_inc(tok_turned, 1)

            pe.wait_ge(const_in, 32)
            for n in range(AHEAD - 1):
                turn_tile(n)
            for m in range(QK_STEPS):
                p, tb, g = m // 16, m // 4 % 4, m % 4
                cols, toks = slice(g * P, (g + 1) * P), slice(tb * BANK, (tb + 1) * BANK)
                pe.wait_ge(w_lo_done, 4 * p + g + 1)
                pe.wait_ge(h_lo_done, min(4 * tb + 4, NT) if p == 0 else NT)
                if m >= 4:
                    pe.wait_ge(res_lo, m - 3)
                for k in range(KT):
                    pe.matmul(mm[:, m % 4, :], w_hi[:, k, cols], hT_hi[:, k, toks], start=(k == 0), stop=False)
                    pe.matmul(mm[:, m % 4, :], w_hi[:, k, cols], hT_lo[:, k, toks], start=False, stop=False)
                    last = pe.matmul(mm[:, m % 4, :], w_lo[:, k, cols], hT_hi[:, k, toks], start=False,
                                     stop=(k == KT - 1))
                last.then_inc(proj_done, 1)
                if m + AHEAD - 1 < NT:
                    turn_tile(m + AHEAD - 1)
            for t in range(3 * NT):
                m, p = QK_STEPS + t, 2 + t // NT
                w, toks = BANK if p < 4 else 2 * P, slice(t % NT * P, (t % NT + 1) * P)
                if t < 4:
                    pe.wait_ge(res_lo, m - 3)
                else:
                    pe.wait_ge(tok_done, t - 3)
                for k in range(KT):
                    pe.wait_ge(w_lo_done, 8 + 4 * (p - 2) + (k // 2 if p < 4 else k // 4) + 1)
                    pe.matmul(mm[:, m % 4, 0:w], hT_hi[:, k, toks], w_hi[:, k, 0:w], start=(k == 0), stop=False)
                    pe.matmul(mm[:, m % 4, 0:w], hT_hi[:, k, toks], w_lo[:, k, 0:w], start=False, stop=False)
                    last = pe.matmul(mm[:, m % 4, 0:w], hT_lo[:, k, toks], w_hi[:, k, 0:w], start=False,
                                     stop=(k == KT - 1))
                    if k % 2 and k < KT - 1 and t % NT == NT - 1:
                        last.then_inc(panel_read, 1)
                last.then_inc(proj_done, 1)
                if t > NT:
                    turn_tok(t - 1)
            turn_tok(3 * NT - 1)


class Tiles:

    def __init__(self, near):
        self.near = near
        self.unit = 256 if near else 128
        self.portions = [(0, 1), (1, 3), (3, 5), (5, 8)] if near else [(0, 3), (3, 7), (7, 11), (11, 16)]

    def chunks(self, t):
        if self.near:
            return key_rows(t // 4)[1] // 4
        return 2 if t in (0, NT - 1) else 3

    def keys(self, ap, t):
        if self.near:
            (r0, rows), c0 = key_rows(t // 4), key_col(t % 4)
            return ap.rearrange("p (r c) -> p r c", c=GW)[:, r0:r0 + rows, c0:c0 + 32]
        k0 = max(t - 1, 0) * P
        return ap[:, k0:k0 + self.chunks(t) * P]

    def value_chunk(self, t, j):
        if self.near:
            return (key_rows(t // 4)[0] // 4 + j) * 4 + t % 4
        return max(t - 1, 0) + j

    def score_cols(self, t):
        n = self.chunks(t) * P
        if self.near:
            return 0, 0, n
        if t == 0:
            return 1 + P, 1 + P, 2 + 3 * P
        return (1, 0, 1 + n) if t == NT - 1 else (1, 1, 2 + n)


def attention_phase(nc, near, qk_dram, v_dram, rel_dram, mask_in, sink_in, ident_in, o_dram, mix_w=None):
    tiles = Tiles(near)
    name = "na" if near else "swa"
    ROUNDS, UNITS = 4, 2 * NT
    TURN_LAG, PV_LAG, NORM_LAG = 3, 5, 1
    OUT_LAG = PV_LAG + 1
    q0, k0 = (0, NAH) if near else (2 * NAH, 2 * NAH + SWH)
    W = 512 if near else 3 * P + 2
    with ExitStack() as ctx:
        def sb(n, shape, dt=F32):
            return ctx.enter_context(nc.sbuf_tensor(f"{name}_{n}", shape, dt))

        def sem(n):
            return nc.alloc_semaphore(f"{name}_{n}")

        q_st = sb("q_stack", [P, 2, S], F32R)
        k_hh = sb("k_hi_twice", [P, 2, S], F32R)
        k_ll = sb("k_lo_twice", [P, 2, S], F32R)
        v_sb = sb("values", [P, 32 if near else NT, P])
        ident = sb("ident", [P, P])
        sn = sb("neg_scores", [P, 4, W])
        pr = sb("probs", [P, 4, W])
        pt = sb("probs_turned", [P, 4, 4 * P])
        o_st = sb("o_stage", [P, 2, BANK])
        negmax = sb("negmax", [P, 4])
        total = sb("total", [P, 4])
        rtotal = sb("rtotal", [P, 4])
        if near:
            mask = sb("mask", [P, 3, 1280])
            rel = sb("rel", [P, 2, ROWS_REL * COLS_REL])
            bias = sb("bias", [P, 2, 3, 1280])
        else:
            mask = sb("mask", [P, 3 * P])
            sinks = sb("sinks", [P, SWH])
            w_raw = sb("w_out_raw", [P, 2, D])
            gcol = sb("g_out", [P, KT])
        sc = ctx.enter_context(nc.psum_tensor(f"{name}_scores", [P, 4, BANK], F32))
        tp = ctx.enter_context(nc.psum_tensor(f"{name}_turned", [P, 2, BANK], F32))
        op = ctx.enter_context(nc.psum_tensor(f"{name}_out", [P, 2, BANK], F32))

        qk_in = [sem(f"qk_in{b}") for b in range(4)]
        v_in = [sem(f"v_in{b}") for b in range(4)]
        const_in, rel_in, sinks_negated = sem("const_in"), sem("rel_in"), sem("sinks_negated")
        bias_made = sem("bias_made")
        w_in, gains_in = [sem(f"w_out_in{i}") for i in range(2)], sem("gains_in")
        w_scaled, w_hi_done, w_lo_done = sem("w_scaled"), sem("w_hi_done"), sem("w_lo_done")
        scored, shifted, exped = sem("scored"), sem("shifted"), sem("exped")
        sink_set, may_shift = sem("sink_set"), sem("may_shift")
        summed, probs_done = sem("summed"), sem("probs_done")
        p_turned, pt_copied = sem("p_turned"), sem("pt_copied")
        pv_done, o_copied = sem("pv_done"), sem("o_copied")
        o_stored = [sem(f"o_stored{i}") for i in range(2)]

        SC_BUFS, SN_BUFS, PT_BANKS, PT_BUFS, O_BANKS = 4, 4, 2, 4, 2

        def stream(eng, stages):
            deepest = max(lag for lag, _ in stages)

            def step(r, s, first, last):
                for lag, stage in stages:
                    u = s - lag
                    if (first and u < 0) or (last and u >= UNITS):
                        continue
                    stage(r + u // UNITS, u % UNITS)

            for s in range(deepest):
                step(0, s, True, False)
            with eng.Fori(0, ROUNDS - 1) as r:
                for s in range(deepest, UNITS + deepest):
                    step(r, s, False, False)
            for s in range(deepest, UNITS + deepest):
                step(ROUNDS - 1, s, False, True)

        block = ctx.enter_context(nc.Block())

        def f32(ap):
            return ap.bitcast(F32)

        @block.sync
        def _(sp):
            heads = qk_dram.rearrange("l (h d) s -> l d h s", d=HD)

            def load_qk(r, b):
                qs = slice(b * BANK, (b + 1) * BANK)
                lo, hi = tiles.portions[b]
                ks = slice(lo * tiles.unit, hi * tiles.unit)
                for e in range(2):
                    head = bass.ds(q0 + 2 * r + e if near else q0 + r + (SWH // SWKV) * e, 1)
                    sp.dma_start(f32(q_st[:, e, qs]), heads[:, :, head, qs]).then_inc(qk_in[b], 16)
                    if near or isinstance(r, int) and r == 0:
                        head = bass.ds(k0 + 2 * r + e, 1) if near else slice(k0 + e, k0 + e + 1)
                        for part, dst in enumerate((k_hh, k_ll)):
                            src = heads[part:part + 1, :, head, ks].broadcast_to([2, HD, 1, ks.stop - ks.start])
                            sp.dma_start(f32(dst[:, e, ks]), src).then_inc(qk_in[b], 16)

            def load_v(r, b):
                lo, hi = tiles.portions[b]
                if near:
                    for g in range(lo, hi):
                        for w in range(4):
                            src = v_dram.rearrange("(g r c) f -> g r c f", r=4, c=GW)[
                                g, :, key_col(w):key_col(w) + 32, bass.ds(r * P, P)]
                            sp.dma_start(v_sb[:, 4 * g + w, :], src).then_inc(v_in[b], 16)
                else:
                    sp.dma_start(v_sb[:, lo:hi, :],
                                 v_dram[lo * P:hi * P, AW:V_WIDTH].rearrange("(c p) f -> p c f", p=P)) \
                        .then_inc(v_in[b], 16)

            def load_rel(r):
                sp.dma_start(rel[:], rel_dram[bass.ds(2 * r, 2)].rearrange("h p f -> p h f")).then_inc(rel_in, 16)

            def store(r, b):
                sp.wait_ge(o_copied, O_BANKS + NT * r + 4 * (b + 1))
                dst = o_dram[bass.ds((r if near else r + 4) * P, P), b * BANK:(b + 1) * BANK]
                sp.dma_start(dst, o_st[:, b % 2, :]).then_inc(o_stored[b % 2], 16)

            if near:
                sp.dma_start(mask[:], mask_in).then_inc(const_in, 16)
                load_rel(0)
            else:
                sp.dma_start(mask[:], mask_in).then_inc(const_in, 16)
                sp.dma_start(sinks[:], sink_in.broadcast_to([P, SWH])).then_inc(const_in, 16)
            sp.dma_start(ident[:], ident_in).then_inc(const_in, 16)
            for b in range(4):
                load_qk(0, b)
                load_v(0, b)
            with sp.Fori(0, ROUNDS - 1) as r:
                if near:
                    sp.wait_ge(bias_made, 3 * r + 3)
                    load_rel(r + 1)
                for b in range(4):
                    sp.wait_ge(scored, UNITS * r + 8 * (b + 1))
                    load_qk(r + 1, b)
                    if near:
                        sp.wait_ge(pv_done, PT_BUFS // 2 + NT * r + 4 * (b + 1))
                        load_v(r + 1, b)
                    store(r, b)
            for b in range(4):
                store(ROUNDS - 1, b)
            for i in range(2):
                sp.wait_ge(o_stored[i], 16 * (2 * ROUNDS + 1))

        @block.gpsimd
        def _(pool):
            def prepare_mix_weights(pool):
                w_out, g_na, g_swa, w_hi, w_lo = mix_w

                def load(k):
                    if k < 4:
                        pool.dma_start(w_raw[:, k % 2, :], w_out[k * P:(k + 1) * P, :]).then_inc(w_in[k % 2], 32)
                        return
                    for e in range(2):
                        r0 = AW + (k - 4 + 4 * e) * HD
                        pool.dma_start(w_raw[e * HD:(e + 1) * HD, k % 2, :], w_out[r0:r0 + HD, :]) \
                            .then_inc(w_in[k % 2], 16)

                with nc.allow_non_contiguous_dma(reason="gains, one for each partition"):
                    pool.dma_start(gcol[:, 0:4], g_na.rearrange("a (k p) -> p (a k)", p=P)).then_inc(gains_in, 16)
                    for e in range(2):
                        pool.dma_start(gcol[e * HD:(e + 1) * HD, 4:8],
                                       g_swa[:, e * 4 * HD:(e + 1) * 4 * HD].rearrange("a (k p) -> p (a k)", p=HD)) \
                            .then_inc(gains_in, 16)
                load(0)
                load(1)
                pool.wait_ge(gains_in, 48)
                for k in range(KT):
                    raw = w_raw[:, k % 2, :]
                    pool.wait_ge(w_in[k % 2], 32 * (k // 2 + 1))
                    nc.gpsimd.tensor_scalar(raw, raw, gcol[:, k:k + 1], None, ALU.mult).then_inc(w_scaled, 1)
                    pool.wait_ge(w_scaled, k + 1)
                    nc.gpsimd.tensor_copy(w_hi[:, k, :], raw).then_inc(w_hi_done, 1)
                    pool.wait_ge(w_hi_done, k + 1)
                    nc.gpsimd.tensor_tensor(w_lo[:, k, :], raw, w_hi[:, k, :], ALU.subtract).then_inc(w_lo_done, 1)
                    if k + 2 < KT:
                        pool.wait_ge(w_lo_done, k + 1)
                        load(k + 2)

            def make_bias(r):
                pool.wait_ge(rel_in, 16 * r + 16)
                for kind, (at, rows, j0, freed) in enumerate(((0, 12, 4, 1), (384, 16, 0, 3), (896, 12, 0, 4))):
                    pool.wait_ge(shifted, UNITS * r + 8 * freed)
                    for e in range(2):
                        for ck, c0 in enumerate((16, 8, 0)):
                            out = bias[:, e, ck, at:at + rows * 32].rearrange("p (r c) -> p r c", c=32)
                            m = mask[:, ck, at:at + rows * 32].rearrange("p (r c) -> p r c", c=32)
                            b = rel[:, e, :].rearrange("p (j c) -> p j c", c=COLS_REL)[:, j0:j0 + rows, c0:c0 + 32]
                            last = nc.gpsimd.tensor_tensor(out, m, b, ALU.subtract)
                    last.then_inc(bias_made, 1)

            if near:
                pool.wait_ge(const_in, 32)
                with pool.Fori(0, ROUNDS) as r:
                    make_bias(r)
            else:
                prepare_mix_weights(pool)

        @block.scalar
        def _(act):
            def exp(r, u):
                i, t = u % 4, u // 2
                _, lo, hi = tiles.score_cols(t)
                act.wait_ge(shifted, UNITS * (r + 1) + u + 1)
                act.wait_ge(p_turned, UNITS * r + u + 1)
                nc.scalar.activation(pr[:, i, lo:hi], sn[:, i, lo:hi], ACT.Exp, bias=negmax[:, i:i + 1],
                                     scale=-1.0, accum_out=total[:, i:i + 1]).then_inc(exped, 1)

            def copy_turned(r, u):
                n = tiles.chunks(u // 2) * P
                act.wait_ge(p_turned, SN_BUFS + UNITS * r + u + 1)
                act.wait_ge(pv_done, PT_BUFS // 2 + NT * r + u // 2 - 1)
                nc.scalar.copy(pt[:, u % 4, 0:n], tp[:, u % 2, 0:n]).then_inc(pt_copied, 1)

            stream(act, [(TURN_LAG, copy_turned), (0, exp)])

        @block.vector
        def _(dve):
            def shift(r, u):
                e, i, t = u % 2, u % 4, u // 2
                n = tiles.chunks(t) * P
                c0, _, _ = tiles.score_cols(t)
                dve.wait_ge(exped, UNITS * r + u + 1)
                if near:
                    if u % 8 == 0 and t // 4 != 2:
                        dve.wait_ge(bias_made, 3 * r + {0: 1, 1: 2, 3: 3}[t // 4])
                    b, cb = t // 4, t % 4
                    at, ck = {0: 0, 1: 384, 2: 384, 3: 896}[b], {0: 0, 1: 1, 2: 1, 3: 2}[cb]
                    add, start = bias[:, e, ck, at:at + n], 3.0e38
                else:
                    if u < 4:
                        dve.sem_inc(may_shift, 1)
                        nc.vector.tensor_copy(sn[:, i, 0:W:W - 1],
                                              sinks[:, bass.ds(r + 4 * e, 1)].broadcast_to([P, 2])) \
                            .then_inc(sink_set, 1)
                        dve.wait_ge(sink_set, 4 * r + u + 1)
                    add, start = mask[:, c0 - 1:c0 - 1 + n], sn[:, i, 0:1]
                dve.wait_ge(scored, UNITS * r + u + 1)
                dve.sem_inc(may_shift, 1)
                nc.vector.tensor_tensor_reduce(sn[:, i, c0:c0 + n], sc[:, u % 4, 0:n], add, 1.0, start,
                                               ALU.add, ALU.min, negmax[:, i:i + 1]).then_inc(shifted, 1)

            def normalise(r, u):
                i, t = u % 4, u // 2
                n = tiles.chunks(t) * P
                c0, _, _ = tiles.score_cols(t)
                dve.wait_ge(exped, SN_BUFS + UNITS * r + u + 1)
                nc.vector.reciprocal(rtotal[:, i:i + 1], total[:, i:i + 1]).then_inc(summed, 1)
                dve.wait_ge(summed, UNITS * r + u + 1)
                nc.vector.tensor_scalar(pr[:, i, c0:c0 + n], pr[:, i, c0:c0 + n], rtotal[:, i:i + 1], None,
                                        ALU.mult).then_inc(probs_done, 1)

            def results(r, u):
                if u % 2 == 0:
                    return
                t = u // 2
                b = t // 4
                dve.wait_ge(pv_done, PT_BUFS // 2 + NT * r + t + 1)
                if t % 4 == 0:
                    dve.wait_ge(o_stored[b % 2], 16 * (2 * r + b // 2 + 1))
                if near:
                    dst = o_st[:, b % 2, :].rearrange("p (r c) -> p r c", c=GW)[:, :, 16 * (t % 4):16 * (t % 4) + 16]
                    src = op[:, t % 2, 0:P].rearrange("p (r c) -> p r c", c=16)
                else:
                    dst, src = o_st[:, b % 2, (t % 4) * P:(t % 4 + 1) * P], op[:, t % 2, 0:P]
                nc.vector.tensor_copy(dst, src).then_inc(o_copied, 1)

            dve.sem_inc(exped, SN_BUFS)
            dve.sem_inc(shifted, UNITS)
            dve.sem_inc(o_copied, O_BANKS)
            for i in range(2):
                dve.sem_inc(o_stored[i], 16)
            if not near:
                dve.wait_ge(const_in, 48)
                nc.vector.tensor_scalar(sinks[:], sinks[:], -1.0, None, ALU.mult).then_inc(sinks_negated, 1)
                dve.wait_ge(sinks_negated, 1)
            stream(dve, [(0, shift), (NORM_LAG, normalise), (OUT_LAG, results)])

        @block.tensor
        def _(pe):
            def score(r, u):
                e, t = u % 2, u // 2
                b, n = t // 4, tiles.chunks(t) * P
                if u % 8 == 0:
                    for i in (b, min(b + 1, 3)):
                        pe.wait_ge(qk_in[i], 96 * (r + 1) if near else 96 + 32 * r)
                pe.wait_ge(shifted, UNITS * (r + 1) - SC_BUFS + u + 1)
                q, out = q_st[:, e, t * P:(t + 1) * P], sc[:, u % 4, 0:n]
                pe.matmul(out, q, tiles.keys(k_hh[:, e, :], t), start=True, stop=False)
                pe.matmul(out, q, tiles.keys(k_ll[:, e, :], t), start=False, stop=True).then_inc(scored, 1)

            def turn(r, u):
                i, t = u % 4, u // 2
                c0, _, _ = tiles.score_cols(t)
                pe.wait_ge(probs_done, UNITS * r + u + 1)
                pe.wait_ge(pt_copied, UNITS * r + u + 1)
                for j in range(tiles.chunks(t)):
                    last = pe.transpose(tp[:, u % 2, j * P:(j + 1) * P], pr[:, i, c0 + j * P:c0 + (j + 1) * P],
                                        ident[:])
                last.then_inc(p_turned, 1)

            def values(r, u):
                if u % 2 == 0:
                    return
                t = u // 2
                b, n = t // 4, tiles.chunks(t)
                if t % 4 == 0:
                    for i in (b, min(b + 1, 3)):
                        lo, hi = tiles.portions[i]
                        pe.wait_ge(v_in[i], 64 * (hi - lo) * (r + 1) if near else 16)
                pe.wait_ge(pt_copied, PT_BANKS + UNITS * r + u + 1)
                pe.wait_ge(o_copied, NT * r + t + 1)
                for j in range(n):
                    v = v_sb[:, tiles.value_chunk(t, j), :]
                    for e in range(2):
                        h = slice(e * HD, (e + 1) * HD)
                        last = pe.matmul(op[h, t % 2, 0:P], v[:, h], pt[:, (u - 1 + e) % 4, j * P:(j + 1) * P],
                                         start=(j == 0), stop=(j == n - 1))
                last.then_inc(pv_done, 1)

            pe.sem_inc(p_turned, SN_BUFS)
            pe.sem_inc(pt_copied, PT_BANKS)
            pe.sem_inc(pv_done, PT_BUFS // 2)
            pe.wait_ge(const_in, 32 if near else 48)
            stream(pe, [(0, score), (TURN_LAG, turn), (PV_LAG, values)])


def mix_phase(nc, x, w_pool, g_ffn, ident_in, ones_in, o_dram, x1, hT_hi, hT_lo, x1_dram, h_dram):
    with ExitStack() as ctx:
        def sb(name, shape, dt=F32):
            return ctx.enter_context(nc.sbuf_tensor(f"mix_{name}", shape, dt))

        def sem(name):
            return nc.alloc_semaphore(f"mix_{name}")

        w_hi, w_lo = w_pool[:, 0:KT], w_pool[:, KT:2 * KT]
        ot = sb("o", [P, 2, KT, P])
        o_hi = sb("o_hi", [P, 2, KT, P], F32R)
        o_lo = sb("o_lo", [P, 2, KT, P], F32R)
        sq = sb("squares", [P, KT, P])
        sqs = sb("squares_summed", [P, 2, P])
        xn = sb("x_normed", [P, D])
        x_stage = sb("x_stage", [P, 2, D])
        gffn = sb("g_ffn", [P, D])
        ident = sb("ident", [P, P])
        ones = sb("ones", [P, 2])
        oms, oinv, orms = (sb(n, [P, NT, 2]) for n in ("o_mean", "o_inv", "o_rms"))
        ssq, msq, inv, rstd = (sb(n, [P, NT]) for n in ("ssq", "mean", "inv", "rstd"))
        mm = ctx.enter_context(nc.psum_tensor("mix_mm", [P, 4, BANK], F32))
        tp = ctx.enter_context(nc.psum_tensor("mix_turn", [P, 2 * BANK], F32))
        st = ctx.enter_context(nc.psum_tensor("mix_stat", [P, BANK], F32))

        o_in = [sem(f"o_in{i}") for i in range(2)]
        x_in = [sem(f"x_in{i}") for i in range(2)]
        const_in = sem("const_in")
        o_squared, o_split_hi, o_split_lo = sem("o_squared"), sem("o_split_hi"), sem("o_split_lo")
        sq_summed, o_stat, o_mean, o_inv, o_rms = (sem(n) for n in ("sq_summed", "o_stat", "o_mean", "o_inv", "o_rms"))
        mm_done, added = sem("mm_done"), sem("added")
        squared, mean_done, inv_done, rstd_done = (sem(n) for n in ("squared", "mean_done", "inv_done", "rstd_done"))
        normed, turned, h_hi_done, h_lo_done = (sem(n) for n in ("normed", "turned", "h_hi_done", "h_lo_done"))
        x1_stored = [sem(f"x1_stored{i}") for i in range(2)]
        h_stored = sem("h_stored")

        def x_of(t):
            return x1[:, t, :] if t < HT else x_stage[:, t % 2, :]

        turned_view = tp[:].rearrange("p (k s) -> p k s", k=KT)
        xn_turned = xn[:].rearrange("p (k s) -> p k s", k=KT)
        block = ctx.enter_context(nc.Block())

        @block.sync
        def _(sp):
            def load_o(t):
                if t >= 2:
                    sp.wait_ge(o_split_lo, t - 1)
                    sp.wait_ge(o_squared, t - 1)
                sp.dma_start(ot[:, t % 2], o_dram[:, t * P:(t + 1) * P].rearrange("(k p) s -> p k s", p=P)) \
                    .then_inc(o_in[t % 2], 16)

            def load_x(t):
                if t >= 2:
                    sp.wait_ge(added, 4 * (t - 1))
                if t >= HT + 2:
                    sp.wait_ge(x1_stored[t % 2], 16 * ((t - HT) // 2))
                    sp.wait_ge(normed, t - 1)
                sp.dma_start(x_of(t), x[t * P:(t + 1) * P, :]).then_inc(x_in[t % 2], 16)

            def store_x1(t):
                sp.wait_ge(added, 4 * (t + 1))
                sp.dma_start(x1_dram[(t - HT) * P:(t - HT + 1) * P, :], x_of(t)).then_inc(x1_stored[t % 2], 16)

            def store_h(t):
                sp.wait_ge(h_hi_done, t + 1)
                sp.dma_start(h_dram[:, :, (t - HT) * P:(t - HT + 1) * P], xn_turned).then_inc(h_stored, 16)

            load_o(0)
            sp.dma_start(ones[:], ones_in).then_inc(const_in, 16)
            load_o(1)
            load_x(0)
            load_x(1)
            sp.dma_start(gffn[:], g_ffn.broadcast_to([P, D])).then_inc(const_in, 16)
            sp.dma_start(ident[:], ident_in).then_inc(const_in, 16)
            for t in range(NT):
                if t + 2 < NT:
                    load_o(t + 2)
                if t > HT:
                    store_h(t - 1)
                if t >= HT:
                    store_x1(t)
                if t + 2 < NT:
                    load_x(t + 2)
            store_h(NT - 1)
            sp.wait_ge(h_stored, 16 * HT)
            for i in range(2):
                sp.wait_ge(x1_stored[i], 16 * HT // 2)

        @block.scalar
        def _(act):
            def take_tile(t):
                act.wait_ge(o_in[t % 2], 16 * (t // 2 + 1))
                if t >= 1:
                    act.wait_ge(sq_summed, t)
                nc.scalar.activation(sq[:], ot[:, t % 2], ACT.Square).then_inc(o_squared, 1)
                if t >= 2:
                    act.wait_ge(mm_done, 4 * (t - 1))
                nc.scalar.copy(o_hi[:, t % 2], ot[:, t % 2]).then_inc(o_split_hi, 1)

            def o_root(t):
                act.wait_ge(o_inv, t + 1)
                nc.scalar.activation(orms[:, t, :], oinv[:, t, :], ACT.Sqrt).then_inc(o_rms, 1)

            def norm(t):
                act.wait_ge(added, 4 * (t + 1))
                if t >= 1:
                    act.wait_ge(turned, t)
                if t > HT:
                    act.wait_ge(h_stored, 16 * (t - HT))
                nc.scalar.activation(xn[:], x_of(t), ACT.Square, accum_out=ssq[:, t:t + 1]).then_inc(squared, 1)
                act.wait_ge(inv_done, t + 1)
                nc.scalar.activation(rstd[:, t:t + 1], inv[:, t:t + 1], ACT.Sqrt).then_inc(rstd_done, 1)

            def turn_hi(t):
                act.wait_ge(turned, t + 1)
                dst = hT_hi[:, :, t * P:(t + 1) * P] if t < HT else xn_turned
                nc.scalar.copy(dst, turned_view).then_inc(h_hi_done, 1)

            take_tile(0)
            o_root(0)
            for t in range(NT):
                if t >= 1:
                    norm(t - 1)
                if t + 1 < NT:
                    take_tile(t + 1)
                    o_root(t + 1)
                if t >= 1:
                    turn_hi(t - 1)
            norm(NT - 1)
            turn_hi(NT - 1)

        @block.vector
        def _(dve):
            def take_tile(t):
                dve.wait_ge(o_squared, t + 1)
                if t >= 1:
                    dve.wait_ge(o_stat, t)
                nc.vector.tensor_reduce(sqs[:], sq[:].rearrange("p (g k) s -> p g s k", g=2),
                                        mybir.AxisListType.X, ALU.add).then_inc(sq_summed, 1)
                dve.wait_ge(o_split_hi, t + 1)
                nc.vector.tensor_tensor(o_lo[:, t % 2], ot[:, t % 2], o_hi[:, t % 2], ALU.subtract) \
                    .then_inc(o_split_lo, 1)

            def o_means(t):
                dve.wait_ge(o_stat, t + 1)
                nc.vector.tensor_scalar(oms[:, t, :], st[:, 0:4:2], 1.0 / AW, EPS, ALU.mult, ALU.add) \
                    .then_inc(o_mean, 1)
                dve.wait_ge(o_mean, t + 1)
                nc.vector.reciprocal(oinv[:, t, :], oms[:, t, :]).then_inc(o_inv, 1)

            def add(t, i):
                n, g = i // 2, i % 2
                dst = x_of(t)[:, n * BANK:(n + 1) * BANK]
                if i == 0:
                    dve.wait_ge(o_rms, t + 1)
                    dve.wait_ge(x_in[t % 2], 16 * (t // 2 + 1))
                dve.wait_ge(mm_done, 4 * t + i + 1)
                if g:
                    dve.wait_ge(added, 4 * t + i)
                nc.vector.scalar_tensor_tensor(out=dst, in0=mm[:, i, :], scalar=orms[:, t, g:g + 1], in1=dst,
                                               op0=ALU.mult, op1=ALU.add).then_inc(added, 1)

            def norm(t):
                dve.wait_ge(squared, t + 1)
                nc.vector.tensor_scalar(msq[:, t:t + 1], ssq[:, t:t + 1], 1.0 / D, EPS, ALU.mult, ALU.add) \
                    .then_inc(mean_done, 1)
                dve.wait_ge(mean_done, t + 1)
                nc.vector.reciprocal(inv[:, t:t + 1], msq[:, t:t + 1]).then_inc(inv_done, 1)
                dve.wait_ge(rstd_done, t + 1)
                nc.vector.scalar_tensor_tensor(out=xn[:], in0=x_of(t), scalar=rstd[:, t:t + 1], in1=gffn[:],
                                               op0=ALU.mult, op1=ALU.mult).then_inc(normed, 1)

            def turn_lo(t):
                toks = slice(t * P, (t + 1) * P)
                dve.wait_ge(h_hi_done, t + 1)
                nc.vector.tensor_tensor(hT_lo[:, :, toks], turned_view, hT_hi[:, :, toks], ALU.subtract) \
                    .then_inc(h_lo_done, 1)

            take_tile(0)
            o_means(0)
            dve.wait_ge(const_in, 48)
            for t in range(NT):
                if t >= 1:
                    norm(t - 1)
                if t + 1 < NT:
                    take_tile(t + 1)
                add(t, 0)
                add(t, 1)
                if t + 1 < NT:
                    o_means(t + 1)
                add(t, 2)
                if 1 <= t <= HT:
                    turn_lo(t - 1)
                add(t, 3)
            norm(NT - 1)

        @block.tensor
        def _(pe):
            def stats(t):
                pe.wait_ge(sq_summed, t + 1)
                if t >= 1:
                    pe.wait_ge(o_mean, t)
                for g in range(2):
                    last = pe.matmul(st[:, 2 * g:2 * g + 2], sqs[:, g, :], ones[:], start=True, stop=True)
                last.then_inc(o_stat, 1)

            def turn(t):
                pe.wait_ge(normed, t + 1)
                if 1 <= t <= HT:
                    pe.wait_ge(h_lo_done, t)
                elif t > HT:
                    pe.wait_ge(h_hi_done, t)
                for k in range(KT):
                    last = pe.transpose(tp[:, k * P:(k + 1) * P], xn[:, k * P:(k + 1) * P], ident[:])
                last.then_inc(turned, 1)

            def product(t, i):
                n, g = i // 2, i % 2
                cols = slice(n * BANK, (n + 1) * BANK)
                if i == 0:
                    pe.wait_ge(o_split_lo, t + 1)
                if t >= 1:
                    pe.wait_ge(added, 4 * (t - 1) + i + 1)
                for k in range(4 * g, 4 * g + 4):
                    pe.matmul(mm[:, i, :], o_hi[:, t % 2, k, :], w_hi[:, k, cols], start=(k % 4 == 0), stop=False)
                    pe.matmul(mm[:, i, :], o_hi[:, t % 2, k, :], w_lo[:, k, cols], start=False, stop=False)
                    last = pe.matmul(mm[:, i, :], o_lo[:, t % 2, k, :], w_hi[:, k, cols], start=False,
                                     stop=(k % 4 == 3))
                last.then_inc(mm_done, 1)

            pe.wait_ge(const_in, 48)
            stats(0)
            for t in range(NT):
                product(t, 0)
                product(t, 1)
                if t + 1 < NT:
                    stats(t + 1)
                product(t, 2)
                if t >= 1:
                    turn(t - 1)
                product(t, 3)
            turn(NT - 1)


def feed_phase(nc, w_gate, w_up, w_down, g_final, w_pool, x1, hT_hi, hT_lo, x1_dram, h_dram, out):
    STEPS = FF // P // 2
    TBS = HS // BANK
    DOWNS = HT * 2
    with ExitStack() as ctx:
        def sb(n, shape, dt=F32):
            return ctx.enter_context(nc.sbuf_tensor(f"ff_{n}", shape, dt))

        def sem(n):
            return nc.alloc_semaphore(f"ff_{n}")

        gu_hi, gu_lo = (w_pool[:, n:n + 4].rearrange("p (f w) (k c) -> p f w k c", f=2, k=KT)
                        for n in (0, 4))
        gu_raw = sb("gu_raw", [P, 2, KT, P])
        d_hi = sb("down_hi", [P, 2, D], F32R)
        d_lo = sb("down_lo", [P, 2, D], F32R)
        d_raw = sb("down_raw", [P, 2, D])
        a_hi, a_lo = (w_pool[:, n:n + 4].rearrange("p (q f) s -> p q f s", f=2)
                      for n in (8, 12))
        silu = sb("silu", [P, 2, BANK])
        prod = sb("prod", [P, 2, BANK])
        gfin = sb("g_final", [P, D])
        ssq, msq, inv, rstd = (sb(n, [P, HT]) for n in ("ssq", "mean", "inv", "rstd"))
        gu = ctx.enter_context(nc.psum_tensor("ff_gu", [P, 4, BANK], F32))
        dn = ctx.enter_context(nc.psum_tensor("ff_down", [P, 4, BANK], F32))

        gu_in = [sem(f"gu_in{i}") for i in range(2)]
        d_in, const_in = sem("down_in"), sem("const_in")
        gu_hi_done, gu_lo_done = sem("gu_hi_done"), sem("gu_lo_done")
        d_hi_done, d_lo_done = sem("d_hi_done"), sem("d_lo_done")
        gu_done, silu_done, prod_done = sem("gu_done"), sem("silu_done"), sem("prod_done")
        a_hi_done, a_lo_done = sem("a_hi_done"), sem("a_lo_done")
        down_done, added = sem("down_done"), sem("added")
        squared, mean_done, inv_done, rstd_done, normed = (
            sem(n) for n in ("squared", "mean_done", "inv_done", "rstd_done", "normed"))
        out_stored, x1_in = [sem(f"out_stored{i}") for i in range(2)], sem("x1_in")
        h_in = [sem(f"h_in{i}") for i in range(KT)]
        h_hi_done, h_lo_done = sem("h_hi_done"), sem("h_lo_done")

        block = ctx.enter_context(nc.Block())
        gate_v = w_gate.rearrange("(k p) n -> p k n", p=P)
        up_v = w_up.rearrange("(k p) n -> p k n", p=P)

        def h_part(ap, n):
            return ap[:, 2 * (n % 4):2 * (n % 4) + 2, n // 4 * BANK:(n // 4 + 1) * BANK]

        RAW = 2

        @block.sync
        def _(sp):
            def load(i, base):
                for f in range(2):
                    for w, view in enumerate((gate_v, up_v)):
                        sp.wait_ge(gu_lo_done, 4 * (base + i) + 2 * f + w + 1)
                        sp.dma_start(gu_raw[:, w], view[:, :, bass.ds((2 * i + f) * P, P)]).then_inc(gu_in[w], 16)
                sp.wait_ge(d_lo_done, base + i + 1)
                sp.dma_start(d_raw[:], w_down[bass.ds(2 * i * P, 2 * P), :].rearrange("(f p) n -> p f n", p=P)) \
                    .then_inc(d_in, 16)

            load(0, 0)
            sp.dma_start(gfin[:], g_final.broadcast_to([P, D])).then_inc(const_in, 16)
            with sp.Fori(1, STEPS) as i:
                load(i, 0)
            with sp.Fori(0, STEPS) as i:
                load(i, STEPS)
            for t in range(HT, NT):
                sp.wait_ge(normed, t + 1)
                sp.dma_start(out[t * P:(t + 1) * P, :], x1[:, t - HT, :]).then_inc(out_stored[1], 16)
            sp.wait_ge(out_stored[1], 16 * HT)

        @block.gpsimd
        def _(pool):
            for tb in range(TBS):
                pool.wait_ge(gu_done, 4 * (STEPS - 1) + 2 + tb + 1)
                for kp in range(KT // 2):
                    ks, toks = slice(2 * kp, 2 * kp + 2), slice(tb * BANK, (tb + 1) * BANK)
                    pool.dma_start(hT_lo[:, ks, toks].bitcast(F32), h_dram[:, ks, toks]) \
                        .then_inc(h_in[4 * tb + kp], 16)
            for t in range(HT):
                pool.wait_ge(normed, t + 1)
                pool.dma_start(out[t * P:(t + 1) * P, :], x1[:, t, :]).then_inc(out_stored[0], 16)
            pool.wait_ge(out_stored[0], 16 * HT)
            pool.dma_start(x1[:], x1_dram.rearrange("(t p) d -> p t d", p=P)).then_inc(x1_in, 16)

        def steps(eng, tile, down, split_gu, split_d, meet, second_half=lambda: None):
            def body(i, par, last=False):
                tile(i, 0, par)
                if not last:
                    split_gu(i + 1, 0)
                down(i - 1, 1 - par)
                split_d(i)
                tile(i, 1, par)
                if not last:
                    split_gu(i + 1, 1)

            for base in (0, STEPS):
                par = base % 2
                if base == 0:
                    split_gu(0, 0)
                    split_gu(0, 1)
                else:
                    meet()
                split_d(base)
                tile(base, 0, par)
                split_gu(base + 1, 0)
                tile(base, 1, par)
                split_gu(base + 1, 1)
                if base:
                    second_half()
                with eng.Fori(0, (STEPS - 3) // 2) as j:
                    body(2 * j + base + 1, 1 - par)
                    body(2 * j + base + 2, par)
                body(base + STEPS - 2, 1 - par)
                body(base + STEPS - 1, par, last=base > 0)

        @block.scalar
        def _(act):
            def split_gu(i, f):
                for w in range(2):
                    if not (isinstance(i, int) and i == 0):
                        act.wait_ge(gu_done, 4 * (i - 1) + 2 * f + 2)
                    act.wait_ge(gu_in[w], 16 * (2 * i + f + 1))
                    nc.scalar.copy(gu_hi[:, f, w], gu_raw[:, w]).then_inc(gu_hi_done, 1)

            def split_d(i):
                if not (isinstance(i, int) and i == 0):
                    act.wait_ge(down_done, DOWNS * i)
                act.wait_ge(d_in, 16 * (i + 1))
                nc.scalar.copy(d_hi[:], d_raw[:]).then_inc(d_hi_done, 1)

            def tile(i, f, par):
                for tb in range(TBS):
                    n = 4 * i + 2 * f + tb
                    act.wait_ge(gu_done, n + 1)
                    act.wait_ge(prod_done, n + 1)
                    nc.scalar.activation(silu[:, tb], gu[:, 2 * tb], ACT.Silu).then_inc(silu_done, 1)
                    act.wait_ge(prod_done, n + 3)
                    nc.scalar.copy(a_hi[:, par, f, tb * BANK:(tb + 1) * BANK], prod[:, tb]).then_inc(a_hi_done, 1)

            def down(i, par):
                pass

            spare = silu[:].rearrange("p a b -> p (a b)")

            def square(t, steps_done):
                act.wait_ge(added, 4 + DOWNS * (steps_done - 1) + 2 * (t + 1))
                nc.scalar.activation(spare, x1[:, t, :], ACT.Square, accum_out=ssq[:, t:t + 1]) \
                    .then_inc(squared, 1)

            def meet():
                for n in range(KT):
                    act.wait_ge(h_in[n], 16)
                    nc.scalar.copy(h_part(hT_hi, n), h_part(hT_lo, n).bitcast(F32)).then_inc(h_hi_done, 1)
                for t in range(HT):
                    if t >= 1:
                        act.wait_ge(squared, t)
                    square(t, STEPS)
                act.wait_ge(inv_done, 1)
                nc.scalar.activation(rstd[:], inv[:], ACT.Sqrt).then_inc(rstd_done, 1)

            steps(act, tile, down, split_gu, split_d, meet)
            for t in range(HT):
                square(t, 2 * STEPS)
                act.wait_ge(inv_done, t + 2)
                nc.scalar.activation(rstd[:, t:t + 1], inv[:, t:t + 1], ACT.Sqrt).then_inc(rstd_done, 1)

        @block.vector
        def _(dve):
            def split_gu(i, f):
                for w in range(2):
                    dve.wait_ge(gu_hi_done, 4 * i + 2 * f + w + 1)
                    nc.vector.tensor_tensor(gu_lo[:, f, w], gu_raw[:, w], gu_hi[:, f, w], ALU.subtract) \
                        .then_inc(gu_lo_done, 1)

            def split_d(i):
                dve.wait_ge(d_hi_done, i + 1)
                nc.vector.tensor_tensor(d_lo[:], d_raw[:], d_hi[:], ALU.subtract).then_inc(d_lo_done, 1)

            def tile(i, f, par):
                for tb in range(TBS):
                    n = 4 * i + 2 * f + tb
                    dve.wait_ge(silu_done, n + 1)
                    nc.vector.tensor_tensor(prod[:, tb], gu[:, 2 * tb + 1], silu[:, tb], ALU.mult).then_inc(prod_done, 1)
                    dve.wait_ge(a_hi_done, n + 1)
                    nc.vector.tensor_tensor(a_lo[:, par, f, tb * BANK:(tb + 1) * BANK], prod[:, tb],
                                            a_hi[:, par, f, tb * BANK:(tb + 1) * BANK], ALU.subtract) \
                        .then_inc(a_lo_done, 1)

            def add(i, m):
                t, n = m // 2, m % 2
                dst = x1[:, t, n * BANK:(n + 1) * BANK]
                dve.wait_ge(down_done, DOWNS * i + m + 1)
                nc.vector.tensor_tensor(dst, dn[:, m % 4], dst, ALU.add).then_inc(added, 1)

            def down(i, par):
                for m in range(DOWNS):
                    add(i, m)

            def inverse(ts, n):
                nc.vector.tensor_scalar(msq[:, ts], ssq[:, ts], 1.0 / D, EPS, ALU.mult, ALU.add).then_inc(mean_done, 1)
                dve.wait_ge(mean_done, n)
                nc.vector.reciprocal(inv[:, ts], msq[:, ts]).then_inc(inv_done, 1)

            def scale(t):
                nc.vector.scalar_tensor_tensor(out=x1[:, t, :], in0=x1[:, t, :], scalar=rstd[:, t:t + 1], in1=gfin[:],
                                               op0=ALU.mult, op1=ALU.mult).then_inc(normed, 1)

            def meet():
                for m in range(DOWNS):
                    add(STEPS - 1, m)
                    if m % 2:
                        n = m // 2
                        dve.wait_ge(h_hi_done, n + 1)
                        nc.vector.tensor_tensor(h_part(hT_lo, n), h_part(hT_lo, n).bitcast(F32), h_part(hT_hi, n),
                                                ALU.subtract).then_inc(h_lo_done, 1)
                dve.wait_ge(squared, HT)
                inverse(slice(0, HT), 1)
                dve.wait_ge(const_in, 16)
                dve.wait_ge(rstd_done, 1)
                for t in range(HT):
                    scale(t)

            def final(t):
                dve.wait_ge(squared, HT + t + 1)
                inverse(slice(t, t + 1), t + 2)
                dve.wait_ge(rstd_done, t + 2)
                scale(t)

            dve.sem_inc(gu_lo_done, RAW)
            dve.sem_inc(d_lo_done, 1)
            dve.sem_inc(prod_done, 2)
            dve.sem_inc(added, 4)
            steps(dve, tile, down, split_gu, split_d, meet,
                  second_half=lambda: dve.wait_ge(x1_in, 16))
            for m in range(DOWNS):
                add(2 * STEPS - 1, m)
                if m % 2 and m >= 3:
                    final(m // 2 - 1)
            final(HT - 1)

        @block.tensor
        def _(pe):
            def split_gu(i, f):
                pass

            def split_d(i):
                pass

            def tile(i, f, par):
                for tb in range(TBS):
                    toks = slice(tb * BANK, (tb + 1) * BANK)
                    pe.wait_ge(prod_done, 4 * i + 2 * f + tb + 1)
                    if isinstance(i, int) and i == STEPS and f == 0:
                        pe.wait_ge(h_lo_done, 4 * (tb + 1))
                    for w in range(2):
                        bank = gu[:, 2 * tb + w]
                        pe.wait_ge(gu_lo_done, RAW + 4 * i + 2 * f + w + 1)
                        for k in range(KT):
                            hi, lo = gu_hi[:, f, w, k, :], gu_lo[:, f, w, k, :]
                            pe.matmul(bank, hi, hT_hi[:, k, toks], start=(k == 0), stop=False)
                            pe.matmul(bank, hi, hT_lo[:, k, toks], start=False, stop=False)
                            last = pe.matmul(bank, lo, hT_hi[:, k, toks], start=False, stop=(k == KT - 1))
                    last.then_inc(gu_done, 1)

            def down(i, par):
                pe.wait_ge(d_lo_done, i + 2)
                pe.wait_ge(a_lo_done, 4 * (i + 1))
                for m in range(DOWNS):
                    t, n = m // 2, m % 2
                    toks, cols = slice(t * P, (t + 1) * P), slice(n * BANK, (n + 1) * BANK)
                    pe.wait_ge(added, DOWNS * i + m + 1)
                    for f in range(2):
                        hi, lo = a_hi[:, par, f, toks], a_lo[:, par, f, toks]
                        pe.matmul(dn[:, m % 4], hi, d_hi[:, f, cols], start=(f == 0), stop=False)
                        pe.matmul(dn[:, m % 4], hi, d_lo[:, f, cols], start=False, stop=False)
                        last = pe.matmul(dn[:, m % 4], lo, d_hi[:, f, cols], start=False, stop=(f == 1))
                    last.then_inc(down_done, 1)

            def meet():
                down(STEPS - 1, 0)

            steps(pe, tile, down, split_gu, split_d, meet)
            down(2 * STEPS - 1, 1)


def rope_tables():
    freq = np.float32(500000.0) ** (-np.arange(0, ROPE, 2, dtype=np.float32) / np.float32(ROPE))
    angle = np.arange(S, dtype=np.float32)[:, None] * freq[None, :]
    cos, sin = np.cos(angle), np.sin(angle)
    return np.concatenate([cos, cos], 1), np.concatenate([-sin, sin], 1)


def neighbour_masks():
    out = np.zeros((P, 3, 1280), np.float32)
    for ck, cb in enumerate((0, 1, 3)):
        at = 0
        for band in (0, 1, 3):
            row0, rows = key_rows(band)
            qr, qc = np.arange(P) // 16 + 8 * band, np.arange(P) % 16 + 16 * cb
            kr, kc = row0 + np.arange(rows), key_col(cb) + np.arange(32)
            r0, c0 = np.clip(qr - 4, 0, S // GW - 8), np.clip(qc - 8, 0, GW - 16)
            rok = (kr >= r0[:, None]) & (kr < r0[:, None] + 8)
            cok = (kc >= c0[:, None]) & (kc < c0[:, None] + 16)
            ok = rok[:, :, None] & cok[:, None, :]
            out[:, ck, at:at + rows * 32] = np.where(ok, 0.0, MASKED).reshape(P, -1)
            at += rows * 32
    return out


def key_rows(band):
    return (0, 12) if band == 0 else (8 * band - 4, 16 if band < 3 else 12)


def key_col(cb):
    return min(max(16 * cb - 8, 0), GW - 32)


def window_mask():
    q, k = np.arange(P)[:, None], np.arange(3 * P)[None, :] - P
    return np.where(np.abs(q - k) <= 128, 0.0, MASKED).astype(np.float32)


def kernel(x, g_norm_mix, w_in, na_rpb, swa_sink, g_out_na, g_out_swa, w_out, g_norm_ffn, w_gate,
           w_up, w_down, g_final):
    import concourse.bacc as _bacc
    from concourse.bass_utils import run_bass_kernel_spmd as _run

    nc = _bacc.Bacc("TRN2", target_bir_lowering=False, num_devices=1)
    cos2, sin2 = rope_tables()
    given = {
        "x": np.asarray(x).reshape(S, D), "g_mix": np.asarray(g_norm_mix), "w_in": np.asarray(w_in)[0],
        "rpb": np.asarray(na_rpb)[0], "sink": np.asarray(swa_sink), "g_na": np.asarray(g_out_na),
        "g_swa": np.asarray(g_out_swa), "w_out": np.asarray(w_out)[0], "g_ffn": np.asarray(g_norm_ffn),
        "w_gate": np.asarray(w_gate)[0], "w_up": np.asarray(w_up)[0], "w_down": np.asarray(w_down)[0],
        "g_final": np.asarray(g_final).reshape(1, D),
        "cos2": cos2, "sin2": sin2, "ident": np.eye(P, dtype=np.float32),
        "na_mask": neighbour_masks(), "swa_mask": window_mask(),
        "zeros": np.zeros(NAH * PAD_R * PAD_C, np.float32), "ones": np.ones((P, 2), np.float32),
    }
    given = {k: np.ascontiguousarray(v) for k, v in given.items()}
    aps = {k: nc.dram_tensor(f"in_{k}", v.shape, F32, kind="ExternalInput").ap() for k, v in given.items()}
    out = nc.dram_tensor("out_0", (S, D), F32, kind="ExternalOutput").ap()
    program(nc, aps, out)
    r = _run(nc, [{f"in_{k}": v for k, v in given.items()}], core_ids=[0])
    return r.results[0]["out_0"].reshape(1, S, D)


def program(nc, a, out, phases=4):
    qk_dram = nc.dram_tensor("qk_scratch", (2, HEADS * HD, S), F32).ap()
    v_dram = nc.dram_tensor("v_scratch", (S, V_WIDTH), F32).ap()
    pad_dram = nc.dram_tensor("pad_scratch", (NAH, PAD_R, PAD_C), F32).ap()
    rel_dram = nc.dram_tensor("rel_scratch", (NAH, P, ROWS_REL * COLS_REL), F32).ap()
    o_dram = nc.dram_tensor("o_scratch", (D, S), F32).ap()
    x1_dram = nc.dram_tensor("x1_scratch", (HS, D), F32).ap()
    h_dram = nc.dram_tensor("ffn_in_scratch", (P, KT, HS), F32).ap()
    pools = ExitStack()
    with nc.cleanup_on_exit():
        project_phase(nc, a["x"], a["g_mix"], a["w_in"], a["rpb"], a["cos2"], a["sin2"], a["ident"],
                      a["zeros"], qk_dram, v_dram, pad_dram, rel_dram)
        attention_phase(nc, True, qk_dram, v_dram, rel_dram, a["na_mask"], a["sink"], a["ident"], o_dram)
    nc.all_engine_barrier()
    w_pool = pools.enter_context(nc.sbuf_tensor("w_pool", [P, 2 * KT, D], F32R))
    with nc.cleanup_on_exit():
        attention_phase(nc, False, qk_dram, v_dram, rel_dram, a["swa_mask"], a["sink"], a["ident"], o_dram,
                        (a["w_out"], a["g_na"], a["g_swa"], w_pool[:, 0:KT], w_pool[:, KT:2 * KT]))
    nc.all_engine_barrier()
    if phases == 3:
        return
    x1 = pools.enter_context(nc.sbuf_tensor("x1", [P, HT, D], F32))
    hT_hi = pools.enter_context(nc.sbuf_tensor("ffn_in_hi", [P, KT, HS], F32R))
    hT_lo = pools.enter_context(nc.sbuf_tensor("ffn_in_lo", [P, KT, HS], F32R))
    mix_phase(nc, a["x"], w_pool, a["g_ffn"], a["ident"], a["ones"], o_dram, x1, hT_hi, hT_lo, x1_dram, h_dram)
    feed_phase(nc, a["w_gate"], a["w_up"], a["w_down"], a["g_final"], w_pool, x1, hT_hi, hT_lo, x1_dram, h_dram,
               out)
    pools.close()
```

```python
from contextlib import ExitStack

import numpy as np
import concourse.bass as bass
from concourse import mybir

ALU = mybir.AluOpType
ACT = mybir.ActivationFunctionType
F32 = mybir.dt.float32
F32R = mybir.dt.float32r

P = 128
BANK = 512
D = 1024
S = 2048
HD = 64
GW = 64
NAH, SWH, SWKV = 8, 8, 2
AW = NAH * HD
KT = D // P
NT = S // P
HS = S // 2
HT = NT // 2
FF = 2816
EPS = 1e-6
SCALE = HD ** -0.5
HEADS = 2 * NAH + SWH + SWKV
ROPE = HD // 4
HALF = ROPE // 2
MASKED = 1e30
ROWS_REL, COLS_REL = 16, 48
BIAS_COLS = 1280
PAD_R, PAD_C = 23, 63


def project_phase(nc, x, g_mix, w_in, rpb, cos2, sin2, ident_in, zeros_in, qk_dram,
                  v_near_dram, v_win_dram, pad_dram, rel_dram, near_mask_in, near_pool):
    with ExitStack() as ctx:
        def sb(name, shape, dt=F32):
            return ctx.enter_context(nc.sbuf_tensor(name, shape, dt))

        def sem(name):
            return nc.alloc_semaphore(name)

        XS, RAW = 3, 4
        xn = sb("x_normed", [P, D])
        gmix = sb("g_mix_rows", [P, D])
        raw = sb("w_raw", [P, RAW, 1024])
        hT_hi = sb("hT_hi", [P, KT, S], F32R)
        hT_lo = sb("hT_lo", [P, KT, S], F32R)
        w_hi = sb("w_hi", [P, KT, BANK], F32R)
        w_lo = sb("w_lo", [P, KT, BANK], F32R)
        xt = sb("x_tile", [P, XS, D])
        ident = sb("ident1", [P, P])
        out_hi = sb("stage_hi", [P, 2, BANK], F32R)
        out_lo = sb("stage_lo", [P, 2, BANK], F32R)
        cosb = sb("cos_rows", [P, NT, ROPE])
        sinb = sb("sin_rows", [P, NT, ROPE])
        rope_c = sb("rope_c", [P, SWH, ROPE])
        rope_s = sb("rope_s", [P, SWH, ROPE])
        ssq = sb("ssq1", [P, NT])
        msq = sb("msq1", [P, NT])
        inv = sb("inv1", [P, NT])
        rstd = sb("rstd1", [P, NT])
        tok = xt
        mm = ctx.enter_context(nc.psum_tensor("proj_psum", [P, 4, BANK], F32))
        tp = ctx.enter_context(nc.psum_tensor("turn_psum", [P, 2, 2 * BANK], F32))

        x_in = [sem(f"x_in{i}") for i in range(XS)]
        w_arrived = [sem(f"w_arrived{i}") for i in range(RAW)]
        const_in, rope_in = sem("const_in1"), sem("rope_in")
        squared, mean_done, inv_done = sem("squared"), sem("mean_done"), sem("inv_done")
        rstd_done, normed, turned = sem("rstd_done"), sem("normed"), sem("turned")
        h_hi_done, h_lo_done = sem("h_hi_done"), sem("h_lo_done")
        w_hi_done, w_lo_done = sem("w_hi_done"), sem("w_lo_done")
        proj_done, panel_read = sem("proj_done"), sem("panel_read")
        res_hi, res_lo = sem("res_hi"), sem("res_lo")
        tok_done, rope_step, roped, tok_turned = sem("tok_done"), sem("rope_step"), sem("roped"), sem("tok_turned")
        stored = [sem(f"stored{i}") for i in range(2)]
        v_stored = [sem(f"v_stored{i}") for i in range(2)]
        v_stored_by_pool = [sem(f"v_stored_by_pool{i}") for i in range(2)]
        table_made, near_in = sem("table_made"), sem("near_in")
        ones_set, table_loaded = sem("ones_set"), sem("table_loaded")

        slices = [(p, slice(0, KT), slice(g * P, (g + 1) * P)) for p in (0, 1) for g in range(4)]
        slices += [(p, slice(2 * i, 2 * i + 2), slice(0, BANK)) for p in (2, 3) for i in range(4)]
        slices += [(4, slice(4 * i, 4 * i + 4), slice(0, 256)) for i in range(2)]
        w_view = w_in.rearrange("(k p) n -> p k n", p=P)
        x_view = x.rearrange("(t p) d -> t p d", p=P)
        rel, mask, _ = near_pool
        near_parts = [(rel[:, e, :], rel_dram[e]) for e in range(2)]
        near_parts += [(mask[:, ck, c:c + BIAS_COLS // 2], near_mask_in[:, ck, c:c + BIAS_COLS // 2])
                       for ck in range(3) for c in (0, BIAS_COLS // 2)]
        AHEAD = 6
        QK_STEPS = 32
        STEPS = QK_STEPS + 3 * NT

        block = ctx.enter_context(nc.Block())

        def raw_of(n):
            _, ks, _ = slices[n]
            return raw[:, n % RAW, :].rearrange("p (k n) -> p k n", k=ks.stop - ks.start)

        def w_part(w, n):
            _, ks, cs = slices[n]
            return w[:, ks, cs]

        def staged(stage, m):
            order = "p (b r c) -> p r b c" if m < 16 else "p (r b c) -> p r b c"
            return stage[:, m % 2, :].rearrange(order, b=4, c=16)

        def result(m):
            return mm[:, m % 4, :].rearrange("p (r b c) -> p r b c", b=4, c=16)

        def split_at(m):
            return {12: [4], 13: [5], 14: [6], 15: [7], QK_STEPS - 2: [8, 9, 10], QK_STEPS - 1: [11],
                    QK_STEPS + NT - 2: [12, 13, 14], QK_STEPS + NT - 1: [15],
                    QK_STEPS + 2 * NT - 2: [16], QK_STEPS + 2 * NT - 1: [17]}.get(m, [])

        def wait_panel(eng, n):
            if 4 <= n < 8:
                eng.wait_ge(proj_done, 12 + n - 4 + 1)
            elif n in (11, 15, 17):
                eng.wait_ge(proj_done, QK_STEPS + {11: 0, 15: NT, 17: 2 * NT}[n])
            elif n >= 8:
                eng.wait_ge(panel_read, {8: 1, 9: 2, 10: 3, 12: 4, 13: 5, 14: 6, 16: 8}[n])

        def wait_tok_slot(eng, t):
            u = t - 2
            if u < 0:
                return
            if u < NT:
                eng.wait_ge(v_stored[u % 2], 64 * (u // 2 + 1))
                eng.wait_ge(v_stored_by_pool[u % 2], 64 * (u // 2 + 1))
            else:
                eng.wait_ge(tok_turned, u - NT + 1)
            if u >= 2 * NT:
                eng.wait_ge(v_stored[u % 2], 64 * (NT // 2) + 16 * ((u - 2 * NT) // 2 + 1))

        def store_v(eng, t, second_row, sems):
            for w in range(4):
                c0 = key_col(w)
                at = (2 * (t % 2) + second_row) * 32
                eng.dma_start(v_near_dram[t // 2, w, at:at + 32, :],
                              tok[second_row * GW + c0:second_row * GW + c0 + 32, t % 2, 0:AW]).then_inc(sems[t % 2], 16)

        @block.sync
        def _(sp):
            def load_w(n):
                if n >= RAW:
                    sp.wait_ge(w_lo_done, n - RAW + 1)
                p, ks, cs = slices[n]
                sp.dma_start(raw_of(n), w_view[:, ks, p * 512 + cs.start:p * 512 + cs.stop]) \
                  .then_inc(w_arrived[n % RAW], 16)

            sp.dma_start(ident[:], ident_in).then_inc(const_in, 16)
            sp.wait_ge(x_in[0], 16)
            for n in range(8):
                load_w(n)
            for m in range(QK_STEPS):
                p, tb, g = m // 16, m // 4 % 4, m % 4
                r0, cols = p * AW + g * P, slice(tb * BANK, (tb + 1) * BANK)
                sp.wait_ge(res_lo, m + 1)
                for part, stage in enumerate((out_hi, out_lo)):
                    src = stage[:, m % 2, :].bitcast(F32)
                    sp.dma_start(qk_dram[part, r0:r0 + P, cols], src) \
                        .then_inc(stored[m % 2], 16)
                if m == 15:
                    for n in range(8, 12):
                        load_w(n)
            for n in range(12, 16):
                load_w(n)
            for t in range(3 * NT):
                p, tt = 2 + t // NT, t % NT
                rows = slice(tt * P, (tt + 1) * P)
                m = QK_STEPS + t - NT
                if p == 2:
                    sp.wait_ge(tok_done, t + 1)
                    store_v(sp, t, 0, v_stored)
                    continue
                if p == 4:
                    sp.wait_ge(tok_done, t + 1)
                    sp.dma_start(v_win_dram[rows, :], tok[:, t % 2, P:2 * P]) \
                        .then_inc(v_stored[t % 2], 16)
                if t == NT:
                    for n in (16, 17):
                        load_w(n)
                if t == 2 * NT + 1:
                    sp.wait_ge(w_lo_done, len(slices))
                    sp.wait_ge(turned, NT)
                    sp.wait_ge(table_made, 16 * (2 + 8 * NAH))
                if 2 * NT + 1 <= t < 2 * NT + 1 + len(near_parts):
                    dst, src = near_parts[t - 2 * NT - 1]
                    sp.dma_start(dst, src).then_inc(near_in, 16)
                sp.wait_ge(res_lo, m + 1)
                for part, stage in enumerate((out_hi, out_lo)):
                    src = stage[:, m % 2, :].bitcast(F32)
                    if p == 3:
                        sp.dma_start(qk_dram[part, 8 * P:12 * P, rows].rearrange("(g p) s -> p g s", p=P),
                                     src.rearrange("p (g s) -> p g s", g=4)).then_inc(stored[m % 2], 16)
                    else:
                        sp.dma_start(qk_dram[part, 12 * P:13 * P, rows], src[:, 0:P]).then_inc(stored[m % 2], 16)
            for i in range(2):
                sp.wait_ge(stored[i], 16 * (QK_STEPS + 2 * NT))
                sp.wait_ge(v_stored[i], 40 * NT)
            sp.wait_ge(near_in, 16 * len(near_parts))

        @block.gpsimd
        def _(pool):
            for n in range(4):
                pool.wait_ge(w_arrived[n], 16)
                nc.gpsimd.tensor_copy(w_part(w_hi, n), raw_of(n)).then_inc(w_hi_done, 1)
                pool.wait_ge(w_hi_done, n + 1)
                nc.gpsimd.tensor_tensor(w_part(w_lo, n), raw_of(n), w_part(w_hi, n), ALU.subtract) \
                    .then_inc(w_lo_done, 1)
            pool.dma_start(cosb[:], cos2.rearrange("(t p) c -> p t c", p=P)).then_inc(rope_in, 16)
            pool.dma_start(sinb[:], sin2.rearrange("(t p) c -> p t c", p=P)).then_inc(rope_in, 16)
            pool.dma_start(pad_dram.rearrange("h r c -> (h r c)"), zeros_in).then_inc(table_made, 16)
            pool.wait_ge(table_made, 16)
            with nc.allow_non_contiguous_dma(reason="small table"):
                pool.dma_start(pad_dram[:, 4:19, 16:47], rpb).then_inc(table_made, 16)
            pool.wait_ge(table_made, 32)
            for h in range(NAH):
                for qr in range(8):
                    src = bass.AP(pad_dram.tensor, (h * PAD_R + 7 - qr) * PAD_C + 15,
                                  [[PAD_C, ROWS_REL], [-1, 16], [1, COLS_REL]])
                    dst = rel_dram[h, qr * 16:(qr + 1) * 16, :].rearrange("q (j c) -> j q c", c=COLS_REL)
                    pool.dma_start(dst, src).then_inc(table_made, 16)
            pool.wait_ge(table_made, 16 * (2 + 8 * NAH))
            for t in range(NT):
                pool.wait_ge(tok_done, t + 1)
                store_v(pool, t, 1, v_stored_by_pool)
            for i in range(2):
                pool.wait_ge(v_stored_by_pool[i], 32 * NT)

        @block.scalar
        def _(act):
            def load_x(t):
                act.dma_start(xt[:, t % XS, :], x_view[t]).then_inc(x_in[t % XS], 16)

            load_x(0)
            act.wait_ge(ones_set, 1)
            nc.scalar.activation(rstd[:, NT - 1:NT], inv[:, NT - 1:NT], ACT.Sqrt).then_inc(table_loaded, 1)
            act.dma_start(gmix[:], g_mix.broadcast_to([P, D])).then_inc(const_in, 16)
            load_x(1)
            load_x(2)

            def turn_hi(t):
                act.wait_ge(turned, t + 1)
                nc.scalar.copy(hT_hi[:, :, t * P:(t + 1) * P],
                               tp[:, t % 2, :].rearrange("p (k s) -> p k s", k=KT)).then_inc(h_hi_done, 1)

            def root(n, spare):
                act.wait_ge(x_in[n % XS], 16 * (n // XS + 1))
                nc.scalar.activation(spare, xt[:, n % XS, :], ACT.Square, accum_out=ssq[:, n:n + 1]).then_inc(squared, 1)
                act.wait_ge(inv_done, n + 1)
                nc.scalar.activation(rstd[:, n:n + 1], inv[:, n:n + 1], ACT.Sqrt).then_inc(rstd_done, 1)

            def norm_step(n):
                if n - 1 < NT:
                    turn_hi(n - 1)
                if n < NT:
                    if n <= NT - XS:
                        load_x(n - 1 + XS)
                    root(n, xn[:])

            def split_hi(n):
                wait_panel(act, n)
                act.wait_ge(w_arrived[n % RAW], 16 * (n // RAW + 1))
                nc.scalar.copy(w_part(w_hi, n), raw_of(n)).then_inc(w_hi_done, 1)

            def turn_tok_hi(t):
                m, w = QK_STEPS + t - NT, 4 * P if t < 2 * NT else P
                act.wait_ge(tok_turned, t - NT + 1)
                act.wait_ge(stored[m % 2], 32 * (m // 2))
                nc.scalar.copy(out_hi[:, m % 2, 0:w], tp[:, t % 2, 0:w]).then_inc(res_hi, 1)

            stage_spare = out_hi[:].bitcast(F32).rearrange("p a b -> p (a b)")
            for n in range(AHEAD):
                root(n, stage_spare)
                if n >= 1:
                    turn_hi(n - 1)
                    load_x(n - 1 + XS)
            for m in range(QK_STEPS):
                act.wait_ge(proj_done, m + 1)
                if m >= 2:
                    act.wait_ge(stored[m % 2], 32 * (m // 2))
                nc.scalar.mul(staged(out_hi, m), result(m), 1.0 if m < 16 else -SCALE).then_inc(res_hi, 1)
                if m + AHEAD < NT + 1:
                    norm_step(m + AHEAD)
                for n in split_at(m):
                    split_hi(n)
            for t in range(3 * NT):
                m, w = QK_STEPS + t, BANK if t < 2 * NT else 2 * P
                act.wait_ge(proj_done, m + 1)
                wait_tok_slot(act, t)
                nc.scalar.mul(tok[:, t % 2, 0:w], mm[:, m % 4, 0:w],
                              -SCALE if NT <= t < 2 * NT else 1.0).then_inc(tok_done, 1)
                if t > NT:
                    turn_tok_hi(t - 1)
                for n in split_at(m):
                    split_hi(n)
            turn_tok_hi(3 * NT - 1)

        @block.vector
        def _(dve):
            def turn_lo(t):
                dve.wait_ge(h_hi_done, t + 1)
                nc.vector.tensor_tensor(hT_lo[:, :, t * P:(t + 1) * P],
                                        tp[:, t % 2, :].rearrange("p (k s) -> p k s", k=KT),
                                        hT_hi[:, :, t * P:(t + 1) * P], ALU.subtract).then_inc(h_lo_done, 1)

            def normed_tile(n):
                dve.wait_ge(squared, n + 1)
                nc.vector.tensor_scalar(msq[:, n:n + 1], ssq[:, n:n + 1], 1.0 / D, EPS,
                                        ALU.mult, ALU.add).then_inc(mean_done, 1)
                dve.wait_ge(mean_done, n + 1)
                nc.vector.reciprocal(inv[:, n:n + 1], msq[:, n:n + 1]).then_inc(inv_done, 1)
                dve.wait_ge(rstd_done, n + 1)
                if n >= 1:
                    dve.wait_ge(turned, n)
                nc.vector.scalar_tensor_tensor(out=xn[:], in0=xt[:, n % XS, :], scalar=rstd[:, n:n + 1],
                                               in1=gmix[:], op0=ALU.mult, op1=ALU.mult).then_inc(normed, 1)

            def norm_step(n):
                if n - 1 < NT:
                    turn_lo(n - 1)
                if n < NT:
                    normed_tile(n)

            def split_lo(n):
                dve.wait_ge(w_hi_done, n + 1)
                nc.vector.tensor_tensor(w_part(w_lo, n), raw_of(n), w_part(w_hi, n), ALU.subtract) \
                    .then_inc(w_lo_done, 1)

            def rope(t):
                heads, tt, done = (SWH, t % NT, 3 * (t - NT)) if t < 2 * NT else (SWKV, t % NT, 3 * (t - NT))
                v = tok[:, t % 2, 0:heads * HD].rearrange("p (h d) -> p h d", d=HD)
                cos = cosb[:, tt:tt + 1, :].broadcast_to([P, heads, ROPE])
                sin = sinb[:, tt:tt + 1, :].broadcast_to([P, heads, ROPE])
                dve.wait_ge(tok_done, t + 1)
                nc.vector.tensor_tensor(rope_c[:, 0:heads, :], v[:, :, 0:ROPE], cos, ALU.mult).then_inc(rope_step, 1)
                nc.vector.tensor_tensor(rope_s[:, 0:heads, 0:HALF], v[:, :, HALF:ROPE], sin[:, :, 0:HALF],
                                        ALU.mult).then_inc(rope_step, 1)
                nc.vector.tensor_tensor(rope_s[:, 0:heads, HALF:ROPE], v[:, :, 0:HALF], sin[:, :, HALF:ROPE],
                                        ALU.mult).then_inc(rope_step, 1)
                dve.wait_ge(rope_step, done + 3)
                nc.vector.tensor_tensor(v[:, :, 0:ROPE], rope_c[:, 0:heads, :], rope_s[:, 0:heads, :],
                                        ALU.add).then_inc(roped, 1)
                dve.wait_ge(roped, t - NT + 1)

            def turn_tok_lo(t):
                m, w = QK_STEPS + t - NT, 4 * P if t < 2 * NT else P
                dve.wait_ge(res_hi, m + 1)
                nc.vector.tensor_tensor(out_lo[:, m % 2, 0:w], tp[:, t % 2, 0:w], out_hi[:, m % 2, 0:w],
                                        ALU.subtract).then_inc(res_lo, 1)

            nc.vector.memset(inv[:, NT - 1:NT], 1.0).then_inc(ones_set, 1)
            dve.wait_ge(const_in, 32)
            dve.wait_ge(table_loaded, 1)
            for n in range(AHEAD):
                normed_tile(n)
                if n >= 1:
                    turn_lo(n - 1)
            for m in range(QK_STEPS):
                dve.wait_ge(res_hi, m + 1)
                if m < 16:
                    low = nc.vector.tensor_tensor(staged(out_lo, m), result(m), staged(out_hi, m), ALU.subtract)
                else:
                    low = nc.vector.scalar_tensor_tensor(out=staged(out_lo, m), in0=result(m), scalar=-SCALE,
                                                         in1=staged(out_hi, m), op0=ALU.mult, op1=ALU.subtract)
                low.then_inc(res_lo, 1)
                if m + AHEAD < NT + 1:
                    norm_step(m + AHEAD)
                for n in split_at(m):
                    split_lo(n)
            dve.wait_ge(rope_in, 32)
            for t in range(3 * NT):
                if t >= NT:
                    rope(t)
                if t > NT:
                    turn_tok_lo(t - 1)
                for n in split_at(QK_STEPS + t):
                    split_lo(n)
            turn_tok_lo(3 * NT - 1)

        @block.tensor
        def _(pe):
            def turn_tile(n):
                pe.wait_ge(normed, n + 1)
                if n >= 2:
                    pe.wait_ge(h_lo_done, n - 1)
                for k in range(KT):
                    last = pe.transpose(tp[:, n % 2, k * P:(k + 1) * P], xn[:, k * P:(k + 1) * P], ident[:])
                last.then_inc(turned, 1)

            def turn_tok(t):
                pe.wait_ge(roped, t - NT + 1)
                if t - NT >= 2:
                    pe.wait_ge(res_lo, QK_STEPS + t - NT - 1)
                for g in range(4 if t < 2 * NT else 1):
                    last = pe.transpose(tp[:, t % 2, g * P:(g + 1) * P], tok[:, t % 2, g * P:(g + 1) * P], ident[:])
                last.then_inc(tok_turned, 1)

            pe.wait_ge(const_in, 32)
            for n in range(AHEAD - 1):
                turn_tile(n)
            for m in range(QK_STEPS):
                p, tb, g = m // 16, m // 4 % 4, m % 4
                cols, toks = slice(g * P, (g + 1) * P), slice(tb * BANK, (tb + 1) * BANK)
                pe.wait_ge(w_lo_done, 4 * p + g + 1)
                pe.wait_ge(h_lo_done, min(4 * tb + 4, NT) if p == 0 else NT)
                if m >= 4:
                    pe.wait_ge(res_lo, m - 3)
                for k in range(KT):
                    pe.matmul(mm[:, m % 4, :], w_hi[:, k, cols], hT_hi[:, k, toks], start=(k == 0), stop=False)
                    pe.matmul(mm[:, m % 4, :], w_hi[:, k, cols], hT_lo[:, k, toks], start=False, stop=False)
                    last = pe.matmul(mm[:, m % 4, :], w_lo[:, k, cols], hT_hi[:, k, toks], start=False,
                                     stop=(k == KT - 1))
                    if k % 2 and k < KT - 1 and m == QK_STEPS - 1:
                        last.then_inc(panel_read, 1)
                last.then_inc(proj_done, 1)
                if m + AHEAD - 1 < NT:
                    turn_tile(m + AHEAD - 1)
            for t in range(3 * NT):
                m, p = QK_STEPS + t, 2 + t // NT
                w, toks = BANK if p < 4 else 2 * P, slice(t % NT * P, (t % NT + 1) * P)
                if t < 4:
                    pe.wait_ge(res_lo, m - 3)
                else:
                    pe.wait_ge(tok_done, t - 3)
                for k in range(KT):
                    pe.wait_ge(w_lo_done, 8 + 4 * (p - 2) + (k // 2 if p < 4 else k // 4) + 1)
                    pe.matmul(mm[:, m % 4, 0:w], hT_hi[:, k, toks], w_hi[:, k, 0:w], start=(k == 0), stop=False)
                    pe.matmul(mm[:, m % 4, 0:w], hT_hi[:, k, toks], w_lo[:, k, 0:w], start=False, stop=False)
                    last = pe.matmul(mm[:, m % 4, 0:w], hT_lo[:, k, toks], w_hi[:, k, 0:w], start=False,
                                     stop=(k == KT - 1))
                    if k % 2 and k < KT - 1 and t % NT == NT - 1:
                        last.then_inc(panel_read, 1)
                last.then_inc(proj_done, 1)
                if t > NT:
                    turn_tok(t - 1)
            turn_tok(3 * NT - 1)


class Tiles:

    def __init__(self, near):
        self.near = near
        self.unit = 256 if near else 128
        self.portions = [(0, 1), (1, 3), (3, 5), (5, 8)] if near else [(0, 2), (2, 6), (6, 10), (10, 16)]

    def chunks(self, t):
        if self.near:
            return key_rows(t // 4)[1] // 4
        return 2 if t in (0, NT - 1) else 3

    def new_portions(self, t):
        def last(t):
            end = sum(key_rows(t // 4)) // 4 if self.near else min(t + 2, NT)
            return next(i for i, (lo, hi) in enumerate(self.portions) if end <= hi)

        return range(0 if t == 0 else last(t - 1) + 1, last(t) + 1)

    def keys(self, ap, t):
        if self.near:
            (r0, rows), c0 = key_rows(t // 4), key_col(t % 4)
            return ap.rearrange("p (r c) -> p r c", c=GW)[:, r0:r0 + rows, c0:c0 + 32]
        k0 = max(t - 1, 0) * P
        return ap[:, k0:k0 + self.chunks(t) * P]

    def value_chunk(self, t, j):
        if self.near:
            return (key_rows(t // 4)[0] // 4 + j) * 4 + t % 4
        return max(t - 1, 0) + j

    def score_cols(self, t):
        n = self.chunks(t) * P
        if self.near:
            return 0, 0, n
        if t == 0:
            return 1 + P, 1 + P, 2 + 3 * P
        return (1, 0, 1 + n) if t == NT - 1 else (1, 1, 2 + n)


def attention_phase(nc, qk_dram, v_near_dram, v_win_dram, rel_dram, win_mask_in, sink_in, ident_in,
                    o_dram, near_pool, w_pool, w_out, g_na, g_swa):
    NEAR, WIN = Tiles(True), Tiles(False)
    ROUNDS, NEAR_ROUNDS, UNITS = 8, 4, 2 * NT
    TURN_LAG, PV_LAG, NORM_LAG = 5, 7, 2
    OUT_LAG = PV_LAG + 1
    SC_BUFS, SN_BUFS, PT_BANKS, PT_BUFS, O_BANKS = 4, 8, 2, 4, 2
    W = 3 * P + 2
    ROW_KINDS = ((0, 12, 4, 1), (384, 16, 0, 3), (896, 12, 0, 4))
    with ExitStack() as ctx:
        def sb(n, shape, dt=F32):
            return ctx.enter_context(nc.sbuf_tensor(f"att_{n}", shape, dt))

        def sem(n):
            return nc.alloc_semaphore(f"att_{n}")

        q_st = sb("q_stack", [P, 2, S], F32R)
        k_st = sb("k_stack", [P, 2, 2, S], F32R)
        v_sb = sb("values", [P, 32, P])
        ident = sb("ident", [P, P])
        sn = sb("neg_scores", [P, SN_BUFS, BANK])
        pr = sb("probs", [P, SN_BUFS, BANK])
        pt = sb("probs_turned", [P, PT_BUFS, 4 * P])
        o_st = sb("o_stage", [P, 2, BANK])
        negmax = sb("negmax", [P, SN_BUFS])
        total = sb("total", [P, SN_BUFS])
        rtotal = sb("rtotal", [P, SN_BUFS])
        win_mask = sb("win_mask", [P, 3 * P])
        sinks = sb("sinks", [P, SWH])
        w_raw = sb("w_out_raw", [P, 2, D])
        gcol = sb("g_out", [P, KT])
        rel, mask, bias = near_pool
        sc = ctx.enter_context(nc.psum_tensor("att_scores", [P, 4, BANK], F32))
        tp = ctx.enter_context(nc.psum_tensor("att_turned", [P, 2, BANK], F32))
        op = ctx.enter_context(nc.psum_tensor("att_out", [P, 2, BANK], F32))

        q_in = [sem(f"q_in{b}") for b in range(4)]
        k_in = [sem(f"k_in{b}") for b in range(4)]
        v_in = [sem(f"v_in{b}") for b in range(4)]
        ident_arrived, win_in, rel_in = sem("ident_in"), sem("win_in"), sem("rel_in")
        bias_made, sinks_negated = sem("bias_made"), sem("sinks_negated")
        w_in, gains_in = [sem(f"w_out_in{i}") for i in range(2)], sem("gains_in")
        w_scaled, w_hi_done, w_lo_done = sem("w_scaled"), sem("w_hi_done"), sem("w_lo_done")
        scored, shifted, exped = sem("scored"), sem("shifted"), sem("exped")
        sink_set, may_shift = sem("sink_set"), sem("may_shift")
        summed, probs_done = sem("summed"), sem("probs_done")
        p_turned, pt_copied = sem("p_turned"), sem("pt_copied")
        pv_done, o_copied = sem("pv_done"), sem("o_copied")
        o_stored = [sem(f"o_stored{i}") for i in range(2)]

        def stream(eng, stages):
            deepest = max(lag for lag, _ in stages)

            def step(kind, next_kind, r, s, first=False, last=False):
                for lag, stage in stages:
                    u = s - lag
                    if (first and u < 0) or (last and u >= UNITS):
                        continue
                    stage(kind if u < UNITS else next_kind, r + u // UNITS, u % UNITS)

            def body(kind, next_kind, r, last=False):
                for s in range(deepest, UNITS + deepest):
                    step(kind, next_kind, r, s, last=last)

            for s in range(deepest):
                step(NEAR, NEAR, 0, s, first=True)
            with eng.Fori(0, NEAR_ROUNDS - 1) as r:
                body(NEAR, NEAR, r)
            body(NEAR, WIN, NEAR_ROUNDS - 1)
            with eng.Fori(NEAR_ROUNDS, ROUNDS - 1) as r:
                body(WIN, WIN, r)
            body(WIN, WIN, ROUNDS - 1, last=True)

        block = ctx.enter_context(nc.Block())

        def f32(ap):
            return ap.bitcast(F32)

        @block.sync
        def _(sp):
            heads = qk_dram.rearrange("l (h d) s -> l d h s", d=HD)

            def load_q(kind, r, b):
                qs = slice(b * BANK, (b + 1) * BANK)
                pair = bass.ds(2 * r, 2) if kind.near else bass.ds(2 * NAH - NEAR_ROUNDS + r, 2, SWH // SWKV)
                for part in range(2):
                    sp.dma_start(f32(q_st[part * HD:(part + 1) * HD, :, qs]), heads[part, :, pair, qs]) \
                        .then_inc(q_in[b], 16)

            def load_k(kind, r, b):
                lo, hi = kind.portions[b]
                ks = slice(lo * kind.unit, hi * kind.unit)
                pair = bass.ds(NAH + 2 * r, 2) if kind.near else slice(2 * NAH + SWH, HEADS)
                for part in range(2):
                    for twice in range(2):
                        sp.dma_start(f32(k_st[twice * HD:(twice + 1) * HD, :, part, ks]), heads[part, :, pair, ks]) \
                            .then_inc(k_in[b], 16)

            def load_v(kind, r, b):
                lo, hi = kind.portions[b]
                if kind.near:
                    sp.dma_start(v_sb[:, 4 * lo:4 * hi, :],
                                 v_near_dram[lo:hi, :, :, bass.ds(r * P, P)].rearrange("g w p f -> p (g w) f")) \
                        .then_inc(v_in[b], 16)
                else:
                    sp.dma_start(v_sb[:, lo:hi, :], v_win_dram[lo * P:hi * P, :].rearrange("(c p) f -> p c f", p=P)) \
                        .then_inc(v_in[b], 16)

            def load_rel(r):
                sp.dma_start(rel[:], rel_dram[bass.ds(2 * r, 2)].rearrange("h p f -> p h f")).then_inc(rel_in, 16)

            def store(r, b):
                sp.wait_ge(o_copied, O_BANKS + 4 * r + b + 1)
                sp.dma_start(o_dram[bass.ds(r * P, P), b * BANK:(b + 1) * BANK], o_st[:, b % 2, :]) \
                    .then_inc(o_stored[b % 2], 16)

            def advance(kind, r):
                load_keys = kind.near or isinstance(r, int)
                for b in range(4):
                    sp.wait_ge(scored, UNITS * r + 8 * (b + 1))
                    load_q(kind, r + 1, b)
                    if load_keys:
                        load_k(kind, r + 1, b)
                        sp.wait_ge(pv_done, PT_BUFS // 2 + NT * r + 4 * (b + 1))
                        load_v(kind, r + 1, b)
                    store(r, b)

            load_q(NEAR, 0, 0)
            load_k(NEAR, 0, 0)
            load_k(NEAR, 0, 1)
            sp.dma_start(ident[:], ident_in).then_inc(ident_arrived, 16)
            load_v(NEAR, 0, 0)
            load_v(NEAR, 0, 1)
            load_q(NEAR, 0, 1)
            for b in range(2, 4):
                load_q(NEAR, 0, b)
                load_k(NEAR, 0, b)
                load_v(NEAR, 0, b)
            sp.dma_start(win_mask[:], win_mask_in).then_inc(win_in, 16)
            sp.dma_start(sinks[:], sink_in.broadcast_to([P, SWH])).then_inc(win_in, 16)
            with sp.Fori(0, NEAR_ROUNDS - 1) as r:
                sp.wait_ge(bias_made, 3 * r + 3)
                load_rel(r + 1)
                advance(NEAR, r)
            advance(WIN, NEAR_ROUNDS - 1)
            with sp.Fori(NEAR_ROUNDS, ROUNDS - 1) as r:
                advance(WIN, r)
            for b in range(4):
                store(ROUNDS - 1, b)
            for i in range(2):
                sp.wait_ge(o_stored[i], 16 * (2 * ROUNDS + 1))

        @block.gpsimd
        def _(pool):
            def make_bias(r):
                pool.wait_ge(rel_in, 16 * r + 16)
                for kind, (at, rows, j0, freed) in enumerate(ROW_KINDS):
                    pool.wait_ge(shifted, UNITS * r + 8 * freed)
                    for e in range(2):
                        for ck, c0 in enumerate((16, 8, 0)):
                            out = bias[:, e, ck, at:at + rows * 32].rearrange("p (r c) -> p r c", c=32)
                            m = mask[:, ck, at:at + rows * 32].rearrange("p (r c) -> p r c", c=32)
                            b = rel[:, e, :].rearrange("p (j c) -> p j c", c=COLS_REL)[:, j0:j0 + rows, c0:c0 + 32]
                            last = nc.gpsimd.tensor_tensor(out, m, b, ALU.subtract)
                    last.then_inc(bias_made, 1)

            def load_w(k):
                if k < 4:
                    pool.dma_start(w_raw[:, k % 2, :], w_out[k * P:(k + 1) * P, :]).then_inc(w_in[k % 2], 32)
                    return
                for e in range(2):
                    r0 = AW + (k - 4 + 4 * e) * HD
                    pool.dma_start(w_raw[e * HD:(e + 1) * HD, k % 2, :], w_out[r0:r0 + HD, :]) \
                        .then_inc(w_in[k % 2], 16)

            pool.sem_inc(rel_in, 16)
            with pool.Fori(0, NEAR_ROUNDS) as r:
                make_bias(r)

            with nc.allow_non_contiguous_dma(reason="gains, one for each partition"):
                pool.dma_start(gcol[:, 0:4], g_na.rearrange("a (k p) -> p (a k)", p=P)).then_inc(gains_in, 16)
                for e in range(2):
                    pool.dma_start(gcol[e * HD:(e + 1) * HD, 4:8],
                                   g_swa[:, e * 4 * HD:(e + 1) * 4 * HD].rearrange("a (k p) -> p (a k)", p=HD)) \
                        .then_inc(gains_in, 16)
            load_w(0)
            load_w(1)
            pool.wait_ge(gains_in, 48)
            pool.wait_ge(shifted, UNITS * (NEAR_ROUNDS + 1))
            for k in range(KT):
                raw, w_hi, w_lo = w_raw[:, k % 2, :], w_pool[:, k, :], w_pool[:, KT + k, :]
                pool.wait_ge(w_in[k % 2], 32 * (k // 2 + 1))
                nc.gpsimd.tensor_scalar(raw, raw, gcol[:, k:k + 1], None, ALU.mult).then_inc(w_scaled, 1)
                pool.wait_ge(w_scaled, k + 1)
                nc.gpsimd.tensor_copy(w_hi, raw).then_inc(w_hi_done, 1)
                pool.wait_ge(w_hi_done, k + 1)
                nc.gpsimd.tensor_tensor(w_lo, raw, w_hi, ALU.subtract).then_inc(w_lo_done, 1)
                if k + 2 < KT:
                    pool.wait_ge(w_lo_done, k + 1)
                    load_w(k + 2)

        @block.scalar
        def _(act):
            def exp(kind, r, u):
                i, t = u % SN_BUFS, u // 2
                _, lo, hi = kind.score_cols(t)
                act.wait_ge(shifted, UNITS * (r + 1) + u + 1)
                act.wait_ge(p_turned, UNITS * r + u + 1)
                nc.scalar.activation(pr[:, i, lo:hi], sn[:, i, lo:hi], ACT.Exp, bias=negmax[:, i:i + 1],
                                     scale=-1.0, accum_out=total[:, i:i + 1]).then_inc(exped, 1)

            def copy_turned(kind, r, u):
                n = kind.chunks(u // 2) * P
                act.wait_ge(p_turned, SN_BUFS + UNITS * r + u + 1)
                act.wait_ge(pv_done, PT_BUFS // 2 + NT * r + u // 2 - 1)
                nc.scalar.copy(pt[:, u % PT_BUFS, 0:n], tp[:, u % 2, 0:n]).then_inc(pt_copied, 1)

            stream(act, [(TURN_LAG, copy_turned), (0, exp)])

        @block.vector
        def _(dve):
            def shift(kind, r, u):
                e, i, t = u % 2, u % SN_BUFS, u // 2
                n = kind.chunks(t) * P
                c0, _, _ = kind.score_cols(t)
                dve.wait_ge(exped, UNITS * r + u + 1)
                if kind.near:
                    if u % 8 == 0 and t // 4 != 2:
                        dve.wait_ge(bias_made, 3 * r + {0: 1, 1: 2, 3: 3}[t // 4])
                    b, cb = t // 4, t % 4
                    at, ck = {0: 0, 1: 384, 2: 384, 3: 896}[b], {0: 0, 1: 1, 2: 1, 3: 2}[cb]
                    add, start = bias[:, e, ck, at:at + n], 3.0e38
                else:
                    if isinstance(r, int) and r == NEAR_ROUNDS and u == 0:
                        dve.wait_ge(win_in, 32)
                        nc.vector.tensor_scalar(sinks[:], sinks[:], -1.0, None, ALU.mult).then_inc(sinks_negated, 1)
                        dve.wait_ge(sinks_negated, 1)
                    if u < SN_BUFS:
                        dve.sem_inc(may_shift, 1)
                        nc.vector.tensor_copy(sn[:, i, 0:W:W - 1],
                                              sinks[:, bass.ds(r - NEAR_ROUNDS + 4 * e, 1)].broadcast_to([P, 2])) \
                            .then_inc(sink_set, 1)
                        dve.wait_ge(sink_set, SN_BUFS * (r - NEAR_ROUNDS) + u + 1)
                    add, start = win_mask[:, c0 - 1:c0 - 1 + n], sn[:, i, 0:1]
                dve.wait_ge(scored, UNITS * r + u + 1)
                dve.sem_inc(may_shift, 1)
                nc.vector.tensor_tensor_reduce(sn[:, i, c0:c0 + n], sc[:, u % SC_BUFS, 0:n], add, 1.0, start,
                                               ALU.add, ALU.min, negmax[:, i:i + 1]).then_inc(shifted, 1)

            def invert(kind, r, u):
                i = u % SN_BUFS
                dve.wait_ge(exped, SN_BUFS + UNITS * r + u + 1)
                nc.vector.reciprocal(rtotal[:, i:i + 1], total[:, i:i + 1]).then_inc(summed, 1)

            def normalise(kind, r, u):
                i, t = u % SN_BUFS, u // 2
                n = kind.chunks(t) * P
                c0, _, _ = kind.score_cols(t)
                dve.wait_ge(summed, UNITS * r + u + 1)
                nc.vector.tensor_scalar(pr[:, i, c0:c0 + n], pr[:, i, c0:c0 + n], rtotal[:, i:i + 1], None,
                                        ALU.mult).then_inc(probs_done, 1)

            def results(kind, r, u):
                if u % 8 != 7:
                    return
                b = u // 8
                dve.wait_ge(pv_done, PT_BUFS // 2 + NT * r + 4 * (b + 1))
                dve.wait_ge(o_stored[b % 2], 16 * (2 * r + b // 2 + 1))
                dst, src = o_st[:, b % 2, :], op[:, b % 2, :]
                if kind.near:
                    dst = dst.rearrange("p (r t c) -> p r t c", t=4, c=16)
                    src = src.rearrange("p (t r c) -> p r t c", t=4, c=16)
                nc.vector.tensor_copy(dst, src).then_inc(o_copied, 1)

            dve.sem_inc(exped, SN_BUFS)
            dve.sem_inc(shifted, UNITS)
            dve.sem_inc(o_copied, O_BANKS)
            for i in range(2):
                dve.sem_inc(o_stored[i], 16)
            stream(dve, [(NORM_LAG, invert), (0, shift), (NORM_LAG, normalise), (OUT_LAG, results)])

        @block.tensor
        def _(pe):
            def score(kind, r, u):
                e, t = u % 2, u // 2
                b, n = t // 4, kind.chunks(t) * P
                if e == 0:
                    if t % 4 == 0:
                        pe.wait_ge(q_in[b], 32 * (r + 1))
                    for i in kind.new_portions(t):
                        pe.wait_ge(k_in[i], 64 * (r + 1) if kind.near else 64 * (NEAR_ROUNDS + 1))
                pe.wait_ge(shifted, UNITS * (r + 1) - SC_BUFS + u + 1)
                q, out = q_st[:, e, t * P:(t + 1) * P], sc[:, u % SC_BUFS, 0:n]
                pe.matmul(out, q, kind.keys(k_st[:, e, 0, :], t), start=True, stop=False)
                pe.matmul(out, q, kind.keys(k_st[:, e, 1, :], t), start=False, stop=True).then_inc(scored, 1)

            def turn(kind, r, u):
                i, t = u % SN_BUFS, u // 2
                c0, _, _ = kind.score_cols(t)
                if u == 0 and isinstance(r, int) and r == 0:
                    pe.wait_ge(ident_arrived, 16)
                pe.wait_ge(probs_done, UNITS * r + u + 1)
                pe.wait_ge(pt_copied, UNITS * r + u + 1)
                for j in range(kind.chunks(t)):
                    last = pe.transpose(tp[:, u % 2, j * P:(j + 1) * P], pr[:, i, c0 + j * P:c0 + (j + 1) * P],
                                        ident[:])
                last.then_inc(p_turned, 1)

            def values(kind, r, u):
                if u % 2 == 0:
                    return
                t = u // 2
                b, n = t // 4, kind.chunks(t)
                for i in kind.new_portions(t):
                    pe.wait_ge(v_in[i], 16 * (r + 1) if kind.near else 16 * (NEAR_ROUNDS + 1))
                pe.wait_ge(pt_copied, PT_BANKS + UNITS * r + u + 1)
                if t % 4 == 0:
                    pe.wait_ge(o_copied, 4 * r + b + 1)
                for j in range(n):
                    v = v_sb[:, kind.value_chunk(t, j), :]
                    for e in range(2):
                        h = slice(e * HD, (e + 1) * HD)
                        last = pe.matmul(op[h, b % 2, t % 4 * P:(t % 4 + 1) * P], v[:, h],
                                         pt[:, (u - 1 + e) % PT_BUFS, j * P:(j + 1) * P],
                                         start=(j == 0), stop=(j == n - 1))
                last.then_inc(pv_done, 1)

            pe.sem_inc(p_turned, SN_BUFS)
            pe.sem_inc(pt_copied, PT_BANKS)
            pe.sem_inc(pv_done, PT_BUFS // 2)
            stream(pe, [(0, score), (TURN_LAG, turn), (PV_LAG, values)])


def mix_phase(nc, x, w_pool, g_ffn, w_gate, w_up, ident_in, ones_in, o_dram, first, x1, hT_hi, hT_lo, x1_dram,
              h_dram):
    with ExitStack() as ctx:
        def sb(name, shape, dt=F32):
            return ctx.enter_context(nc.sbuf_tensor(f"mix_{name}", shape, dt))

        def sem(name):
            return nc.alloc_semaphore(f"mix_{name}")

        w_hi, w_lo = w_pool[:, 0:KT], w_pool[:, KT:2 * KT]
        ot, o_hi, o_lo = first
        sq = sb("squares", [P, KT, P])
        sqs = sb("squares_summed", [P, 2, P])
        xn = sb("x_normed", [P, D])
        x_stage = sb("x_stage", [P, 2, D])
        gffn = sb("g_ffn", [P, D])
        ident = sb("ident", [P, P])
        ones = sb("ones", [P, 2])
        oms, oinv, orms = (sb(n, [P, NT, 2]) for n in ("o_mean", "o_inv", "o_rms"))
        ssq, msq, inv, rstd = (sb(n, [P, NT]) for n in ("ssq", "mean", "inv", "rstd"))
        mm = ctx.enter_context(nc.psum_tensor("mix_mm", [P, 4, BANK], F32))
        tp = ctx.enter_context(nc.psum_tensor("mix_turn", [P, 2 * BANK], F32))
        st = ctx.enter_context(nc.psum_tensor("mix_stat", [P, BANK], F32))

        o_in = [sem(f"o_in{i}") for i in range(2)]
        x_in = [sem(f"x_in{i}") for i in range(2)]
        const_in = sem("const_in")
        o_squared, o_split_hi, o_split_lo = sem("o_squared"), sem("o_split_hi"), sem("o_split_lo")
        sq_summed, o_stat, o_mean, o_inv, o_rms = (sem(n) for n in ("sq_summed", "o_stat", "o_mean", "o_inv", "o_rms"))
        mm_done, added = sem("mm_done"), sem("added")
        squared, mean_done, inv_done, rstd_done = (sem(n) for n in ("squared", "mean_done", "inv_done", "rstd_done"))
        normed, turned, h_hi_done, h_lo_done = (sem(n) for n in ("normed", "turned", "h_hi_done", "h_lo_done"))
        x1_stored = [sem(f"x1_stored{i}") for i in range(2)]
        h_stored = sem("h_stored")
        gu_in = [sem(f"gu_in{i}") for i in range(2)]
        gu_hi_done = sem("gu_hi_done")

        def x_of(t):
            return x1[:, t, :] if t < HT else x_stage[:, t % 2, :]

        turned_view = tp[:].rearrange("p (k s) -> p k s", k=KT)
        xn_turned = xn[:].rearrange("p (k s) -> p k s", k=KT)
        block = ctx.enter_context(nc.Block())

        @block.sync
        def _(sp):
            def load_o(t):
                if t >= 2:
                    sp.wait_ge(o_split_lo, t - 1)
                    sp.wait_ge(o_squared, t - 1)
                sp.dma_start(ot[:, t % 2], o_dram[:, t * P:(t + 1) * P].rearrange("(k p) s -> p k s", p=P)) \
                    .then_inc(o_in[t % 2], 16)

            def load_x(t):
                if t >= 2:
                    sp.wait_ge(added, 4 * (t - 1))
                if t >= HT + 2:
                    sp.wait_ge(x1_stored[t % 2], 16 * ((t - HT) // 2))
                    sp.wait_ge(normed, t - 1)
                sp.dma_start(x_of(t), x[t * P:(t + 1) * P, :]).then_inc(x_in[t % 2], 16)

            def store_x1(t):
                sp.wait_ge(added, 4 * (t + 1))
                sp.dma_start(x1_dram[(t - HT) * P:(t - HT + 1) * P, :], x_of(t)).then_inc(x1_stored[t % 2], 16)

            def store_h(t):
                sp.wait_ge(h_hi_done, t + 1)
                sp.dma_start(h_dram[:, :, (t - HT) * P:(t - HT + 1) * P], xn_turned).then_inc(h_stored, 16)

            load_o(0)
            sp.dma_start(ones[:], ones_in).then_inc(const_in, 16)
            load_o(1)
            load_x(0)
            load_x(1)
            sp.dma_start(gffn[:], g_ffn.broadcast_to([P, D])).then_inc(const_in, 16)
            sp.dma_start(ident[:], ident_in).then_inc(const_in, 16)
            for t in range(NT):
                if t + 2 < NT:
                    load_o(t + 2)
                if t > HT:
                    store_h(t - 1)
                if t >= HT:
                    store_x1(t)
                if t + 2 < NT:
                    load_x(t + 2)
                if t == NT - 2:
                    for w, weights in enumerate((w_gate, w_up)):
                        sp.wait_ge(o_split_lo, NT)
                        sp.wait_ge(o_squared, NT)
                        sp.dma_start(ot[:, w], weights[:, 0:P].rearrange("(k p) n -> p k n", p=P)) \
                            .then_inc(gu_in[w], 16)
            store_h(NT - 1)
            sp.wait_ge(h_stored, 16 * HT)
            for i in range(2):
                sp.wait_ge(x1_stored[i], 16 * HT // 2)

        @block.scalar
        def _(act):
            def take_tile(t):
                act.wait_ge(o_in[t % 2], 16 * (t // 2 + 1))
                if t >= 2:
                    act.wait_ge(mm_done, 4 * (t - 1))
                nc.scalar.copy(o_hi[:, t % 2], ot[:, t % 2]).then_inc(o_split_hi, 1)
                if t >= 1:
                    act.wait_ge(sq_summed, t)
                nc.scalar.activation(sq[:], ot[:, t % 2], ACT.Square).then_inc(o_squared, 1)

            def o_root(t):
                act.wait_ge(o_inv, t + 1)
                nc.scalar.activation(orms[:, t, :], oinv[:, t, :], ACT.Sqrt).then_inc(o_rms, 1)

            def norm(t):
                act.wait_ge(added, 4 * (t + 1))
                if t >= 1:
                    act.wait_ge(turned, t)
                if t > HT:
                    act.wait_ge(h_stored, 16 * (t - HT))
                nc.scalar.activation(xn[:], x_of(t), ACT.Square, accum_out=ssq[:, t:t + 1]).then_inc(squared, 1)
                act.wait_ge(inv_done, t + 1)
                nc.scalar.activation(rstd[:, t:t + 1], inv[:, t:t + 1], ACT.Sqrt).then_inc(rstd_done, 1)

            def turn_hi(t):
                act.wait_ge(turned, t + 1)
                dst = hT_hi[:, :, t * P:(t + 1) * P] if t < HT else xn_turned
                nc.scalar.copy(dst, turned_view).then_inc(h_hi_done, 1)

            def split_gu(w):
                act.wait_ge(mm_done, 4 * (NT - 1 + w))
                act.wait_ge(gu_in[w], 16)
                nc.scalar.copy(o_hi[:, w], ot[:, w]).then_inc(gu_hi_done, 1)

            take_tile(0)
            for t in range(NT):
                if t >= 1:
                    norm(t - 1)
                if t == 0:
                    o_root(0)
                if t + 1 < NT:
                    take_tile(t + 1)
                if t >= 1:
                    turn_hi(t - 1)
                if t + 1 < NT:
                    o_root(t + 1)
            split_gu(0)
            norm(NT - 1)
            split_gu(1)
            turn_hi(NT - 1)

        @block.vector
        def _(dve):
            def take_tile(t):
                dve.wait_ge(o_split_hi, t + 1)
                nc.vector.tensor_tensor(o_lo[:, t % 2], ot[:, t % 2], o_hi[:, t % 2], ALU.subtract) \
                    .then_inc(o_split_lo, 1)
                dve.wait_ge(o_squared, t + 1)
                if t >= 1:
                    dve.wait_ge(o_stat, t)
                nc.vector.tensor_reduce(sqs[:], sq[:].rearrange("p (g k) s -> p g s k", g=2),
                                        mybir.AxisListType.X, ALU.add).then_inc(sq_summed, 1)

            def o_means(t):
                dve.wait_ge(o_stat, t + 1)
                nc.vector.tensor_scalar(oms[:, t, :], st[:, 0:4:2], 1.0 / AW, EPS, ALU.mult, ALU.add) \
                    .then_inc(o_mean, 1)
                dve.wait_ge(o_mean, t + 1)
                nc.vector.reciprocal(oinv[:, t, :], oms[:, t, :]).then_inc(o_inv, 1)

            def add(t, i):
                n, g = i // 2, i % 2
                dst = x_of(t)[:, n * BANK:(n + 1) * BANK]
                if i == 0:
                    dve.wait_ge(o_rms, t + 1)
                    dve.wait_ge(x_in[t % 2], 16 * (t // 2 + 1))
                dve.wait_ge(mm_done, 4 * t + i + 1)
                if g:
                    dve.wait_ge(added, 4 * t + i)
                nc.vector.scalar_tensor_tensor(out=dst, in0=mm[:, i, :], scalar=orms[:, t, g:g + 1], in1=dst,
                                               op0=ALU.mult, op1=ALU.add).then_inc(added, 1)

            def norm(t):
                dve.wait_ge(squared, t + 1)
                nc.vector.tensor_scalar(msq[:, t:t + 1], ssq[:, t:t + 1], 1.0 / D, EPS, ALU.mult, ALU.add) \
                    .then_inc(mean_done, 1)
                dve.wait_ge(mean_done, t + 1)
                nc.vector.reciprocal(inv[:, t:t + 1], msq[:, t:t + 1]).then_inc(inv_done, 1)
                dve.wait_ge(rstd_done, t + 1)
                nc.vector.scalar_tensor_tensor(out=xn[:], in0=x_of(t), scalar=rstd[:, t:t + 1], in1=gffn[:],
                                               op0=ALU.mult, op1=ALU.mult).then_inc(normed, 1)

            def turn_lo(t):
                toks = slice(t * P, (t + 1) * P)
                dve.wait_ge(h_hi_done, t + 1)
                nc.vector.tensor_tensor(hT_lo[:, :, toks], turned_view, hT_hi[:, :, toks], ALU.subtract) \
                    .then_inc(h_lo_done, 1)

            def split_gu(w):
                dve.wait_ge(gu_hi_done, w + 1)
                nc.vector.tensor_tensor(o_lo[:, w], ot[:, w], o_hi[:, w], ALU.subtract)

            take_tile(0)
            o_means(0)
            dve.wait_ge(const_in, 48)
            for t in range(NT):
                if t >= 1:
                    norm(t - 1)
                if t + 1 < NT:
                    take_tile(t + 1)
                add(t, 0)
                add(t, 1)
                if 1 <= t <= HT:
                    turn_lo(t - 1)
                add(t, 2)
                if t + 1 < NT:
                    o_means(t + 1)
                if t == NT - 1:
                    split_gu(0)
                add(t, 3)
            norm(NT - 1)
            split_gu(1)

        @block.tensor
        def _(pe):
            def stats(t):
                pe.wait_ge(sq_summed, t + 1)
                if t >= 1:
                    pe.wait_ge(o_mean, t)
                for g in range(2):
                    last = pe.matmul(st[:, 2 * g:2 * g + 2], sqs[:, g, :], ones[:], start=True, stop=True)
                last.then_inc(o_stat, 1)

            def turn(t):
                pe.wait_ge(normed, t + 1)
                if 1 <= t <= HT:
                    pe.wait_ge(h_lo_done, t)
                elif t > HT:
                    pe.wait_ge(h_hi_done, t)
                for k in range(KT):
                    last = pe.transpose(tp[:, k * P:(k + 1) * P], xn[:, k * P:(k + 1) * P], ident[:])
                last.then_inc(turned, 1)

            def product(t, i):
                n, g = i // 2, i % 2
                cols = slice(n * BANK, (n + 1) * BANK)
                if i == 0:
                    pe.wait_ge(o_split_lo, t + 1)
                if t >= 1:
                    pe.wait_ge(added, 4 * (t - 1) + i + 1)
                for k in range(4 * g, 4 * g + 4):
                    pe.matmul(mm[:, i, :], o_hi[:, t % 2, k, :], w_hi[:, k, cols], start=(k % 4 == 0), stop=False)
                    pe.matmul(mm[:, i, :], o_hi[:, t % 2, k, :], w_lo[:, k, cols], start=False, stop=False)
                    last = pe.matmul(mm[:, i, :], o_lo[:, t % 2, k, :], w_hi[:, k, cols], start=False,
                                     stop=(k % 4 == 3))
                last.then_inc(mm_done, 1)

            for t in range(NT):
                product(t, 0)
                if t == 0:
                    pe.wait_ge(const_in, 48)
                    stats(0)
                product(t, 1)
                if t >= 1:
                    turn(t - 1)
                product(t, 2)
                if t + 1 < NT:
                    stats(t + 1)
                product(t, 3)
            turn(NT - 1)


def feed_phase(nc, w_gate, w_up, w_down, g_final, w_pool, first, x1, hT_hi, hT_lo, x1_dram, h_dram, out):
    STEPS = FF // P // 2
    TBS = HS // BANK
    DOWNS = HT * 2
    with ExitStack() as ctx:
        def sb(n, shape, dt=F32):
            return ctx.enter_context(nc.sbuf_tensor(f"ff_{n}", shape, dt))

        def sem(n):
            return nc.alloc_semaphore(f"ff_{n}")

        gu_raw, first_hi, first_lo = first
        gu_hi, gu_lo = ([part, w_pool[:, n:n + 2].rearrange("p w (k c) -> p w k c", k=KT)]
                        for part, n in ((first_hi, 0), (first_lo, 2)))
        d_hi, d_lo = w_pool[:, 4:6], w_pool[:, 6:8]
        d_raw = sb("down_raw", [P, 2, D])
        a_hi, a_lo = (w_pool[:, n:n + 4].rearrange("p (q f) s -> p q f s", f=2)
                      for n in (8, 12))
        silu = sb("silu", [P, 2, BANK])
        prod = sb("prod", [P, 2, BANK])
        gfin = sb("g_final", [P, D])
        ssq, msq, inv, rstd = (sb(n, [P, HT]) for n in ("ssq", "mean", "inv", "rstd"))
        gu = ctx.enter_context(nc.psum_tensor("ff_gu", [P, 4, BANK], F32))
        dn = ctx.enter_context(nc.psum_tensor("ff_down", [P, 4, BANK], F32))

        gu_in = [sem(f"gu_in{i}") for i in range(2)]
        d_in, const_in = sem("down_in"), sem("const_in")
        gu_hi_done, gu_lo_done = sem("gu_hi_done"), sem("gu_lo_done")
        d_hi_done, d_lo_done = sem("d_hi_done"), sem("d_lo_done")
        gu_done, silu_done, prod_done = sem("gu_done"), sem("silu_done"), sem("prod_done")
        a_hi_done, a_lo_done = sem("a_hi_done"), sem("a_lo_done")
        down_done, added = sem("down_done"), sem("added")
        squared, mean_done, inv_done, rstd_done, normed = (
            sem(n) for n in ("squared", "mean_done", "inv_done", "rstd_done", "normed"))
        out_stored, x1_in = [sem(f"out_stored{i}") for i in range(2)], sem("x1_in")
        h_in = [sem(f"h_in{i}") for i in range(KT)]
        h_hi_done, h_lo_done = sem("h_hi_done"), sem("h_lo_done")

        block = ctx.enter_context(nc.Block())
        gate_v = w_gate.rearrange("(k p) n -> p k n", p=P)
        up_v = w_up.rearrange("(k p) n -> p k n", p=P)

        def h_part(ap, n):
            return ap[:, 2 * (n % 4):2 * (n % 4) + 2, n // 4 * BANK:(n // 4 + 1) * BANK]

        RAW = 2

        @block.sync
        def _(sp):
            def load(i, base):
                for f in range(1 if isinstance(i, int) and i == base == 0 else 0, 2):
                    for w, view in enumerate((gate_v, up_v)):
                        sp.wait_ge(gu_lo_done, 4 * (base + i) + 2 * f + w + 1)
                        sp.dma_start(gu_raw[:, w], view[:, :, bass.ds((2 * i + f) * P, P)]).then_inc(gu_in[w], 16)
                sp.wait_ge(d_lo_done, base + i + 1)
                sp.dma_start(d_raw[:], w_down[bass.ds(2 * i * P, 2 * P), :].rearrange("(f p) n -> p f n", p=P)) \
                    .then_inc(d_in, 16)

            load(0, 0)
            sp.dma_start(gfin[:], g_final.broadcast_to([P, D])).then_inc(const_in, 16)
            with sp.Fori(1, STEPS) as i:
                load(i, 0)
            with sp.Fori(0, STEPS) as i:
                load(i, STEPS)
            for t in range(HT, NT):
                sp.wait_ge(normed, t + 1)
                sp.dma_start(out[t * P:(t + 1) * P, :], x1[:, t - HT, :]).then_inc(out_stored[1], 16)
            sp.wait_ge(out_stored[1], 16 * HT)

        @block.gpsimd
        def _(pool):
            for tb in range(TBS):
                pool.wait_ge(gu_done, 4 * (STEPS - 1) + 2 + tb + 1)
                for kp in range(KT // 2):
                    ks, toks = slice(2 * kp, 2 * kp + 2), slice(tb * BANK, (tb + 1) * BANK)
                    pool.dma_start(hT_lo[:, ks, toks].bitcast(F32), h_dram[:, ks, toks]) \
                        .then_inc(h_in[4 * tb + kp], 16)
            for t in range(HT):
                pool.wait_ge(normed, t + 1)
                pool.dma_start(out[t * P:(t + 1) * P, :], x1[:, t, :]).then_inc(out_stored[0], 16)
            pool.wait_ge(out_stored[0], 16 * HT)
            pool.dma_start(x1[:], x1_dram.rearrange("(t p) d -> p t d", p=P)).then_inc(x1_in, 16)

        def steps(eng, tile, down, split_gu, split_d, meet, second_half=lambda: None):
            def body(i, par, last=False):
                tile(i, 0, par)
                down(i - 1, 1 - par)
                if not last:
                    split_gu(i + 1, 0)
                split_d(i)
                tile(i, 1, par)
                if not last:
                    split_gu(i + 1, 1)

            for base in (0, STEPS):
                par = base % 2
                if base == 0:
                    split_gu(0, 1)
                else:
                    meet()
                split_d(base)
                tile(base, 0, par)
                split_gu(base + 1, 0)
                tile(base, 1, par)
                split_gu(base + 1, 1)
                if base:
                    second_half()
                with eng.Fori(0, (STEPS - 3) // 2) as j:
                    body(2 * j + base + 1, 1 - par)
                    body(2 * j + base + 2, par)
                body(base + STEPS - 2, 1 - par)
                body(base + STEPS - 1, par, last=base > 0)

        @block.scalar
        def _(act):
            def split_gu(i, f):
                for w in range(2):
                    if not (isinstance(i, int) and i == 0):
                        act.wait_ge(gu_done, 4 * (i - 1) + 2 * f + 2)
                    act.wait_ge(gu_in[w], 16 * (2 * i + f))
                    nc.scalar.copy(gu_hi[f][:, w], gu_raw[:, w]).then_inc(gu_hi_done, 1)

            def split_d(i):
                if not (isinstance(i, int) and i == 0):
                    act.wait_ge(down_done, DOWNS * i)
                act.wait_ge(d_in, 16 * (i + 1))
                nc.scalar.copy(d_hi[:], d_raw[:]).then_inc(d_hi_done, 1)

            def tile(i, f, par):
                for tb in range(TBS):
                    n = 4 * i + 2 * f + tb
                    act.wait_ge(gu_done, n + 1)
                    act.wait_ge(prod_done, n + 1)
                    nc.scalar.activation(silu[:, tb], gu[:, 2 * tb], ACT.Silu).then_inc(silu_done, 1)
                    act.wait_ge(prod_done, n + 3)
                    nc.scalar.copy(a_hi[:, par, f, tb * BANK:(tb + 1) * BANK], prod[:, tb]).then_inc(a_hi_done, 1)

            def down(i, par):
                pass

            spare = silu[:].rearrange("p a b -> p (a b)")

            def square(t, steps_done):
                act.wait_ge(added, 4 + DOWNS * (steps_done - 1) + 2 * (t + 1))
                nc.scalar.activation(spare, x1[:, t, :], ACT.Square, accum_out=ssq[:, t:t + 1]) \
                    .then_inc(squared, 1)

            def meet():
                for n in range(KT):
                    act.wait_ge(h_in[n], 16)
                    nc.scalar.copy(h_part(hT_hi, n), h_part(hT_lo, n).bitcast(F32)).then_inc(h_hi_done, 1)
                for t in range(HT):
                    if t >= 1:
                        act.wait_ge(squared, t)
                    square(t, STEPS)
                act.wait_ge(inv_done, 1)
                nc.scalar.activation(rstd[:], inv[:], ACT.Sqrt).then_inc(rstd_done, 1)

            steps(act, tile, down, split_gu, split_d, meet)
            for t in range(HT):
                square(t, 2 * STEPS)
                act.wait_ge(inv_done, t + 2)
                nc.scalar.activation(rstd[:, t:t + 1], inv[:, t:t + 1], ACT.Sqrt).then_inc(rstd_done, 1)

        @block.vector
        def _(dve):
            def split_gu(i, f):
                for w in range(2):
                    dve.wait_ge(gu_hi_done, 4 * i + 2 * f + w + 1)
                    nc.vector.tensor_tensor(gu_lo[f][:, w], gu_raw[:, w], gu_hi[f][:, w], ALU.subtract) \
                        .then_inc(gu_lo_done, 1)

            def split_d(i):
                dve.wait_ge(d_hi_done, i + 1)
                nc.vector.tensor_tensor(d_lo[:], d_raw[:], d_hi[:], ALU.subtract).then_inc(d_lo_done, 1)

            def tile(i, f, par):
                for tb in range(TBS):
                    n = 4 * i + 2 * f + tb
                    dve.wait_ge(silu_done, n + 1)
                    nc.vector.tensor_tensor(prod[:, tb], gu[:, 2 * tb + 1], silu[:, tb], ALU.mult).then_inc(prod_done, 1)
                    dve.wait_ge(a_hi_done, n + 1)
                    nc.vector.tensor_tensor(a_lo[:, par, f, tb * BANK:(tb + 1) * BANK], prod[:, tb],
                                            a_hi[:, par, f, tb * BANK:(tb + 1) * BANK], ALU.subtract) \
                        .then_inc(a_lo_done, 1)

            def add(i, m):
                t, n = m // 2, m % 2
                dst = x1[:, t, n * BANK:(n + 1) * BANK]
                dve.wait_ge(down_done, DOWNS * i + m + 1)
                nc.vector.tensor_tensor(dst, dn[:, m % 4], dst, ALU.add).then_inc(added, 1)

            def down(i, par):
                for m in range(DOWNS):
                    add(i, m)

            def inverse(ts, n):
                nc.vector.tensor_scalar(msq[:, ts], ssq[:, ts], 1.0 / D, EPS, ALU.mult, ALU.add).then_inc(mean_done, 1)
                dve.wait_ge(mean_done, n)
                nc.vector.reciprocal(inv[:, ts], msq[:, ts]).then_inc(inv_done, 1)

            def scale(t):
                nc.vector.scalar_tensor_tensor(out=x1[:, t, :], in0=x1[:, t, :], scalar=rstd[:, t:t + 1], in1=gfin[:],
                                               op0=ALU.mult, op1=ALU.mult).then_inc(normed, 1)

            def meet():
                for m in range(DOWNS):
                    add(STEPS - 1, m)
                    if m % 2:
                        n = m // 2
                        dve.wait_ge(h_hi_done, n + 1)
                        nc.vector.tensor_tensor(h_part(hT_lo, n), h_part(hT_lo, n).bitcast(F32), h_part(hT_hi, n),
                                                ALU.subtract).then_inc(h_lo_done, 1)
                dve.wait_ge(squared, HT)
                inverse(slice(0, HT), 1)
                dve.wait_ge(const_in, 16)
                dve.wait_ge(rstd_done, 1)
                for t in range(HT):
                    scale(t)

            def final(t):
                dve.wait_ge(squared, HT + t + 1)
                inverse(slice(t, t + 1), t + 2)
                dve.wait_ge(rstd_done, t + 2)
                scale(t)

            dve.sem_inc(gu_hi_done, 2)
            dve.sem_inc(gu_lo_done, RAW + 2)
            dve.sem_inc(d_lo_done, 1)
            dve.sem_inc(prod_done, 2)
            dve.sem_inc(added, 4)
            steps(dve, tile, down, split_gu, split_d, meet,
                  second_half=lambda: dve.wait_ge(x1_in, 16))
            for m in range(DOWNS):
                add(2 * STEPS - 1, m)
                if m % 2 and m >= 3:
                    final(m // 2 - 1)
            final(HT - 1)

        @block.tensor
        def _(pe):
            def split_gu(i, f):
                pass

            def split_d(i):
                pass

            def tile(i, f, par):
                for tb in range(TBS):
                    toks = slice(tb * BANK, (tb + 1) * BANK)
                    pe.wait_ge(prod_done, 4 * i + 2 * f + tb + 1)
                    if isinstance(i, int) and i == STEPS and f == 0:
                        pe.wait_ge(h_lo_done, 4 * (tb + 1))
                    for w in range(2):
                        bank = gu[:, 2 * tb + w]
                        pe.wait_ge(gu_lo_done, RAW + 4 * i + 2 * f + w + 1)
                        for k in range(KT):
                            hi, lo = gu_hi[f][:, w, k, :], gu_lo[f][:, w, k, :]
                            pe.matmul(bank, hi, hT_hi[:, k, toks], start=(k == 0), stop=False)
                            pe.matmul(bank, hi, hT_lo[:, k, toks], start=False, stop=False)
                            last = pe.matmul(bank, lo, hT_hi[:, k, toks], start=False, stop=(k == KT - 1))
                    last.then_inc(gu_done, 1)

            def down(i, par):
                pe.wait_ge(d_lo_done, i + 2)
                for m in range(DOWNS):
                    t, n = m // 2, m % 2
                    if t % (HT // TBS) == 0 and n == 0:
                        pe.wait_ge(a_lo_done, 4 * i + 3 + t // (HT // TBS))
                    toks, cols = slice(t * P, (t + 1) * P), slice(n * BANK, (n + 1) * BANK)
                    pe.wait_ge(added, DOWNS * i + m + 1)
                    for f in range(2):
                        hi, lo = a_hi[:, par, f, toks], a_lo[:, par, f, toks]
                        pe.matmul(dn[:, m % 4], hi, d_hi[:, f, cols], start=(f == 0), stop=False)
                        pe.matmul(dn[:, m % 4], hi, d_lo[:, f, cols], start=False, stop=False)
                        last = pe.matmul(dn[:, m % 4], lo, d_hi[:, f, cols], start=False, stop=(f == 1))
                    last.then_inc(down_done, 1)

            def meet():
                down(STEPS - 1, 0)

            steps(pe, tile, down, split_gu, split_d, meet)
            down(2 * STEPS - 1, 1)


def rope_tables():
    freq = np.float32(500000.0) ** (-np.arange(0, ROPE, 2, dtype=np.float32) / np.float32(ROPE))
    angle = np.arange(S, dtype=np.float32)[:, None] * freq[None, :]
    cos, sin = np.cos(angle), np.sin(angle)
    return np.concatenate([cos, cos], 1), np.concatenate([-sin, sin], 1)


def neighbour_masks():
    out = np.zeros((P, 3, 1280), np.float32)
    for ck, cb in enumerate((0, 1, 3)):
        at = 0
        for band in (0, 1, 3):
            row0, rows = key_rows(band)
            qr, qc = np.arange(P) // 16 + 8 * band, np.arange(P) % 16 + 16 * cb
            kr, kc = row0 + np.arange(rows), key_col(cb) + np.arange(32)
            r0, c0 = np.clip(qr - 4, 0, S // GW - 8), np.clip(qc - 8, 0, GW - 16)
            rok = (kr >= r0[:, None]) & (kr < r0[:, None] + 8)
            cok = (kc >= c0[:, None]) & (kc < c0[:, None] + 16)
            ok = rok[:, :, None] & cok[:, None, :]
            out[:, ck, at:at + rows * 32] = np.where(ok, 0.0, MASKED).reshape(P, -1)
            at += rows * 32
    return out


def key_rows(band):
    return (0, 12) if band == 0 else (8 * band - 4, 16 if band < 3 else 12)


def key_col(cb):
    return min(max(16 * cb - 8, 0), GW - 32)


def window_mask():
    q, k = np.arange(P)[:, None], np.arange(3 * P)[None, :] - P
    return np.where(np.abs(q - k) <= 128, 0.0, MASKED).astype(np.float32)


def kernel(x, g_norm_mix, w_in, na_rpb, swa_sink, g_out_na, g_out_swa, w_out, g_norm_ffn, w_gate,
           w_up, w_down, g_final):
    import concourse.bacc as _bacc
    from concourse.bass_utils import run_bass_kernel_spmd as _run

    nc = _bacc.Bacc("TRN2", target_bir_lowering=False, num_devices=1)
    cos2, sin2 = rope_tables()
    given = {
        "x": np.asarray(x).reshape(S, D), "g_mix": np.asarray(g_norm_mix), "w_in": np.asarray(w_in)[0],
        "rpb": np.asarray(na_rpb)[0], "sink": np.asarray(swa_sink), "g_na": np.asarray(g_out_na),
        "g_swa": np.asarray(g_out_swa), "w_out": np.asarray(w_out)[0], "g_ffn": np.asarray(g_norm_ffn),
        "w_gate": np.asarray(w_gate)[0], "w_up": np.asarray(w_up)[0], "w_down": np.asarray(w_down)[0],
        "g_final": np.asarray(g_final).reshape(1, D),
        "cos2": cos2, "sin2": sin2, "ident": np.eye(P, dtype=np.float32),
        "na_mask": neighbour_masks(), "swa_mask": window_mask(),
        "zeros": np.zeros(NAH * PAD_R * PAD_C, np.float32), "ones": np.ones((P, 2), np.float32),
    }
    given = {k: np.ascontiguousarray(v) for k, v in given.items()}
    aps = {k: nc.dram_tensor(f"in_{k}", v.shape, F32, kind="ExternalInput").ap() for k, v in given.items()}
    out = nc.dram_tensor("out_0", (S, D), F32, kind="ExternalOutput").ap()
    program(nc, aps, out)
    r = _run(nc, [{f"in_{k}": v for k, v in given.items()}], core_ids=[0])
    return r.results[0]["out_0"].reshape(1, S, D)


def program(nc, a, out):
    qk_dram = nc.dram_tensor("qk_scratch", (2, HEADS * HD, S), F32).ap()
    v_near_dram = nc.dram_tensor("v_near_scratch", (S // GW // 4, 4, P, AW), F32).ap()
    v_win_dram = nc.dram_tensor("v_window_scratch", (S, SWKV * HD), F32).ap()
    pad_dram = nc.dram_tensor("pad_scratch", (NAH, PAD_R, PAD_C), F32).ap()
    rel_dram = nc.dram_tensor("rel_scratch", (NAH, P, ROWS_REL * COLS_REL), F32).ap()
    o_dram = nc.dram_tensor("o_scratch", (D, S), F32).ap()
    x1_dram = nc.dram_tensor("x1_scratch", (HS, D), F32).ap()
    h_dram = nc.dram_tensor("ffn_in_scratch", (P, KT, HS), F32).ap()
    pools = ExitStack()
    with ExitStack() as early:
        near_pool = [early.enter_context(nc.sbuf_tensor(n, shape, F32)) for n, shape in (
            ("rel", [P, 2, ROWS_REL * COLS_REL]), ("near_mask", [P, 3, BIAS_COLS]), ("bias", [P, 2, 3, BIAS_COLS]))]
    with nc.cleanup_on_exit():
        project_phase(nc, a["x"], a["g_mix"], a["w_in"], a["rpb"], a["cos2"], a["sin2"], a["ident"],
                      a["zeros"], qk_dram, v_near_dram, v_win_dram, pad_dram, rel_dram, a["na_mask"], near_pool)
    nc.all_engine_barrier()
    w_pool = pools.enter_context(nc.sbuf_tensor("w_pool", [P, 2 * KT, D], F32R))
    with nc.cleanup_on_exit():
        attention_phase(nc, qk_dram, v_near_dram, v_win_dram, rel_dram, a["swa_mask"], a["sink"], a["ident"],
                        o_dram, near_pool, w_pool, a["w_out"], a["g_na"], a["g_swa"])
    nc.all_engine_barrier()
    first = [pools.enter_context(nc.sbuf_tensor(f"first_{n}", [P, 2, KT, P], dt))
             for n, dt in (("raw", F32), ("hi", F32R), ("lo", F32R))]
    x1 = pools.enter_context(nc.sbuf_tensor("x1", [P, HT, D], F32))
    hT_hi = pools.enter_context(nc.sbuf_tensor("ffn_in_hi", [P, KT, HS], F32R))
    hT_lo = pools.enter_context(nc.sbuf_tensor("ffn_in_lo", [P, KT, HS], F32R))
    mix_phase(nc, a["x"], w_pool, a["g_ffn"], a["w_gate"], a["w_up"], a["ident"], a["ones"], o_dram, first, x1,
              hT_hi, hT_lo, x1_dram, h_dram)
    feed_phase(nc, a["w_gate"], a["w_up"], a["w_down"], a["g_final"], w_pool, first, x1, hT_hi, hT_lo, x1_dram, h_dram,
               out)
    pools.close()
```
